# Optimizing a Trainium2 kernel written in Bass

```python
import math
import jax
import jax.numpy as jnp
from jax import lax
import numpy as np

D_MODEL = 1024
BATCH = 1
SEQ = 1024
DEPTH = 1

CTX_LEN = 256
GRID_W = 64
D_MIX = D_MODEL
W_A = D_MIX // 4
W_B = D_MIX // 4
W_C = D_MIX // 4
W_D = D_MIX - W_A - W_B - W_C
MLSTM_HEADS = 4
MLSTM_HD = W_A // MLSTM_HEADS
MLSTM_CHUNK = 64
SGU_GROUPS = 4
SGU_GD = W_B // SGU_GROUPS
SGU_CHUNK = 128
CONV_WIDTH = 31
CONV_PAD = CONV_WIDTH // 2
S5_P = 16
S5_GROUPS = W_D // S5_P
S5_N = 64
D_FF = -(-8 * D_MODEL // (3 * 256)) * 256
ALPHA = (2 * DEPTH) ** 0.25
BETA = (8 * DEPTH) ** -0.25
LN_EPS = 1e-5
OFF_B = 4 * W_A + 4 * MLSTM_HEADS
OFF_C = OFF_B + 2 * W_B
OFF_D = OFF_C + 2 * W_C
P_IN = OFF_D + W_D


def layer_norm(x, w, b):
    xf = x.astype(jnp.float32)
    mu = jnp.mean(xf, -1, keepdims=True)
    var = jnp.mean(jnp.square(xf - mu), -1, keepdims=True)
    return ((xf - mu) * lax.rsqrt(var + LN_EPS) * w + b).astype(x.dtype)

def swiglu(h, w_in, w_out):
    g, u = jnp.split(h @ w_in, 2, axis=-1)
    return (jax.nn.silu(g) * u) @ w_out

def mlstm_split(z, gate_bias):
    bsz, t, _ = z.shape
    heads = lambda a: a.reshape(bsz, t, MLSTM_HEADS, MLSTM_HD).transpose(0, 2, 1, 3)
    q, k, v, o = (z[..., i * W_A:(i + 1) * W_A] for i in range(4))
    g = (z[..., 4 * W_A:] + gate_bias).astype(jnp.float32)
    g = g.reshape(bsz, t, 4, MLSTM_HEADS).transpose(2, 0, 3, 1)
    gates = (g[0], jax.nn.log_sigmoid(g[1]), g[2], jax.nn.log_sigmoid(g[3]))
    return heads(q), heads(k) * MLSTM_HD ** -0.5, heads(v), o, gates

def mlstm_zero_state(bsz):
    return (jnp.zeros((bsz, MLSTM_HEADS, MLSTM_HD, MLSTM_HD), jnp.float32),
            jnp.zeros((bsz, MLSTM_HEADS, MLSTM_HD), jnp.float32),
            jnp.zeros((bsz, MLSTM_HEADS), jnp.float32))

def mlstm_context_state(k, v, ig, lf):
    k, v = k.astype(jnp.float32), v.astype(jnp.float32)
    cum = jnp.cumsum(lf, axis=-1)
    logw = cum[..., -1:] - cum + ig
    m = jnp.max(logw, axis=-1)
    e = jnp.exp(logw - m[..., None])
    C = jnp.einsum('bht,bhtv,bhtk->bhvk', e, v, k)
    n = jnp.einsum('bht,bhtk->bhk', e, k)
    return (C, n, m)

def mlstm_chunkwise(q, k, v, ig, lf, state):
    bsz, nh, t, d = q.shape
    nc = t // MLSTM_CHUNK
    chunks = lambda a: jnp.moveaxis(a.astype(jnp.float32).reshape(bsz, nh, nc, MLSTM_CHUNK, *a.shape[3:]), 2, 0)
    xs = tuple(chunks(a) for a in (q, k, v, ig, lf))
    lower = jnp.tril(jnp.ones((MLSTM_CHUNK, MLSTM_CHUNK), bool))

    def step(carry, inp):
        C, n, m = carry
        qc, kc, vc, ic, fc = inp
        b = jnp.cumsum(fc, axis=-1)
        logw = jnp.where(lower, b[..., :, None] - b[..., None, :] + ic[..., None, :], -jnp.inf)
        inter = b + m[..., None]
        m_t = jnp.maximum(inter, jnp.max(logw, axis=-1))
        w_inter = jnp.exp(inter - m_t)
        s = jnp.einsum('bhtd,bhsd->bhts', qc, kc) * jnp.exp(logw - m_t[..., None])
        num = jnp.einsum('bhts,bhsd->bhtd', s, vc) + w_inter[..., None] * jnp.einsum('bhvk,bhtk->bhtv', C, qc)
        den = jnp.sum(s, axis=-1) + w_inter * jnp.einsum('bhk,bhtk->bht', n, qc)
        h = num / jnp.maximum(jnp.abs(den), jnp.exp(-m_t))[..., None]
        b_end = b[..., -1]
        logu = b_end[..., None] - b + ic
        m_new = jnp.maximum(b_end + m, jnp.max(logu, axis=-1))
        e = jnp.exp(logu - m_new[..., None])
        decay = jnp.exp(b_end + m - m_new)
        C = decay[..., None, None] * C + jnp.einsum('bhs,bhsv,bhsk->bhvk', e, vc, kc)
        n = decay[..., None] * n + jnp.einsum('bhs,bhsk->bhk', e, kc)
        return (C, n, m_new), h

    state, h = lax.scan(step, state, xs)
    return jnp.moveaxis(h, 0, 2).reshape(bsz, nh, t, d), state

def mlstm_readout(h, o, norm_w):
    bsz, _, t, _ = h.shape
    h = h.transpose(0, 2, 1, 3)
    mu = jnp.mean(h, -1, keepdims=True)
    var = jnp.mean(jnp.square(h - mu), -1, keepdims=True)
    hn = (h - mu) * lax.rsqrt(var + LN_EPS) * norm_w.reshape(MLSTM_HEADS, MLSTM_HD)
    return (hn.reshape(bsz, t, W_A) * jax.nn.sigmoid(o.astype(jnp.float32))).astype(o.dtype)

def mlstm_mixer(zl, zc, gate_bias, norm_w, need_ctx):
    ql, kl, vl, ol, gl = mlstm_split(zl, gate_bias)
    qc, kc, vc, oc, gc = mlstm_split(zc, gate_bias)
    hl_dirs, hc_dirs = [], []
    for d in range(2):
        orient = (lambda a: jnp.flip(a, axis=2)) if d else (lambda a: a)
        if need_ctx:
            hc, state = mlstm_chunkwise(orient(qc), orient(kc), orient(vc), orient(gc[2 * d]),
                                        orient(gc[2 * d + 1]), mlstm_zero_state(zc.shape[0]))
            hc_dirs.append(orient(hc))
        else:
            state = mlstm_context_state(orient(kc), orient(vc), orient(gc[2 * d]), orient(gc[2 * d + 1]))
        hl, _ = mlstm_chunkwise(orient(ql), orient(kl), orient(vl), orient(gl[2 * d]), orient(gl[2 * d + 1]), state)
        hl_dirs.append(orient(hl))
    yl = mlstm_readout(hl_dirs[0] + hl_dirs[1], ol, norm_w)
    yc = mlstm_readout(hc_dirs[0] + hc_dirs[1], oc, norm_w) if need_ctx else None
    return yl, yc

def sgu_mixer(z, ln_w, ln_b, w_s, b_s):
    bsz, t, _ = z.shape
    u = jax.nn.gelu(z[..., :W_B])
    v = layer_norm(jax.nn.gelu(z[..., W_B:]), ln_w, ln_b)
    v = v.reshape(bsz, t // SGU_CHUNK, SGU_CHUNK, SGU_GROUPS, SGU_GD)
    v = jnp.einsum('gts,bnsgc->bntgc', w_s, v) + b_s.T[:, :, None]
    return u * v.reshape(bsz, t, W_B)

def conv_mixer(z, w, b, ln_w, ln_b, rows):
    a = z[..., :W_C] * jax.nn.sigmoid(z[..., W_C:])
    bsz, t, ch = a.shape
    a = a.reshape(bsz * rows, t // rows, ch)
    a = lax.conv_general_dilated(a, w[:, None, :], window_strides=(1,), padding=[(CONV_PAD, CONV_PAD)],
                                 dimension_numbers=('NWC', 'WIO', 'NWC'), feature_group_count=ch)
    a = a.reshape(bsz, t, ch) + b
    return jax.nn.silu(layer_norm(a, ln_w, ln_b))

def s5_discretize(a_re, a_im, log_dt, b_re, b_im):
    lam = lax.complex(a_re.astype(jnp.float32), a_im.astype(jnp.float32))
    lam_dt = lam * jnp.exp(log_dt.astype(jnp.float32))[:, None]
    a_bar = jnp.exp(lam_dt)
    b_bar = ((a_bar - 1.0) / lam)[..., None] * lax.complex(b_re.astype(jnp.float32), b_im.astype(jnp.float32))
    return lam_dt, a_bar, b_bar

def s5_scan(bu, a_bar):
    def combine(left, right):
        a_l, b_l = left
        a_r, b_r = right
        return a_r * a_l, a_r * b_l + b_r
    a = jnp.broadcast_to(a_bar, (1,) + bu.shape[1:])
    return lax.associative_scan(combine, (a, bu), axis=1)[1]

def s5_final_state(bu, lam_dt):
    t = bu.shape[1]
    lags = jnp.arange(t - 1, -1, -1, dtype=jnp.float32)
    return jnp.einsum('tgn,btgn->bgn', jnp.exp(lags[:, None, None] * lam_dt), bu)

def s5_mixer(zl, zc, a_re, a_im, log_dt, b_re, b_im, c_re, c_im, d_skip, glu_w, glu_b, need_ctx):
    grouped = lambda z: z.astype(jnp.float32).reshape(z.shape[0], z.shape[1], S5_GROUPS, S5_P)
    ul, uc = grouped(zl), grouped(zc)
    xl_dirs, xc_dirs = [], []
    for d in range(2):
        orient = (lambda a: jnp.flip(a, axis=1)) if d else (lambda a: a)
        lam_dt, a_bar, b_bar = s5_discretize(a_re[d], a_im[d], log_dt[d], b_re, b_im)
        bul = orient(jnp.einsum('btgp,gnp->btgn', ul, b_bar))
        buc = orient(jnp.einsum('btgp,gnp->btgn', uc, b_bar))
        if need_ctx:
            sc = s5_scan(buc, a_bar)
            h0 = sc[:, -1]
            xc_dirs.append(orient(sc))
        else:
            h0 = s5_final_state(buc, lam_dt)
        sl = s5_scan(bul.at[:, 0].add(a_bar * h0), a_bar)
        xl_dirs.append(orient(sl))
    c_mat = lax.complex(c_re.astype(jnp.float32), c_im.astype(jnp.float32))
    d_mat = d_skip.astype(jnp.float32).reshape(S5_GROUPS, S5_P)

    def readout(states, u, dtype):
        y = jnp.real(jnp.einsum('gpn,btgn->btgp', c_mat, states)) + d_mat * u
        y = jax.nn.gelu(y.reshape(u.shape[0], u.shape[1], W_D))
        return (y * jax.nn.sigmoid(y @ glu_w.astype(jnp.float32) + glu_b.astype(jnp.float32))).astype(dtype)

    yl = readout(xl_dirs[0] + xl_dirs[1], ul, zl.dtype)
    yc = readout(xc_dirs[0] + xc_dirs[1], uc, zc.dtype) if need_ctx else None
    return yl, yc

def first_inputs(seed: int = 0) -> dict:
    key = jax.random.key(seed)
    ks = iter(jax.random.split(key, 48))
    f32 = jnp.float32
    nrm = lambda shape, scale: jax.random.normal(next(ks), shape, f32) * scale
    L, D = DEPTH, D_MODEL
    x = nrm((BATCH, SEQ, D), 1.0)
    c = nrm((BATCH, D), 1.0)
    ctx = nrm((BATCH, CTX_LEN, D), 1.0)
    c_ctx = nrm((D,), 1.0)
    w_mod = nrm((L, D, 6 * D), 0.5 * D ** -0.5)
    b_mod = nrm((L, 6 * D), 0.02)
    w_in = nrm((L, D, P_IN), D ** -0.5)
    ig_b = nrm((L, 2, 1, MLSTM_HEADS), 0.1)
    fg_b = jnp.linspace(3.0, 6.0, MLSTM_HEADS, dtype=f32) + nrm((L, 2, 1, MLSTM_HEADS), 0.1)
    mlstm_gate_bias = jnp.concatenate([ig_b, fg_b], axis=2).reshape(L, 4 * MLSTM_HEADS)
    mlstm_norm_w = 1.0 + nrm((L, W_A), 0.02)
    sgu_ln_w = 1.0 + nrm((L, W_B), 0.02)
    sgu_ln_b = nrm((L, W_B), 0.02)
    sgu_w = nrm((L, SGU_GROUPS, SGU_CHUNK, SGU_CHUNK), SGU_CHUNK ** -0.5)
    sgu_b = 1.0 + nrm((L, SGU_GROUPS, SGU_CHUNK), 0.02)
    conv_w = nrm((L, CONV_WIDTH, W_C), CONV_WIDTH ** -0.5)
    conv_b = nrm((L, W_C), 0.02)
    conv_ln_w = 1.0 + nrm((L, W_C), 0.02)
    conv_ln_b = nrm((L, W_C), 0.02)
    s5_a_re = -0.5 + nrm((L, 2, S5_GROUPS, S5_N), 0.01)
    s5_a_im = math.pi * jnp.arange(S5_N, dtype=f32) + nrm((L, 2, S5_GROUPS, S5_N), 0.01)
    s5_log_dt = jax.random.uniform(next(ks), (L, 2, S5_GROUPS), f32, math.log(1e-3), math.log(1e-1))
    s5_b_re = nrm((L, S5_GROUPS, S5_N, S5_P), (2 * S5_P) ** -0.5)
    s5_b_im = nrm((L, S5_GROUPS, S5_N, S5_P), (2 * S5_P) ** -0.5)
    s5_c_re = nrm((L, S5_GROUPS, S5_P, S5_N), (2 * S5_N) ** -0.5)
    s5_c_im = nrm((L, S5_GROUPS, S5_P, S5_N), (2 * S5_N) ** -0.5)
    s5_d = nrm((L, W_D), 1.0)
    s5_glu_w = nrm((L, W_D, W_D), W_D ** -0.5)
    s5_glu_b = nrm((L, W_D), 0.02)
    w_out = nrm((L, D_MIX, D), BETA * D_MIX ** -0.5)
    ln1_w = 1.0 + nrm((L, D), 0.02)
    ln1_b = nrm((L, D), 0.02)
    w_ffn_in = nrm((L, D, 2 * D_FF), D ** -0.5)
    w_ffn_out = nrm((L, D_FF, D), BETA * D_FF ** -0.5)
    ln2_w = 1.0 + nrm((L, D), 0.02)
    ln2_b = nrm((L, D), 0.02)
    return {'x': x, 'c': c, 'ctx': ctx, 'c_ctx': c_ctx, 'w_mod': w_mod, 'b_mod': b_mod, 'w_in': w_in,
            'mlstm_gate_bias': mlstm_gate_bias, 'mlstm_norm_w': mlstm_norm_w,
            'sgu_ln_w': sgu_ln_w, 'sgu_ln_b': sgu_ln_b, 'sgu_w': sgu_w, 'sgu_b': sgu_b,
            'conv_w': conv_w, 'conv_b': conv_b, 'conv_ln_w': conv_ln_w, 'conv_ln_b': conv_ln_b,
            's5_a_re': s5_a_re, 's5_a_im': s5_a_im, 's5_log_dt': s5_log_dt, 's5_b_re': s5_b_re,
            's5_b_im': s5_b_im, 's5_c_re': s5_c_re, 's5_c_im': s5_c_im, 's5_d': s5_d,
            's5_glu_w': s5_glu_w, 's5_glu_b': s5_glu_b, 'w_out': w_out, 'ln1_w': ln1_w, 'ln1_b': ln1_b,
            'w_ffn_in': w_ffn_in, 'w_ffn_out': w_ffn_out, 'ln2_w': ln2_w, 'ln2_b': ln2_b}

def first_block(x, c, ctx, c_ctx, w_mod, b_mod, w_in, mlstm_gate_bias, mlstm_norm_w,
              sgu_ln_w, sgu_ln_b, sgu_w, sgu_b, conv_w, conv_b, conv_ln_w, conv_ln_b,
              s5_a_re, s5_a_im, s5_log_dt, s5_b_re, s5_b_im, s5_c_re, s5_c_im, s5_d,
              s5_glu_w, s5_glu_b, w_out, ln1_w, ln1_b, w_ffn_in, w_ffn_out, ln2_w, ln2_b):
    rows = x.shape[1] // GRID_W
    xc = ctx
    for l in range(DEPTH):
        need_ctx = l < DEPTH - 1
        w_in_l = w_in[l]
        mod = jax.nn.silu(c) @ w_mod[l] + b_mod[l]
        mod_c = jax.nn.silu(c_ctx) @ w_mod[l] + b_mod[l]
        sh1, sc1, g1, sh2, sc2, g2 = jnp.split(mod[:, None, :], 6, axis=-1)
        sh1c, sc1c, g1c, sh2c, sc2c, g2c = jnp.split(mod_c, 6, axis=-1)
        h = x * (1.0 + sc1) + sh1
        hc = xc * (1.0 + sc1c) + sh1c
        z = h @ w_in_l
        zc_a = hc @ w_in_l[:, :OFF_B]
        zc_d = hc @ w_in_l[:, OFF_D:]
        y_a, yc_a = mlstm_mixer(z[..., :OFF_B], zc_a, mlstm_gate_bias[l], mlstm_norm_w[l], need_ctx)
        y_b = sgu_mixer(z[..., OFF_B:OFF_C], sgu_ln_w[l], sgu_ln_b[l], sgu_w[l], sgu_b[l])
        y_c = conv_mixer(z[..., OFF_C:OFF_D], conv_w[l], conv_b[l], conv_ln_w[l], conv_ln_b[l], rows)
        y_d, yc_d = s5_mixer(z[..., OFF_D:], zc_d, s5_a_re[l], s5_a_im[l], s5_log_dt[l], s5_b_re[l], s5_b_im[l],
                             s5_c_re[l], s5_c_im[l], s5_d[l], s5_glu_w[l], s5_glu_b[l], need_ctx)
        y = jnp.concatenate([y_a, y_b, y_c, y_d], axis=-1) @ w_out[l]
        x = layer_norm(ALPHA * x + g1 * y, ln1_w[l], ln1_b[l])
        x = layer_norm(ALPHA * x + g2 * swiglu(x * (1.0 + sc2) + sh2, w_ffn_in[l], w_ffn_out[l]), ln2_w[l], ln2_b[l])
        if need_ctx:
            yc_b = sgu_mixer(hc @ w_in_l[:, OFF_B:OFF_C], sgu_ln_w[l], sgu_ln_b[l], sgu_w[l], sgu_b[l])
            yc_c = conv_mixer(hc @ w_in_l[:, OFF_C:OFF_D], conv_w[l], conv_b[l], conv_ln_w[l], conv_ln_b[l], 1)
            yc = jnp.concatenate([yc_a, yc_b, yc_c, yc_d], axis=-1) @ w_out[l]
            xc = layer_norm(ALPHA * xc + g1c * yc, ln1_w[l], ln1_b[l])
            xc = layer_norm(ALPHA * xc + g2c * swiglu(xc * (1.0 + sc2c) + sh2c, w_ffn_in[l], w_ffn_out[l]),
                            ln2_w[l], ln2_b[l])
    return x


_first_inputs = first_inputs


def first_inputs(seed=0):
    import zlib

    import numpy as np

    out = dict(_first_inputs(seed))
    spreads = {}
    factors = {'ctx': 6.508,
     'c_ctx': 7.612,
     'b_mod': 4.658,
     'mlstm_norm_w': 64.0,
     'sgu_ln_w': 60.145,
     'sgu_ln_b': 59.579,
     'sgu_b': 63.078,
     'conv_b': 8.0,
     'conv_ln_w': 60.666,
     'conv_ln_b': 64.0,
     's5_a_re': 64.0,
     's5_a_im': 64.0,
     's5_log_dt': 64.0,
     's5_b_re': 64.0,
     's5_b_im': 64.0,
     's5_c_re': 64.0,
     's5_c_im': 64.0,
     's5_glu_w': 18.351,
     's5_glu_b': 64.0,
     'ln1_w': 8.152,
     'ln1_b': 7.59,
     'ln2_w': 8.199,
     'ln2_b': 8.095}
    for name, (base, spread) in spreads.items():
        noise = np.random.default_rng([zlib.crc32(name.encode()), seed]).standard_normal(out[name].shape)
        drawn = base * np.exp(spread * noise) if base else spread * noise
        out[name] = jnp.asarray(drawn.astype(out[name].dtype))
    for name, factor in factors.items():
        out[name] = (out[name] * factor).astype(out[name].dtype)
    return out


_narrow_inputs = first_inputs


def first_inputs(seed=0):
    out = dict(_narrow_inputs(seed))
    wider = {'mlstm_norm_w': 6.0,
     'sgu_ln_w': 4.97,
     'sgu_ln_b': 4.92,
     'sgu_b': 5.02,
     'conv_ln_w': 4.89,
     'conv_ln_b': 5.13,
     's5_d': 9.54,
     's5_glu_w': 12.0,
     's5_glu_b': 12.0,
     'ln2_w': 3.32,
     'ln2_b': 3.25}
    for name, times in wider.items():
        mean = out[name].mean()
        out[name] = (mean + times * (out[name] - mean)).astype(out[name].dtype)
    return out


EPS = 1e-6
CONV_WIDTH_2 = 4
MIX_WIDTH = 2 * D_MODEL
ATT_HEAD_DIM = 64
ATT_WIDTH = MIX_WIDTH // 4
ATT_HEADS = ATT_WIDTH // ATT_HEAD_DIM
Q_BLOCK = 128
SSD_HEAD_DIM = 64
SSD_WIDTH = MIX_WIDTH // 2
SSD_HEADS = SSD_WIDTH // SSD_HEAD_DIM
SSD_GROUPS = 2
SSD_STATE = 128
SSD_CHUNK = 128
SSD_CONV_DIM = SSD_WIDTH + 2 * SSD_GROUPS * SSD_STATE
DT_MIN = 0.001
DT_MAX = 0.1
LRU_WIDTH = MIX_WIDTH // 4
LRU_BLOCKS = 8
LRU_BLOCK_DIM = LRU_WIDTH // LRU_BLOCKS
LRU_C = 8.0
IN_SIZES = (ATT_WIDTH, ATT_WIDTH, ATT_WIDTH, ATT_WIDTH, ATT_HEADS,
            SSD_WIDTH, SSD_CONV_DIM, SSD_HEADS,
            LRU_WIDTH, LRU_WIDTH)
D_IN = sum(IN_SIZES)


def rms_norm(x, g):
    xf = x.astype(jnp.float32)
    return xf * lax.rsqrt(jnp.mean(xf * xf, axis=-1, keepdims=True) + EPS) * g

def causal_dwconv(x, w, b):
    k = w.shape[0]
    y = lax.conv_general_dilated(
        x, w.astype(x.dtype)[:, None, :], window_strides=(1,),
        padding=((k - 1, 0),), dimension_numbers=('NWC', 'WIO', 'NWC'),
        feature_group_count=x.shape[-1])
    return y + b

def fox_attention(q, k, v, log_f, q_g, k_g):
    bsz, seq = q.shape[0], q.shape[1]
    nb = seq // Q_BLOCK
    q = rms_norm(q, q_g)
    k = rms_norm(k, k_g)
    c = jnp.cumsum(log_f.astype(jnp.float32), axis=1)
    qb = q.reshape(bsz, nb, Q_BLOCK, ATT_HEADS, ATT_HEAD_DIM).transpose(1, 0, 3, 2, 4)
    cq = c.reshape(bsz, nb, Q_BLOCK, ATT_HEADS).transpose(1, 0, 3, 2)
    kt = k.transpose(0, 2, 1, 3)
    vt = v.transpose(0, 2, 1, 3)
    ck = c.transpose(0, 2, 1)
    kpos = jnp.arange(seq)
    scale = ATT_HEAD_DIM ** -0.5

    def one_block(args):
        q_i, c_i, blk = args
        logits = jnp.einsum('bhqd,bhkd->bhqk', q_i, kt) * scale + (c_i[..., :, None] - ck[:, :, None, :])
        qpos = blk * Q_BLOCK + jnp.arange(Q_BLOCK)
        logits = jnp.where(kpos[None, :] <= qpos[:, None], logits, -jnp.inf)
        p = jax.nn.softmax(logits.astype(jnp.float32), axis=-1)
        return jnp.einsum('bhqk,bhkd->bhqd', p, vt)

    o = lax.map(one_block, (qb, cq, jnp.arange(nb)))
    return o.transpose(1, 0, 3, 2, 4).reshape(bsz, seq, ATT_WIDTH)

def ssd_mixer(xbc_raw, dt_raw, z, conv_w, conv_b, dt_bias, a_log, d_skip, norm_g):
    bsz, seq = xbc_raw.shape[0], xbc_raw.shape[1]
    nc = seq // SSD_CHUNK
    e = SSD_HEADS // SSD_GROUPS
    gn = SSD_GROUPS * SSD_STATE
    xbc = jax.nn.silu(causal_dwconv(xbc_raw, conv_w, conv_b))
    xs, bm, cm = jnp.split(xbc, [SSD_WIDTH, SSD_WIDTH + gn], axis=-1)
    dt = jax.nn.softplus(dt_raw + dt_bias)
    a = -jnp.exp(a_log.astype(jnp.float32))
    xh = xs.reshape(bsz, seq, SSD_HEADS, SSD_HEAD_DIM)
    xdt = (xh * dt[..., None]).reshape(bsz, nc, SSD_CHUNK, SSD_GROUPS, e, SSD_HEAD_DIM)
    adt = (dt * a).reshape(bsz, nc, SSD_CHUNK, SSD_GROUPS, e).transpose(0, 1, 3, 4, 2)
    bc = bm.reshape(bsz, nc, SSD_CHUNK, SSD_GROUPS, SSD_STATE)
    cc = cm.reshape(bsz, nc, SSD_CHUNK, SSD_GROUPS, SSD_STATE)
    a_cs = jnp.cumsum(adt, axis=-1)
    causal = jnp.tril(jnp.ones((SSD_CHUNK, SSD_CHUNK), dtype=bool))
    seg = a_cs[..., :, None] - a_cs[..., None, :]
    lmat = jnp.exp(jnp.where(causal, seg, -jnp.inf))
    cb = jnp.einsum('bclgn,bcsgn->bcgls', cc, bc)
    y_diag = jnp.einsum('bcgels,bcsgep->bclgep', cb[:, :, :, None] * lmat, xdt)
    decay_states = jnp.exp(a_cs[..., -1:] - a_cs)
    states = jnp.einsum('bclgn,bcgel,bclgep->bcgepn', bc, decay_states, xdt)
    tot = jnp.concatenate([jnp.zeros_like(a_cs[:, :1, ..., -1]), a_cs[..., -1]], axis=1)
    tot_cs = jnp.cumsum(tot, axis=1)
    seg_c = tot_cs[:, :, None] - tot_cs[:, None, :]
    causal_c = jnp.tril(jnp.ones((nc + 1, nc + 1), dtype=bool))[None, :, :, None, None]
    decay_chunk = jnp.exp(jnp.where(causal_c, seg_c, -jnp.inf))
    states_pad = jnp.concatenate([jnp.zeros_like(states[:, :1]), states], axis=1)
    new_states = jnp.einsum('bzcge,bcgepn->bzgepn', decay_chunk, states_pad)
    prev_states = new_states[:, :nc]
    y_off = jnp.einsum('bclgn,bcgepn,bcgel->bclgep', cc, prev_states, jnp.exp(a_cs))
    y = (y_diag + y_off).reshape(bsz, seq, SSD_HEADS, SSD_HEAD_DIM) + xh * d_skip[:, None]
    y = y.reshape(bsz, seq, SSD_WIDTH)
    gated = (y * jax.nn.silu(z)).reshape(bsz, seq, SSD_GROUPS, SSD_WIDTH // SSD_GROUPS)
    gated = rms_norm(gated, 1.0).reshape(bsz, seq, SSD_WIDTH)
    return gated * norm_g

def _lin_combine(c1, c2):
    a1, b1 = c1
    a2, b2 = c2
    return a1 * a2, a2 * b1 + b2

def rglru_mixer(x_raw, conv_w, conv_b, w_a, b_a, w_x, b_x, lam):
    bsz, seq = x_raw.shape[0], x_raw.shape[1]
    xc = causal_dwconv(x_raw, conv_w, conv_b)
    xb = xc.reshape(bsz, seq, LRU_BLOCKS, LRU_BLOCK_DIM)
    r = jax.nn.sigmoid(jnp.einsum('bsnd,nde->bsne', xb, w_a).reshape(bsz, seq, LRU_WIDTH) + b_a)
    i = jax.nn.sigmoid(jnp.einsum('bsnd,nde->bsne', xb, w_x).reshape(bsz, seq, LRU_WIDTH) + b_x)
    log_a = (-LRU_C * r * jax.nn.softplus(-lam)).astype(jnp.float32)
    a = jnp.exp(log_a)
    mult = jnp.sqrt(-jnp.expm1(2.0 * log_a))
    mult = jnp.where((jnp.arange(seq) == 0)[None, :, None], 1.0, mult)
    b = mult * (i * xc)
    _, h = lax.associative_scan(_lin_combine, (a, b), axis=1)
    return h

def second_inputs(seed: int = 0) -> dict:
    key = jax.random.key(seed)
    ks = jax.random.split(key, 24)
    f32 = jnp.float32
    L = DEPTH
    nrm = lambda k, s: jax.random.normal(k, s, f32)
    x = nrm(ks[0], (BATCH, SEQ, D_MODEL))
    norm_g = 1.0 + 0.05 * nrm(ks[1], (L, D_MODEL))
    w_in = nrm(ks[2], (L, D_MODEL, D_IN)) * D_MODEL ** -0.5
    q_norm_g = 1.0 + 0.05 * nrm(ks[3], (L, ATT_HEAD_DIM))
    k_norm_g = 1.0 + 0.05 * nrm(ks[4], (L, ATT_HEAD_DIM))
    forget_b = jax.random.uniform(ks[5], (L, ATT_HEADS), f32, minval=1.0, maxval=4.0)
    ssd_conv_w = nrm(ks[6], (L, CONV_WIDTH_2, SSD_CONV_DIM)) * CONV_WIDTH_2 ** -0.5
    ssd_conv_b = 0.02 * nrm(ks[7], (L, SSD_CONV_DIM))
    dt0 = jnp.exp(jax.random.uniform(ks[8], (L, SSD_HEADS), f32) * (math.log(DT_MAX) - math.log(DT_MIN)) + math.log(DT_MIN))
    ssd_dt_bias = dt0 + jnp.log(-jnp.expm1(-dt0))
    ssd_a_log = jnp.log(jax.random.uniform(ks[9], (L, SSD_HEADS), f32, minval=1.0, maxval=16.0))
    ssd_d = 1.0 + 0.1 * nrm(ks[10], (L, SSD_HEADS))
    ssd_norm_g = 1.0 + 0.05 * nrm(ks[11], (L, SSD_WIDTH))
    lru_conv_w = nrm(ks[12], (L, CONV_WIDTH_2, LRU_WIDTH)) * CONV_WIDTH_2 ** -0.5
    lru_conv_b = 0.02 * nrm(ks[13], (L, LRU_WIDTH))
    lru_w_a = nrm(ks[14], (L, LRU_BLOCKS, LRU_BLOCK_DIM, LRU_BLOCK_DIM)) * LRU_BLOCK_DIM ** -0.5
    lru_b_a = 0.02 * nrm(ks[15], (L, LRU_WIDTH))
    lru_w_x = nrm(ks[16], (L, LRU_BLOCKS, LRU_BLOCK_DIM, LRU_BLOCK_DIM)) * LRU_BLOCK_DIM ** -0.5
    lru_b_x = 0.02 * nrm(ks[17], (L, LRU_WIDTH))
    a_pow_c = jax.random.uniform(ks[18], (L, LRU_WIDTH), f32, minval=0.9, maxval=0.999)
    s = a_pow_c ** (1.0 / LRU_C)
    lru_lambda = jnp.log(s) - jnp.log1p(-s)
    w_out = nrm(ks[19], (L, MIX_WIDTH, D_MODEL)) * MIX_WIDTH ** -0.5
    return {'x': x, 'norm_g': norm_g, 'w_in': w_in, 'q_norm_g': q_norm_g, 'k_norm_g': k_norm_g,
            'forget_b': forget_b, 'ssd_conv_w': ssd_conv_w, 'ssd_conv_b': ssd_conv_b,
            'ssd_dt_bias': ssd_dt_bias, 'ssd_a_log': ssd_a_log, 'ssd_d': ssd_d,
            'ssd_norm_g': ssd_norm_g, 'lru_conv_w': lru_conv_w, 'lru_conv_b': lru_conv_b,
            'lru_w_a': lru_w_a, 'lru_b_a': lru_b_a, 'lru_w_x': lru_w_x, 'lru_b_x': lru_b_x,
            'lru_lambda': lru_lambda, 'w_out': w_out}

def second_block(x, norm_g, w_in, q_norm_g, k_norm_g, forget_b, ssd_conv_w, ssd_conv_b,
              ssd_dt_bias, ssd_a_log, ssd_d, ssd_norm_g, lru_conv_w, lru_conv_b,
              lru_w_a, lru_b_a, lru_w_x, lru_b_x, lru_lambda, w_out):
    out_dtype = x.dtype
    h = x.astype(jnp.float32)
    bsz, seq = h.shape[0], h.shape[1]
    split_points = np.cumsum(IN_SIZES)[:-1].tolist()
    for l in range(DEPTH):
        u = rms_norm(h, norm_g[l])
        proj = jnp.einsum('bsd,de->bse', u, w_in[l])
        (q, k, v, z_att, f_raw, z_ssd, xbc, dt_raw, x_lru, z_lru) = jnp.split(proj, split_points, axis=-1)
        hs = (bsz, seq, ATT_HEADS, ATT_HEAD_DIM)
        log_f = jax.nn.log_sigmoid(f_raw + forget_b[l])
        y_att = fox_attention(q.reshape(hs), k.reshape(hs), v.reshape(hs), log_f,
                              q_norm_g[l], k_norm_g[l]) * jax.nn.silu(z_att)
        y_ssd = ssd_mixer(xbc, dt_raw, z_ssd, ssd_conv_w[l], ssd_conv_b[l], ssd_dt_bias[l],
                          ssd_a_log[l], ssd_d[l], ssd_norm_g[l])
        y_lru = rglru_mixer(x_lru, lru_conv_w[l], lru_conv_b[l], lru_w_a[l], lru_b_a[l],
                            lru_w_x[l], lru_b_x[l], lru_lambda[l]) * jax.nn.silu(z_lru)
        mix = jnp.concatenate([y_att, y_ssd, y_lru], axis=-1)
        h = h + jnp.einsum('bse,ed->bsd', mix, w_out[l])
    return h.astype(out_dtype)


def setup_inputs(seed=0):
    out = dict(first_inputs(seed))
    for name, value in second_inputs(seed + 1).items():
        if name != "x":
            out[name + "_2"] = value
    return out


def reference(
    x, c, ctx, c_ctx, w_mod, b_mod, w_in, mlstm_gate_bias, mlstm_norm_w, sgu_ln_w, sgu_ln_b,
    sgu_w, sgu_b, conv_w, conv_b, conv_ln_w, conv_ln_b, s5_a_re, s5_a_im, s5_log_dt, s5_b_re,
    s5_b_im, s5_c_re, s5_c_im, s5_d, s5_glu_w, s5_glu_b, w_out, ln1_w, ln1_b, w_ffn_in,
    w_ffn_out, ln2_w, ln2_b, norm_g_2, w_in_2, q_norm_g_2, k_norm_g_2, forget_b_2, ssd_conv_w_2,
    ssd_conv_b_2, ssd_dt_bias_2, ssd_a_log_2, ssd_d_2, ssd_norm_g_2, lru_conv_w_2, lru_conv_b_2,
    lru_w_a_2, lru_b_a_2, lru_w_x_2, lru_b_x_2, lru_lambda_2, w_out_2,
):
    x = first_block(
        x, c, ctx, c_ctx, w_mod, b_mod, w_in, mlstm_gate_bias, mlstm_norm_w, sgu_ln_w, sgu_ln_b,
        sgu_w, sgu_b, conv_w, conv_b, conv_ln_w, conv_ln_b, s5_a_re, s5_a_im, s5_log_dt,
        s5_b_re, s5_b_im, s5_c_re, s5_c_im, s5_d, s5_glu_w, s5_glu_b, w_out, ln1_w, ln1_b,
        w_ffn_in, w_ffn_out, ln2_w, ln2_b,
    )
    return second_block(
        x, norm_g_2, w_in_2, q_norm_g_2, k_norm_g_2, forget_b_2, ssd_conv_w_2, ssd_conv_b_2,
        ssd_dt_bias_2, ssd_a_log_2, ssd_d_2, ssd_norm_g_2, lru_conv_w_2, lru_conv_b_2,
        lru_w_a_2, lru_b_a_2, lru_w_x_2, lru_b_x_2, lru_lambda_2, w_out_2,
    )


_drawn_inputs = setup_inputs


def setup_inputs(seed=0):
    import zlib

    import numpy as np

    out = dict(_drawn_inputs(seed))
    spreads = {}
    factors = {'s5_glu_b': 8.0,
     'norm_g_2': 6.458,
     'q_norm_g_2': 8.0,
     'k_norm_g_2': 8.0,
     'forget_b_2': 8.0,
     'ssd_conv_b_2': 64.0,
     'ssd_dt_bias_2': 2.919,
     'ssd_d_2': 200.0,
     'ssd_norm_g_2': 47.361,
     'lru_conv_b_2': 8.0,
     'lru_w_a_2': 6.585,
     'lru_b_a_2': 200.0,
     'lru_w_x_2': 3.319,
     'lru_b_x_2': 64.0}
    for name, (base, spread) in spreads.items():
        noise = np.random.default_rng([zlib.crc32(name.encode()), seed]).standard_normal(out[name].shape)
        drawn = base * np.exp(spread * noise) if base else spread * noise
        out[name] = jnp.asarray(drawn.astype(out[name].dtype))
    for name, factor in factors.items():
        out[name] = (out[name] * factor).astype(out[name].dtype)
    return out
```

```python
import math
from contextlib import ExitStack

import concourse.bass as bass
from concourse import mybir

P = 128
F32 = mybir.dt.float32
ALU = mybir.AluOpType
ACT = mybir.ActivationFunctionType
AX = mybir.AxisListType.X
PSB = 512

D = 1024
KT = D // P
T = 1024
NT = T // P
HALF = 512
TC = 256
NTC = TC // P

W_MIX = D // 4
HEADS, HD = 4, 64
O_Q, O_K, O_V, O_O, O_G = 0, W_MIX, 2 * W_MIX, 3 * W_MIX, 4 * W_MIX
O_B = O_G + 4 * HEADS
O_C = O_B + 2 * W_MIX
O_D = O_C + 2 * W_MIX
P_IN = O_D + W_MIX
CONV_W, CONV_PAD, GRID = 31, 15, 64
ROWS = T // GRID
S5G, S5P, S5N = 16, 16, 64
S5L = 8
S5C = T // S5L
S5CC = TC // S5L
D_FF = -(-8 * D // (3 * 256)) * 256
FT = D_FF // P
ALPHA = 2.0 ** 0.25
LN_EPS = 1e-5
EPS = 1e-6

ATT_W, ATT_H, ATT_HD = 512, 8, 64
SSD_W, SSD_H, SSD_P, SSD_G, SSD_N, SSD_C = 1024, 16, 64, 2, 128, 128
SSD_CONV = SSD_W + 2 * SSD_G * SSD_N
LRU_W, LRU_B, LRU_BD, LRU_C = 512, 8, 64, 8.0
TAPS = 4
Q_OFF, K_OFF, V_OFF, ZA_OFF = 0, ATT_W, 2 * ATT_W, 3 * ATT_W
F_OFF = 4 * ATT_W
ZS_OFF = F_OFF + ATT_H
XBC_OFF = ZS_OFF + SSD_W
DT_OFF = XBC_OFF + SSD_CONV
XL_OFF = DT_OFF + SSD_H
ZL_OFF = XL_OFF + LRU_W
D_IN = ZL_OFF + LRU_W
MIX_W = 2 * D
MT = MIX_W // P


class Views:
    pass


class Named:

    def __init__(self, by_name):
        self.by_name = by_name

    def __getattr__(self, name):
        return self.by_name[name]


class Arena:

    def __init__(self, tensor, size):
        self.t, self.size = tensor, size

    def view(self, at, *shape, parts=P):
        n = math.prod(shape)
        assert at + n <= self.size, (at, shape)
        v = self.t[0:parts, at:at + n]
        if len(shape) == 2:
            v = v.rearrange("p (a b) -> p a b", b=shape[1])
        elif len(shape) == 3:
            v = v.rearrange("p (a b c) -> p a b c", b=shape[1], c=shape[2])
        return v


PACKS = [
    [("b_mod", 48), ("ln1_w", 8), ("ln1_b", 8), ("ln2_w", 8), ("ln2_b", 8), ("norm_g_2", 8),
     ("mlstm_norm_w", 2), ("conv_b", 2), ("conv_ln_w", 2), ("conv_ln_b", 2), ("s5_glu_b", 2)],
    [("ssd_conv_w_2", 48), ("ssd_conv_b_2", 12), ("ssd_norm_g_2", 8), ("lru_conv_w_2", 16),
     ("lru_conv_b_2", 4), ("lru_b_a_2", 4), ("lru_b_x_2", 4), ("lru_lambda_2", 4)],
    [("conv_w", 62), ("c", 8), ("c_ctx", 8), ("q_norm_g_2", 1), ("k_norm_g_2", 1)],
]
COL = {}
_at = 0
for _p in PACKS:
    for _name, _n in _p:
        COL[_name] = (_at, _n)
        _at += _n
N_COLS = _at

SIZE = 52800
M_IDENT, M_ONES, M_MEAN, M_TLE, M_TGE, M_TLT, M_TGT, M_BLK = (128 * i for i in range(8))
M_COLS = 1024
M_MOD = M_COLS + N_COLS
M_CS = M_MOD + 96
M_SC1 = M_CS + 16
M_SC2 = M_SC1 + 16
M_WX = M_SC2 + 8
M_SMALL = M_WX + 32
BASE = 2048
assert M_SMALL + 300 < BASE
TILE8 = KT * T
X0 = BASE
H0 = X0 + TILE8
C0 = H0 + TILE8
Z0 = C0 + KT * TC
Z_TILES = 12
KC0 = Z0 + Z_TILES * T
VT0 = KC0 + 2 * TC
VC0 = VT0 + NT * HEADS * (HD + 1)
GT0 = VC0 + NTC * HEADS * (HD + 1)
SV0 = GT0 + (NT + NTC) * 16
U50 = SV0 + NT * W_MIX
U5C0 = U50 + 2048
WR0 = U5C0 + 2048
assert WR0 + 10368 <= SIZE, WR0


N_SEMAPHORES = 150
used_semaphores = [0]


def semaphores(nc, ctx, prefix, names):
    n = len(names.split())
    if used_semaphores[0] + n > N_SEMAPHORES:
        free = sorted(nc.released_uncleared_semaphores)
        with nc.Block() as block:
            @block.gpsimd
            def _(pool):
                first = free[0]
                for a, b in zip(free, free[1:] + [None]):
                    if b != a + 1:
                        pool.sem_clear(range(first, a + 1))
                        first = b
        used_semaphores[0] = 0
    used_semaphores[0] += n
    return Named({n: ctx.enter_context(nc.semaphore(f"{prefix}_{n}")) for n in names.split()})


def psum(nc, ctx, name, *shape):
    return ctx.enter_context(nc.psum_tensor(name, [P, *shape], F32))


def col(S, name, i=0, n=1, parts=slice(0, P)):
    at, _ = COL[name]
    return S.cols[parts, at + i:at + i + n]


def stage_constants(nc, I, S):
    with ExitStack() as ctx:
        s = semaphores(nc, ctx, "c", "memset masks rows xin cin turned bank_free cols act silu mod_w0 mod_w1 mod_w2 "
                                     "slot_free mod_mm dve h")
        A = S.arena
        xtok = A.view(Z0, NT, D)
        ctok = A.view(Z0 + NT * D, NTC, D)
        rows = A.view(H0, 3, P)
        ring = [A.view(Z0 + (NT + NTC) * D + i * 4096, KT, 512) for i in range(3)]
        mod_w = [s.mod_w0, s.mod_w1, s.mod_w2]
        n_mod = 6 * D // 512
        ps = psum(nc, ctx, "c_turn", 6, PSB)
        pm = psum(nc, ctx, "c_mod", PSB)
        n_rows_dma = 0

        with nc.Block() as block:
            @block.sync
            def _(sp):
                n = 0
                for p, pack in enumerate(PACKS):
                    at = 0
                    for name, k in pack:
                        a = I[name]
                        if name in ("q_norm_g_2", "k_norm_g_2"):
                            for half in range(2):
                                sp.dma_start(rows[at:at + 1, p, half * 64:half * 64 + 64], a).then_inc(s.rows, 16)
                                n += 1
                        else:
                            flat = {1: "a -> a", 2: "a b -> (a b)", 3: "a b c -> (a b c)"}[len(a.shape)]
                            v = (a.rearrange(flat) if len(a.shape) > 1 else a).rearrange("(r q) -> r q", q=P)
                            sp.dma_start(rows[at:at + k, p, :], v).then_inc(s.rows, 16)
                            n += 1
                        at += k
                S.n_rows = n
                sp.dma_start(xtok, I["x"].rearrange("b (i p) d -> p (b i) d", p=P)).then_inc(s.xin, 16)
                sp.dma_start(ctok, I["ctx"].rearrange("b (i p) d -> p (b i) d", p=P)).then_inc(s.cin, 16)

            @block.scalar
            def _(act):
                for m in range(n_mod):
                    if m >= 3:
                        act.wait_ge(s.slot_free, m - 2)
                    act.dma_start(ring[m % 3], I["w_mod"].rearrange("l (k p) n -> p (l k) n", p=P)[
                        :, :, m * 512:m * 512 + 512]).then_inc(mod_w[m % 3], 16)
                    if m == 2:
                        act.wait_ge(s.cols, 3)
                        nc.scalar.activation(S.cs[:, :, 0], col(S, "c", 0, 8), ACT.Silu).then_inc(s.silu, 1)
                        nc.scalar.activation(S.cs[:, :, 1], col(S, "c_ctx", 0, 8), ACT.Silu).then_inc(s.silu, 1)

            @block.gpsimd
            def _(pool):
                pool.memset(S.ident, 0.0).then_inc(s.memset, 1)
                for m in (S.ones, S.t_le, S.t_ge, S.t_lt, S.t_gt):
                    pool.memset(m, 1.0).then_inc(s.memset, 1)
                pool.memset(S.mean, 1.0 / D).then_inc(s.memset, 1)
                pool.wait_ge(s.memset, 7)
                pool.affine_select(out=S.ident, in_=S.ident, compare_op=ALU.not_equal, fill=1.0, base=0,
                                   pattern=[[-1, P]], channel_multiplier=1).then_inc(s.masks, 1)
                for m, sign, op in ((S.t_le, 1, ALU.is_ge), (S.t_ge, -1, ALU.is_ge),
                                    (S.t_lt, 1, ALU.is_gt), (S.t_gt, -1, ALU.is_gt)):
                    pool.affine_select(out=m, in_=m, compare_op=op, fill=0.0, base=0, pattern=[[sign, P]],
                                       channel_multiplier=-sign).then_inc(s.masks, 1)

            @block.tensor
            def _(pe):
                pe.wait_ge(s.masks, 5)
                pe.wait_ge(s.rows, 16 * S.n_rows)
                for p, pack in enumerate(PACKS):
                    k = sum(n for _, n in pack)
                    pe.transpose(ps[:, p, 0:k], rows[0:k, p, :], S.ident[0:k, 0:k]).then_inc(s.turned, 1)
                pe.wait_ge(s.xin, 16)
                pe.wait_ge(s.cin, 16)
                b = 3
                for k in range(KT):
                    for src, dst_tiles in ((xtok, 4), (xtok, 8), (ctok, 2)):
                        n0 = {4: 0, 8: 4, 2: 0}[dst_tiles]
                        n1 = {4: 4, 8: 8, 2: 2}[dst_tiles]
                        if b >= 6:
                            pe.wait_ge(s.bank_free, b - 5)
                        for i in range(n0, n1):
                            t = pe.transpose(ps[:, b % 6, (i - n0) * P:(i - n0 + 1) * P],
                                             src[:, i, k * P:(k + 1) * P], S.ident)
                        t.then_inc(s.turned, 1)
                        b += 1
                pe.wait_ge(s.silu, 2)
                for m in range(n_mod):
                    pe.wait_ge(mod_w[m % 3], 16 * (m // 3 + 1))
                    for j in range(4):
                        for k in range(KT):
                            mm = pe.matmul(pm[:, (4 * m + j) * 2:(4 * m + j) * 2 + 2],
                                           ring[m % 3][:, k, j * P:(j + 1) * P], S.cs[:, k, :],
                                           start=(k == 0), stop=(k == KT - 1))
                    mm.then_inc(s.slot_free, 1)

            @block.vector
            def _(dve):
                nc.vector.memset(S.blk, 0.0).then_inc(s.dve, 1)
                dve.wait_ge(s.dve, 1)
                for half in (slice(0, 64), slice(64, 128)):
                    nc.vector.memset(S.blk[half, half], 1.0 / 64)
                at = 0
                for p, pack in enumerate(PACKS):
                    k = sum(n for _, n in pack)
                    dve.wait_ge(s.turned, p + 1)
                    nc.vector.tensor_copy(S.cols[:, at:at + k], ps[:, p, 0:k]).then_inc(s.cols, 1)
                    at += k
                dve.wait_ge(s.cols, 3)
                nc.vector.memset(S.small[:, 0:1], 0.0).then_inc(s.bank_free, 3)
                b = 3
                for k in range(KT):
                    for n in (4, 8, 2):
                        dve.wait_ge(s.turned, b + 1)
                        if n == 2:
                            dst, w = S.ctxT[:, k, :], TC
                        else:
                            dst, w = S.xT[:, k, (n - 4) * P:n * P], HALF
                        nc.vector.tensor_copy(dst, ps[:, b % 6, 0:w]).then_inc(s.bank_free, 1)
                        b += 1
                dve.wait_ge(s.slot_free, n_mod)
                at, _ = COL["b_mod"]
                nc.vector.tensor_tensor(S.mod, pm[:, 0:96].rearrange("p (a b) -> p a b", b=2),
                                        S.cols[:, at:at + 48].unsqueeze(2).broadcast_to([P, 48, 2]),
                                        ALU.add).then_inc(s.dve, 1)
                dve.wait_ge(s.dve, 2)
                nc.vector.tensor_scalar(S.sc1, S.mod[:, 8:16, :], 1.0, None, ALU.add).then_inc(s.dve, 1)
                nc.vector.tensor_scalar(S.sc2, S.mod[:, 32:40, 0], 1.0, None, ALU.add).then_inc(s.dve, 1)
                w, b = col(S, "ln1_w", 0, KT), col(S, "ln1_b", 0, KT)
                nc.vector.tensor_scalar(S.x_w, w, ALPHA, None, ALU.mult)
                nc.vector.tensor_scalar(S.x_b, b, ALPHA, None, ALU.mult)
                dve.wait_ge(s.dve, 4)
                nc.vector.tensor_tensor(S.h_w, w, S.sc2, ALU.mult)
                nc.vector.tensor_tensor(S.h_b, b, S.sc2, ALU.mult).then_inc(s.dve, 1)
                dve.wait_ge(s.dve, 5)
                nc.vector.tensor_tensor(S.h_b, S.h_b, S.mod[:, 24:32, 0], ALU.add)
                dve.wait_ge(s.dve, 4)
                dve.wait_ge(s.bank_free, 3 + 3 * KT)
                for k in range(KT):
                    nc.vector.tensor_scalar(S.hT[:, k, :], S.xT[:, k, :], S.sc1[:, k, 0:1], S.mod[:, k, 0:1],
                                            ALU.mult, ALU.add).then_inc(s.h, 1)
                    nc.vector.tensor_scalar(S.ctxT[:, k, :], S.ctxT[:, k, :], S.sc1[:, k, 1:2],
                                            S.mod[:, k, 1:2], ALU.mult, ALU.add)
                for k in range(KT):
                    dve.wait_ge(s.h, k + 1)
                    nc.vector.tensor_scalar(S.xT[:, k, :], S.xT[:, k, :], ALPHA, None, ALU.mult)


def dense(nc, S, name, weights, n_tiles, kt, moving, width, evac, ring_at, evac_engine="scalar",
          irregular=False):
    halves = max(1, width // HALF)
    w = min(width, HALF)
    assert n_tiles % 4 == 0
    with ExitStack() as ctx:
        s = semaphores(nc, ctx, name, "w0 w1 w2 w3 bank_free done")
        slots = [S.arena.view(ring_at + i * kt * P, kt, P) for i in range(4)]
        loaded = [s.w0, s.w1, s.w2, s.w3]
        ps = psum(nc, ctx, f"{name}_ps", 8, PSB)
        with nc.Block() as block:
            @block.sync
            def _(sp):
                for j in range(4):
                    sp.dma_start(slots[j], weights(j)).then_inc(loaded[j], 16)
                if irregular:
                    for m in range(4, n_tiles):
                        sp.wait_ge(s.done, halves * (m - 3))
                        sp.dma_start(slots[m % 4], weights(m)).then_inc(loaded[m % 4], 16)
                elif n_tiles > 4:
                    with sp.Fori(1, n_tiles // 4) as i:
                        for j in range(4):
                            sp.wait_ge(s.done, i * (4 * halves) + halves * (j - 3))
                            sp.dma_start(slots[j], weights(i * 4 + j)).then_inc(loaded[j], 16)

            @block.tensor
            def _(pe):
                with pe.Fori(0, n_tiles // 4) as i:
                    for j in range(4):
                        pe.wait_ge(loaded[j], i * 16 + 16)
                        for h in range(halves):
                            pe.wait_ge(s.bank_free, i * (4 * halves) + (halves * j + h + 1))
                            for k in range(kt):
                                mm = pe.matmul(ps[:, 2 * j + h, 0:w], slots[j][:, k, :],
                                               moving(k)[:, h * w:(h + 1) * w],
                                               start=(k == 0), stop=(k == kt - 1))
                            mm.then_inc(s.done, 1)
    
            def copy_out(engine, e):
                e.sem_inc(s.bank_free, 4 * halves)
                if irregular:
                    for m in range(n_tiles):
                        for h in range(halves):
                            e.wait_ge(s.done, halves * m + h + 1)
                            evac(engine, ps[:, 2 * (m % 4) + h, 0:w], m, h).then_inc(s.bank_free, 1)
                    return
                with e.Fori(0, n_tiles // 4) as i:
                    for j in range(4):
                        for h in range(halves):
                            e.wait_ge(s.done, i * (4 * halves) + (halves * j + h + 1))
                            evac(engine, ps[:, 2 * j + h, 0:w], i * 4 + j, h).then_inc(s.bank_free, 1)

            if evac_engine == "scalar":
                @block.scalar
                def _(act):
                    copy_out(nc.scalar, act)
            else:
                @block.vector
                def _(dve):
                    copy_out(nc.vector, dve)



class Chain:

    def __init__(self, engine, sem):
        self.engine, self.sem, self.n = engine, sem, 0

    def __call__(self, ins):
        ins.then_inc(self.sem, 1)
        self.n += 1
        self.engine.wait_ge(self.sem, self.n)


def stage_project_1(nc, I, S):
    w = I["w_in"].rearrange("l (k p) n -> p (l k) n", p=P)
    first = [O_Q, O_Q + P, O_K, O_K + P, O_O, O_O + P, O_B, O_B + P] + [O_C + i * P for i in range(4)]
    funcs = [ACT.Copy] * 4 + [ACT.Sigmoid] * 2 + [ACT.Gelu_apprx_tanh] * 2 + [ACT.Copy] * 2 + [ACT.Sigmoid] * 2

    def evac(act, bank, m, h):
        return act.activation(S.z[:, m, h * HALF:(h + 1) * HALF], bank, funcs[m])

    dense(nc, S, "p1", lambda m: w[:, :, first[m]:first[m] + P], Z_TILES, KT, lambda k: S.hT[:, k, :], T, evac,
          WR0, irregular=True)


def stage_project_tokens_1(nc, I, S):
    A = S.arena
    n_tok = W_MIX + 16 + W_MIX
    wt = A.view(WR0, KT, n_tok)
    wd = A.view(WR0 + KT * n_tok, KT, W_MIX)
    wk = A.view(WR0 + KT * (n_tok + W_MIX), KT, W_MIX)
    w = I["w_in"].rearrange("l (k p) n -> p (l k) n", p=P)
    jobs = []
    for i in range(NT):
        tok = slice(i * P, (i + 1) * P)
        jobs.append((lambda k, tok=tok: S.hT[:, k, tok], lambda k: wt[:, k, 0:272], P, 272, "vg", i))
        jobs.append((lambda k, tok=tok: S.hT[:, k, tok], lambda k: wt[:, k, 272:528], P, 256, "sv", i))
    for i in range(NTC):
        tok = slice(i * P, (i + 1) * P)
        jobs.append((lambda k, tok=tok: S.ctxT[:, k, tok], lambda k: wt[:, k, 0:272], P, 272, "vg", NT + i))
    for j in range(S5L):
        jobs.append((lambda k, j=j: S.hT[:, k, j::S5L], lambda k: wd[:, k, :], P, 256, "s5", j))
    for j in range(S5L):
        jobs.append((lambda k, j=j: S.ctxT[:, k, j::S5L], lambda k: wd[:, k, :], S5CC, 256, "s5c", j))
    for m in range(2):
        jobs.append((lambda k, m=m: wk[:, k, m * P:(m + 1) * P], lambda k: S.ctxT[:, k, :], P, TC, "kc", m))
    with ExitStack() as ctx:
        s = semaphores(nc, ctx, "t1", "wt wd wk done by_dve by_act")
        ps = psum(nc, ctx, "t1_ps", 8, PSB)
        freed = []
        n_act = n_dve = 0
        for j in jobs:
            if j[4] == "sv":
                n_act += 1
                freed.append((s.by_act, n_act))
            else:
                n_dve += 1
                freed.append((s.by_dve, n_dve))
        with nc.Block() as block:
            @block.sync
            def _(sp):
                for a, b, off, n in ((0, 256, O_V, 256), (256, 272, O_G, 16), (272, 528, O_B + W_MIX, 256)):
                    sp.dma_start(wt[:, :, a:b], w[:, :, off:off + n]).then_inc(s.wt, 16)
                sp.dma_start(wd, w[:, :, O_D:O_D + W_MIX]).then_inc(s.wd, 16)
                sp.dma_start(wk, w[:, :, O_K:O_K + W_MIX]).then_inc(s.wk, 16)

            @block.tensor
            def _(pe):
                pe.wait_ge(s.wt, 48)
                for n, (sta, mov, rows, cols, kind, _) in enumerate(jobs):
                    if n == 2 * NT + NTC:
                        pe.wait_ge(s.wd, 16)
                    if kind == "kc":
                        pe.wait_ge(s.wk, 16)
                    if n >= 8:
                        pe.wait_ge(*freed[n - 8])
                    for k in range(KT):
                        mm = pe.matmul(ps[0:rows, n % 8, 0:cols], sta(k), mov(k), start=(k == 0), stop=(k == KT - 1))
                    mm.then_inc(s.done, 1)

            @block.scalar
            def _(act):
                for n, (_, _, rows, cols, kind, i) in enumerate(jobs):
                    if kind == "sv":
                        act.wait_ge(s.done, n + 1)
                        nc.scalar.activation(S.sv[:, i, :], ps[:, n % 8, 0:cols], ACT.Gelu_apprx_tanh)\
                            .then_inc(s.by_act, 1)

            @block.vector
            def _(dve):
                nc.vector.memset(S.vt[:, :, HD:HD + 1], 1.0)
                for n, (_, _, rows, cols, kind, i) in enumerate(jobs):
                    if kind == "sv":
                        continue
                    dve.wait_ge(s.done, n + 1)
                    b = ps[0:rows, n % 8, 0:cols]
                    if kind == "vg":
                        nc.vector.tensor_copy(S.vt[:, i * HEADS:(i + 1) * HEADS, 0:HD],
                                              b[:, 0:256].rearrange("p (h d) -> p h d", h=HEADS))
                        c = nc.vector.tensor_copy(S.gates[:, i, :], b[:, 256:272])
                    elif kind == "s5":
                        c = nc.vector.tensor_copy(S.u5[:, :, i, :], b.rearrange("p (g q) -> p g q", g=S5G))
                    elif kind == "s5c":
                        c = nc.vector.tensor_copy(S.u5c[0:rows, :, i, :], b.rearrange("p (g q) -> p g q", g=S5G))
                    else:
                        c = nc.vector.tensor_copy(S.kc[:, i, :], b)
                    c.then_inc(s.by_dve, 1)


def normalize(nc, S, name, src, n_tiles, count, eps, center, tmp, rs, final):
    with ExitStack() as ctx:
        s = semaphores(nc, ctx, name, "sums centered squared var root inverse scaled")
        ps = psum(nc, ctx, f"{name}_ps", 4, PSB)
        cut = [slice(0, HALF), slice(HALF, T)]
        with nc.Block() as block:
            @block.tensor
            def _(pe):
                for h in range(2):
                    if center:
                        for k in range(n_tiles):
                            mm = pe.matmul(ps[:, h, :], S.ones, src(k)[:, cut[h]], start=(k == 0),
                                           stop=(k == n_tiles - 1))
                        mm.then_inc(s.sums, 1)
                for h in range(2):
                    pe.wait_ge(s.squared, n_tiles * (h + 1))
                    for k in range(n_tiles):
                        mm = pe.matmul(ps[:, 2 + h, :], S.ones, tmp(k)[:, cut[h]], start=(k == 0),
                                       stop=(k == n_tiles - 1))
                    mm.then_inc(s.var, 1)

            @block.vector
            def _(dve):
                if center:
                    for h in range(2):
                        dve.wait_ge(s.sums, h + 1)
                        for k in range(n_tiles):
                            nc.vector.scalar_tensor_tensor(out=src(k)[:, cut[h]], in0=ps[:, h, :],
                                                           scalar=-1.0 / count, in1=src(k)[:, cut[h]],
                                                           op0=ALU.mult, op1=ALU.add).then_inc(s.centered, 1)
                for h in range(2):
                    dve.wait_ge(s.var, h + 1)
                    nc.vector.tensor_scalar(rs[:, cut[h]], ps[:, 2 + h, :], 1.0 / count, eps, ALU.mult, ALU.add)\
                        .then_inc(s.root, 1)
                    dve.wait_ge(s.inverse, h + 1)
                    nc.vector.reciprocal(rs[:, cut[h]], rs[:, cut[h]]).then_inc(s.scaled, 1)
                    dve.wait_ge(s.scaled, (n_tiles + 1) * h + 1)
                    for k in range(n_tiles):
                        nc.vector.tensor_tensor(src(k)[:, cut[h]], src(k)[:, cut[h]], rs[:, cut[h]], ALU.mult)\
                            .then_inc(s.scaled, 1)

            @block.scalar
            def _(act):
                for h in range(2):
                    for k in range(n_tiles):
                        if center:
                            act.wait_ge(s.centered, n_tiles * h + k + 1)
                        nc.scalar.activation(tmp(k)[:, cut[h]], src(k)[:, cut[h]], ACT.Square)\
                            .then_inc(s.squared, 1)
                for h in range(2):
                    act.wait_ge(s.root, h + 1)
                    nc.scalar.activation(rs[:, cut[h]], rs[:, cut[h]], ACT.Sqrt).then_inc(s.inverse, 1)
                for h in range(2):
                    for k in range(n_tiles):
                        act.wait_ge(s.scaled, (n_tiles + 1) * h + k + 2)
                        final(act, k, h, cut[h])


def stage_conv(nc, I, S):
    pad = S.arena.view(WR0, 2 * ROWS, GRID + 2 * CONV_PAD)
    acc = S.arena.view(WR0 + 2 * ROWS * (GRID + 2 * CONV_PAD), 2, T)
    tmp = S.arena.view(WR0 + 2 * ROWS * (GRID + 2 * CONV_PAD) + 2 * T, 3, T)
    with ExitStack() as ctx:
        s = semaphores(nc, ctx, "cv", "pads gated taps")
        with nc.Block() as block:
            @block.vector
            def _(dve):
                nc.vector.memset(pad[:, :, 0:CONV_PAD], 0.0).then_inc(s.pads, 1)
                nc.vector.memset(pad[:, :, CONV_PAD + GRID:], 0.0).then_inc(s.pads, 1)
                for c in range(2):
                    nc.vector.tensor_tensor(pad[:, c * ROWS:(c + 1) * ROWS, CONV_PAD:CONV_PAD + GRID],
                                            S.z[:, 8 + c, :].rearrange("p (r t) -> p r t", r=ROWS),
                                            S.z[:, 10 + c, :].rearrange("p (r t) -> p r t", r=ROWS),
                                            ALU.mult).then_inc(s.pads, 1)
                dve.wait_ge(s.pads, 4)
                for w in range(CONV_W):
                    for c in range(2):
                        src = pad[:, c * ROWS:(c + 1) * ROWS, w:w + GRID]
                        a = acc[:, c, :].rearrange("p (r t) -> p r t", r=ROWS)
                        if w == 0:
                            nc.vector.tensor_scalar(a, src, col(S, "conv_w", c), col(S, "conv_b", c), ALU.mult,
                                                    ALU.add).then_inc(s.taps, 1)
                        else:
                            dve.wait_ge(s.taps, 2 * (w - 1) + c + 1)
                            nc.vector.scalar_tensor_tensor(out=a, in0=src, scalar=col(S, "conv_w", 2 * w + c),
                                                           in1=a, op0=ALU.mult, op1=ALU.add).then_inc(s.taps, 1)

    def final(act, k, h, cut):
        nc.scalar.activation(S.yT[:, 4 + k, cut], acc[:, k, cut], ACT.Silu, bias=col(S, "conv_ln_b", k),
                             scale=col(S, "conv_ln_w", k))

    normalize(nc, S, "cn", lambda k: acc[:, k, :], 2, W_MIX, LN_EPS, True, lambda k: tmp[:, k, :], tmp[:, 2, :],
              final)


def stage_sgu(nc, I, S):
    A = S.arena
    G, GD = 4, 64
    ws = A.view(WR0, G, P)
    wsT = A.view(WR0 + 512, G, P)
    bs = A.view(WR0 + 1024, G, P)
    lnw = A.view(WR0 + 1536, W_MIX)
    lnb = A.view(WR0 + 1792, W_MIX)
    st = A.view(WR0 + 2048, NT, 6)
    mv = A.view(WR0 + 2100, NT, 2)
    rs = A.view(WR0 + 2120, NT)
    with ExitStack() as ctx:
        s = semaphores(nc, ctx, "sg", "ws rows dve root normed wT wTc done")
        pw = psum(nc, ctx, "sg_w", PSB)
        po = psum(nc, ctx, "sg_o", 4, PSB)
        with nc.Block() as block:
            @block.sync
            def _(sp):
                sp.dma_start(ws, I["sgu_w"].rearrange("l g t s -> t (l g) s")).then_inc(s.ws, 16)
                sp.dma_start(bs[0:1, :, :], I["sgu_b"]).then_inc(s.rows, 16)
                sp.dma_start(lnw, I["sgu_ln_w"].broadcast_to([P, W_MIX])).then_inc(s.rows, 16)
                sp.dma_start(lnb, I["sgu_ln_b"].broadcast_to([P, W_MIX])).then_inc(s.rows, 16)

            @block.vector
            def _(dve):
                step = Chain(dve, s.dve)
                for i in range(NT):
                    c = nc.vector.bn_stats(st[:, i, :], S.sv[:, i, :])
                step(c)
                for i in range(NT):
                    c = nc.vector.bn_aggr(mv[:, i, :], st[:, i, :])
                step(c)
                nc.vector.tensor_scalar(rs, mv[:, :, 1], LN_EPS, None, ALU.add).then_inc(s.root, 1)
                dve.wait_ge(s.ws, 16)
                dve.wait_ge(s.wT, 1)
                nc.vector.tensor_copy(wsT, pw[:, :].rearrange("p (g t) -> p g t", g=G)).then_inc(s.wTc, 1)
                dve.wait_ge(s.root, 2)
                step(nc.vector.reciprocal(rs, rs))
                for i in range(NT):
                    c = nc.vector.tensor_scalar(S.sv[:, i, :], S.sv[:, i, :], mv[:, i, 0:1], rs[:, i:i + 1],
                                                ALU.subtract, ALU.mult)
                step(c)
                dve.wait_ge(s.rows, 48)
                step(nc.vector.tensor_tensor(S.sv, S.sv, lnw.unsqueeze(1).broadcast_to([P, NT, W_MIX]), ALU.mult))
                nc.vector.tensor_tensor(S.sv, S.sv, lnb.unsqueeze(1).broadcast_to([P, NT, W_MIX]), ALU.add)\
                    .then_inc(s.normed, 1)
                for n in range(4):
                    c, h = n // 2, n % 2
                    cut = slice(h * HALF, (h + 1) * HALF)
                    dve.wait_ge(s.done, n + 1)
                    nc.vector.tensor_tensor(S.yT[:, 2 + c, cut], po[:, n, :], S.z[:, 6 + c, cut], ALU.mult)

            @block.scalar
            def _(act):
                act.wait_ge(s.root, 1)
                nc.scalar.activation(rs, rs, ACT.Sqrt).then_inc(s.root, 1)

            @block.tensor
            def _(pe):
                pe.wait_ge(s.ws, 16)
                for g in range(G):
                    t = pe.transpose(pw[:, g * P:(g + 1) * P], ws[:, g, :], S.ident)
                t.then_inc(s.wT, 1)
                pe.wait_ge(s.rows, 48)
                pe.wait_ge(s.wTc, 1)
                pe.wait_ge(s.normed, 1)
                for n in range(4):
                    c, h = n // 2, n % 2
                    for i in range(4):
                        for e in range(2):
                            g, o = 2 * c + e, po[e * GD:(e + 1) * GD, n, i * P:(i + 1) * P]
                            pe.matmul(o, S.ones[0:1, 0:GD], bs[0:1, g, :], start=True, stop=False)
                            mm = pe.matmul(o, S.sv[:, 4 * h + i, g * GD:(g + 1) * GD], wsT[:, g, :],
                                           start=False, stop=True)
                    mm.then_inc(s.done, 1)



def log1p_tail(step, nc, e, ln, w, out_t):
    step(nc.vector.tensor_scalar(w, e, -0.25, 1.0 / 3.0, ALU.mult, ALU.add))
    step(nc.vector.tensor_tensor(w, w, e, ALU.mult))
    step(nc.vector.tensor_scalar(w, w, -0.5, None, ALU.add))
    step(nc.vector.tensor_tensor(w, w, e, ALU.mult))
    step(nc.vector.tensor_scalar(w, w, 1.0, None, ALU.add))
    step(nc.vector.tensor_tensor(w, w, e, ALU.mult))
    step(nc.vector.tensor_tensor(w, w, ln, ALU.subtract))
    step(nc.vector.tensor_scalar(e, e, 1.0 / 128.0, None, ALU.is_lt))
    step(nc.vector.tensor_tensor(w, w, e, ALU.mult))
    step(nc.vector.tensor_tensor(out_t, w, ln, ALU.add))


def stage_mlstm_gates(nc, I, S):
    A = S.arena
    N = NT + NTC
    bias = A.view(WR0, 16)
    fg = A.view(WR0 + 16, N, 8)
    e, ln, w = (A.view(WR0 + 96 + 80 * i, N, 8) for i in range(3))
    lf = A.view(WR0 + 336, N, 8)
    rows = A.view(C0, N * P)[0:8, :]
    first = A.view(WR0 + 500, 1)[0:8, :]
    with ExitStack() as ctx:
        s = semaphores(nc, ctx, "mg", "bias dve act exped lf sums a turned max Mt")
        pb = psum(nc, ctx, "mg_b", PSB)
        pt = psum(nc, ctx, "mg_t", 3, PSB)
        pm = psum(nc, ctx, "mg_m", PSB)
        b = pb[:, 0:80].rearrange("p (i n) -> p i n", n=8)
        with nc.Block() as block:
            @block.sync
            def _(sp):
                sp.dma_start(bias, I["mlstm_gate_bias"].broadcast_to([P, 16])).then_inc(s.bias, 16)

            @block.vector
            def _(dve):
                step = Chain(dve, s.dve)
                dve.wait_ge(s.bias, 16)
                g = S.gates.rearrange("p i (d k h) -> p i d k h", d=2, k=2)
                step(nc.vector.tensor_tensor(S.gates, S.gates, bias.unsqueeze(1).broadcast_to([P, N, 16]), ALU.add))
                for d in range(2):
                    c = nc.vector.tensor_copy(fg[:, :, 4 * d:4 * d + 4], g[:, :, d, 1, :])
                step(c)
                step(nc.vector.tensor_scalar(w, fg, -1.0, None, ALU.mult))
                nc.vector.tensor_tensor(e, w, fg, ALU.min).then_inc(s.act, 1)
                dve.wait_ge(s.exped, 2)
                log1p_tail(step, nc, e, ln, w, w)
                step(nc.vector.tensor_scalar(fg, fg, 0.0, None, ALU.min))
                nc.vector.tensor_tensor(lf, fg, w, ALU.subtract).then_inc(s.lf, 1)
                dve.wait_ge(s.sums, 1)
                for d in range(2):
                    nc.vector.tensor_tensor(S.a[:, 0:NT, 4 * d:4 * d + 4], g[:, 0:NT, d, 0, :],
                                            b[:, 0:NT, 4 * d:4 * d + 4], ALU.subtract).then_inc(s.a, 1)
                    nc.vector.tensor_tensor(S.a[:, NT:N, 4 * d:4 * d + 4], g[:, NT:N, d, 0, :],
                                            b[:, NT:N, 4 * d:4 * d + 4], ALU.add).then_inc(s.a, 1)
                dve.wait_ge(s.turned, 1)
                for i in range(3):
                    n = 512 if i < 2 else 256
                    c = nc.vector.tensor_copy(rows[:, 512 * i:512 * i + n], pt[0:8, i, 0:n])
                step(c)
                step(nc.vector.tensor_reduce(first, rows[:, T:], AX, ALU.max))
                toks = rows[:, 0:T]
                nc.vector.tensor_tensor_scan(S.M[0][:, :], toks, toks, first, ALU.max, ALU.max).then_inc(s.max, 1)
                nc.vector.tensor_tensor_scan(S.M[1][:, ::-1], toks[:, ::-1], toks[:, ::-1], first, ALU.max,
                                             ALU.max).then_inc(s.max, 1)
                dve.wait_ge(s.Mt, 1)
                for d in range(2):
                    v = pm[:, 64 * d:64 * d + 64].rearrange("p (i n) -> p i n", n=8)[:, :, 4 * d:4 * d + 4]
                    c = nc.vector.tensor_copy(S.expn[:, :, 4 * d:4 * d + 4], v)
                step(c)
                nc.vector.tensor_tensor(S.expn, S.expn, b[:, 0:NT, :], ALU.add).then_inc(s.act, 1)
                for d in range(2):
                    nc.vector.tensor_scalar(S.M[d][:, :], S.M[d][:, :], -1.0, None, ALU.mult)

            @block.scalar
            def _(act):
                act.wait_ge(s.act, 1)
                nc.scalar.activation(e, e, ACT.Exp).then_inc(s.exped, 1)
                act.wait_ge(s.exped, 1)
                nc.scalar.activation(ln, e, ACT.Ln, bias=1.0).then_inc(s.exped, 1)
                act.wait_ge(s.act, 2)
                nc.scalar.activation(S.expn, S.expn, ACT.Exp, scale=-1.0)

            @block.tensor
            def _(pe):
                pe.wait_ge(s.lf, 1)
                for d in range(2):
                    cut = slice(4 * d, 4 * d + 4)
                    for tiles, own, before in ((range(NT), S.t_le if d == 0 else S.t_ge, d == 0),
                                               (range(NT, N), S.t_gt if d == 0 else S.t_lt, d == 1)):
                        for i in tiles:
                            others = [r for r in tiles if (r < i if before else r > i)]
                            mm = pe.matmul(b[:, i, cut], own, lf[:, i, cut], start=True, stop=not others)
                            for r in others:
                                mm = pe.matmul(b[:, i, cut], S.ones, lf[:, r, cut], start=False,
                                               stop=(r == others[-1]))
                mm.then_inc(s.sums, 1)
                pe.wait_ge(s.a, 4)
                for i in range(N):
                    t = pe.transpose(pt[0:8, i // 4, (i % 4) * P:(i % 4 + 1) * P], S.a[:, i, :], S.ident)
                t.then_inc(s.turned, 1)
                pe.wait_ge(s.max, 2)
                for d in range(2):
                    for i in range(NT):
                        t = pe.transpose(pm[:, 64 * d + 8 * i:64 * d + 8 * i + 8],
                                         S.M[d][:, i * P:(i + 1) * P], S.ident[0:8, 0:8])
                t.then_inc(s.Mt, 1)


def stage_mlstm(nc, I, S):
    A = S.arena
    N = NT + NTC
    order = [NT, NT + 1] + list(range(NT))
    def span(d, i):
        if i >= NT:
            return 0, T
        return (i * P, T) if d == 0 else (0, (i + 1) * P)
    at, n = {}, 0
    for d in range(2):
        for i in order:
            at[d, i] = n
            n += span(d, i)[1] - span(d, i)[0]
    W = A.view(SV0, n)
    NM = A.view(SV0 + n, 2, T)
    Db = A.view(Z0 + 6 * T, 2, 2, T)
    den = A.view(M_SMALL + 150, NT)
    with ExitStack() as ctx:
        s = semaphores(nc, ctx, "ml", "rows rowsc scores e0 e1 m0 m1 w pv dve out")
        pS = psum(nc, ctx, "ml_s", 4, PSB)
        pN = psum(nc, ctx, "ml_n", 2, PSB)
        pO = psum(nc, ctx, "ml_o", 2, PSB)
        U = 2 * HEADS
        with nc.Block() as block:
            @block.tensor
            def _(pe):
                for h in range(HEADS):
                    part = slice(64 * (h % 2), 64 * (h % 2) + 64)
                    for d in range(2):
                        u = 2 * h + d
                        if u:
                            pe.wait_ge(s.rowsc, u)
                        for c in range(2):
                            n = 4 * d + h
                            mm = pe.matmul(pN[:, c, :], S.ident[0:8, n:n + 1].broadcast_to([8, P]),
                                           S.M[d][:, c * HALF:(c + 1) * HALF], start=True, stop=True)
                        mm.then_inc(s.rows, 1)
                    for o, i in enumerate(order):
                        t = N * h + o
                        if t >= 2:
                            pe.wait_ge(s.w, 2 * (t - 1))
                        key = (S.kc[part, h // 2, (i - NT) * P:(i - NT + 1) * P] if i >= NT else
                               S.z[part, 2 + h // 2, i * P:(i + 1) * P])
                        for c in range(2):
                            mm = pe.matmul(pS[:, 2 * (t % 2) + c, :], key,
                                           S.z[part, h // 2, c * HALF:(c + 1) * HALF], start=True, stop=True)
                        mm.then_inc(s.scores, 1)
                    pe.wait_ge(s.w, 2 * N * (h + 1))
                    for d in range(2):
                        u = 2 * h + d
                        if u:
                            pe.wait_ge(s.out, u)
                        for j in range(NT):
                            seen = [i for i in order if i >= NT or (i <= j if d == 0 else i >= j)]
                            for i in seen:
                                a0 = at[d, i] + j * P - span(d, i)[0]
                                mm = pe.matmul(pO[:, j // 4, (j % 4) * 65:(j % 4) * 65 + 65], W[:, a0:a0 + P],
                                               S.vt[:, i * HEADS + h, :], start=(i == seen[0]),
                                               stop=(i == seen[-1]))
                        mm.then_inc(s.pv, 1)

            @block.scalar
            def _(act):
                for h in range(HEADS):
                    for d in range(2):
                        u = 2 * h + d
                        act.wait_ge(s.rows, u + 1)
                        if h:
                            act.wait_ge(s.e0 if d == 0 else s.e1, N * h)
                        nc.scalar.activation(NM[:, d, :], pN[:, :, :].rearrange("p a b -> p (a b)"),
                                             ACT.Copy).then_inc(s.rowsc, 1)
                    act.wait_ge(s.rowsc, 2 * h + 2)
                    for o, i in enumerate(order):
                        t = N * h + o
                        if t >= 2:
                            act.wait_ge(s.w, 2 * (t - 1))
                        for d in range(2):
                            a, b = span(d, i)
                            nc.scalar.activation(Db[:, t % 2, d, a:b], NM[:, d, a:b], ACT.Exp,
                                                 bias=S.a[:, i, 4 * d + h:4 * d + h + 1])\
                                .then_inc((s.e0, s.e1)[d], 1)

            @block.gpsimd
            def _(pool):
                for h in range(HEADS):
                    for o, i in enumerate(order):
                        t = N * h + o
                        if i >= NT:
                            continue
                        for d in range(2):
                            pool.wait_ge((s.e0, s.e1)[d], t + 1)
                            blk = Db[:, t % 2, d, i * P:(i + 1) * P]
                            sign = 1 if d == 0 else -1
                            pool.affine_select(out=blk, in_=blk, compare_op=ALU.is_ge, fill=0.0, base=0,
                                               pattern=[[sign, P]], channel_multiplier=-sign)\
                                .then_inc((s.m0, s.m1)[d], 1)

            @block.vector
            def _(dve):
                step = Chain(dve, s.dve)
                for h in range(HEADS):
                    if h:
                        dve.wait_ge(s.pv, 2 * h)
                    for o, i in enumerate(order):
                        t = N * h + o
                        dve.wait_ge(s.scores, t + 1)
                        for d in range(2):
                            a, b = span(d, i)
                            if i >= NT:
                                dve.wait_ge((s.e0, s.e1)[d], t + 1)
                            else:
                                dve.wait_ge((s.m0, s.m1)[d], NT * h + i + 1)
                            sc = pS[:, 2 * (t % 2):2 * (t % 2) + 2, :].rearrange("p a b -> p (a b)")
                            nc.vector.scalar_tensor_tensor(out=W[:, at[d, i]:at[d, i] + b - a], in0=sc[:, a:b],
                                                           scalar=HD ** -0.5, in1=Db[:, t % 2, d, a:b],
                                                           op0=ALU.mult, op1=ALU.mult).then_inc(s.w, 1)
                    for d in range(2):
                        u = 2 * h + d
                        dve.wait_ge(s.pv, u + 1)
                        o = pO[:, :, 0:260].rearrange("p c (j d) -> p c j d", d=65)
                        dd = den.rearrange("p (c j) -> p c j", c=2)
                        step(nc.vector.tensor_copy(dd, o[:, :, :, 64]))
                        step(nc.vector.scalar_tensor_tensor(out=den, in0=den, scalar=-1.0, in1=den,
                                                            op0=ALU.mult, op1=ALU.max))
                        step(nc.vector.tensor_tensor(den, den, S.expn[:, :, 4 * d + h], ALU.max))
                        step(nc.vector.reciprocal(den, den))
                        for c in range(2):
                            hv = S.htok[:, 4 * c:4 * c + 4, h, :]
                            rb = den[:, 4 * c:4 * c + 4].unsqueeze(2).broadcast_to([P, 4, HD])
                            src = o[:, c, :, 0:64]
                            if d == 0:
                                k = nc.vector.tensor_tensor(hv, src, rb, ALU.mult)
                            else:
                                tmp = S.htmp[:, c, :, :]
                                k = nc.vector.tensor_tensor(tmp, src, rb, ALU.mult)
                        if d == 0:
                            k.then_inc(s.out, 1)
                        else:
                            k.then_inc(s.out, 1)
                            dve.wait_ge(s.out, u + 1)
                            step(nc.vector.tensor_tensor(S.htok[:, :, h, :], S.htok[:, :, h, :],
                                                         S.htmp.rearrange("p c j d -> p (c j) d"), ALU.add))


def stage_mlstm_out(nc, I, S):
    A = S.arena
    h = S.htok
    NH = NT * HEADS
    flat = h.rearrange("p i h d -> p (i h) d")
    sq = A.view(SV0, NH, HD)
    mu = A.view(WR0 + 4096, NH)
    rs = A.view(WR0 + 4200, NH)
    with ExitStack() as ctx:
        s = semaphores(nc, ctx, "mo", "dve root turned out")
        ps = psum(nc, ctx, "mo_ps", 4, PSB)
        with nc.Block() as block:
            @block.vector
            def _(dve):
                step = Chain(dve, s.dve)
                step(nc.vector.tensor_reduce(mu, flat, AX, ALU.add))
                step(nc.vector.tensor_scalar(mu, mu, 1.0 / HD, None, ALU.mult))
                step(nc.vector.tensor_tensor(flat, flat, mu.unsqueeze(2).broadcast_to([P, NH, HD]), ALU.subtract))
                step(nc.vector.tensor_tensor(sq, flat, flat, ALU.mult))
                step(nc.vector.tensor_reduce(rs, sq, AX, ALU.add))
                nc.vector.tensor_scalar(rs, rs, 1.0 / HD, LN_EPS, ALU.mult, ALU.add).then_inc(s.root, 1)
                dve.wait_ge(s.root, 2)
                step(nc.vector.reciprocal(rs, rs))
                step(nc.vector.tensor_tensor(flat, flat, rs.unsqueeze(2).broadcast_to([P, NH, HD]), ALU.mult))
                for n in range(4):
                    c, half = n // 2, n % 2
                    cut = slice(half * HALF, (half + 1) * HALF)
                    dve.wait_ge(s.turned, n + 1)
                    nc.vector.scalar_tensor_tensor(out=S.yT[:, c, cut], in0=ps[:, n, :],
                                                   scalar=col(S, "mlstm_norm_w", c), in1=S.z[:, 4 + c, cut],
                                                   op0=ALU.mult, op1=ALU.mult)

            @block.scalar
            def _(act):
                act.wait_ge(s.root, 1)
                nc.scalar.activation(rs, rs, ACT.Sqrt).then_inc(s.root, 1)

            @block.tensor
            def _(pe):
                pe.wait_ge(s.dve, 7)
                for n in range(4):
                    c, half = n // 2, n % 2
                    for i in range(4):
                        t = pe.transpose(ps[:, n, i * P:(i + 1) * P],
                                         h[:, 4 * half + i, 2 * c:2 * c + 2, :].rearrange("p h d -> p (h d)"),
                                         S.ident)
                    t.then_inc(s.turned, 1)



TWO_PI = 2.0 * math.pi
PI_A = 6.28125
PI_B = 0.0019350051879882812
PI_C = TWO_PI - PI_A - PI_B
MAGIC = 12582912.0


def complex_times(step, nc, out, a, b, tmp):
    (o_re, o_im), (a_re, a_im), (b_re, b_im) = out, a, b
    nc.vector.tensor_tensor(tmp, a_im, b_im, ALU.mult)
    step(nc.vector.tensor_tensor(o_re, a_re, b_re, ALU.mult))
    step(nc.vector.tensor_tensor(o_re, o_re, tmp, ALU.subtract))
    nc.vector.tensor_tensor(tmp, a_im, b_re, ALU.mult)
    step(nc.vector.tensor_tensor(o_im, a_re, b_im, ALU.mult))
    step(nc.vector.tensor_tensor(o_im, o_im, tmp, ALU.add))


def s5_views(S):
    A = S.arena
    V = Views()
    DT = 2 * KT
    z = Z0 + 6 * T
    V.ca = [A.view(z + i * DT * 9 * S5P, DT, 9 * S5P) for i in range(2)]
    z += 2 * DT * 9 * S5P
    V.bb = [A.view(z + i * DT * S5P, DT, S5P) for i in range(2)]
    z += 2 * DT * S5P
    V.pw = [A.view(z + i * DT * 9, 9, DT) for i in range(2)]
    z += 2 * DT * 9
    V.p = [A.view(z + i * DT, DT) for i in range(24)]
    z += 24 * DT
    assert z <= Z0 + 12 * T
    V.K = A.view(SV0, S5G, P)
    V.wvT = [A.view(WR0 + i * 2048, DT, P) for i in range(2)]
    V.wv = [A.view(WR0 + 4096 + i * 2048, DT, S5L * S5P) for i in range(2)]
    V.tab = [A.view(WR0 + 4096 + i * 2560, DT, S5CC + S5C) for i in range(2)]
    V.T = [A.view(H0, S5G, P), A.view(C0, S5G, P)]
    V.Kb = A.view(H0 + 6 * T, S5G, P)
    V.UT = A.view(X0, S5G, S5C + 2 * S5CC)
    V.st = [A.view(X0 + 3072 + i * 2560, DT, S5CC + S5C) for i in range(2)]
    V.yc = A.view(H0, S5L, W_MIX)
    V.ys = A.view(C0, 2, T)
    return V


def stage_s5_params(nc, I, S):
    V = s5_views(S)
    A = S.arena
    DT = 2 * KT
    ld, dt, are, aim, x, y, k1, k2, mag, cs, sn, a1, n1, q_re, q_im, w1, w2, w3, u_re, u_im, v_re, v_im, r8, w4 = V.p
    S.s5_r8, S.s5_u = r8, (u_re, u_im)
    br = [A.view(X0 + i * 128, KT, S5P) for i in range(2)]
    crow = [A.view(X0 + 256 + i * P, P) for i in range(2)]
    cT = [A.view(X0 + 512 + i * P, KT, S5P) for i in range(2)]
    arow = [A.view(X0 + 768 + i * P, P)[0:DT, :] for i in range(2)]
    dcol = A.view(X0 + 1024, S5G)
    ldrow = A.view(X0 + 1040, 2 * DT)
    drow = A.view(X0 + 1100, S5L, S5P)[0:S5G, :, :]
    big = A.view(X0 + 2048, DT * 9 * S5P)
    with ExitStack() as ctx:
        s = semaphores(nc, ctx, "s5", "in_a in_dt in_b in_c in_d turned dve a_dt a_sin a_out zeros shift T0 T1 ca wv wvd tc done"
                                      " shift2 mm")
        pt = psum(nc, ctx, "s5_t", PSB)
        pT = psum(nc, ctx, "s5_T", 4, PSB)
        pw_ps = psum(nc, ctx, "s5_w", 2, PSB)
        with nc.Block() as block:
            @block.sync
            def _(sp):
                for n, name in enumerate(("s5_a_re", "s5_a_im")):
                    sp.dma_start(arow[n], I[name].rearrange("l d (t e) n -> (l d t) (e n)", e=2)).then_inc(s.in_a, 16)
                sp.dma_start(ldrow, I["s5_log_dt"].rearrange("l d g -> l (d g)").broadcast_to([P, 2 * DT]))\
                    .then_inc(s.in_dt, 16)
                for n, name in enumerate(("s5_b_re", "s5_b_im")):
                    sp.dma_start(br[n], I[name].rearrange("l (t e) n p -> (e n) (l t) p", e=2)).then_inc(s.in_b, 16)
                for n, name in enumerate(("s5_c_re", "s5_c_im")):
                    for t in range(KT):
                        sp.dma_start(crow[n][16 * t:16 * t + 16, :].rearrange("p (e n) -> p e n", e=2),
                                     I[name][0, 2 * t:2 * t + 2].rearrange("e p n -> p e n")).then_inc(s.in_c, 16)
                sp.dma_start(drow, I["s5_d"].rearrange("l (g p) -> g l p", p=S5P).broadcast_to([S5G, S5L, S5P]))\
                    .then_inc(s.in_d, 16)
                for d in range(2):
                    sp.wait_ge(s.zeros, 2)
                    sp.wait_ge((s.T0, s.T1)[d], 4)
                    for j in range(S5L):
                        if d == 0:
                            dst, src = V.K[16 * j:16 * j + 16, :, 16 * j:P], V.T[0][0:16, :, 0:P - 16 * j]
                        else:
                            dst, src = V.Kb[16 * j:16 * j + 16, :, 0:16 * j + 16], V.T[1][0:16, :, 16 * (7 - j):P]
                        sp.dma_start(dst, src).then_inc((s.shift, s.shift2)[d], 16)

            @block.scalar
            def _(act):
                act.wait_ge(s.in_dt, 16)
                for e in range(2):
                    half = slice(64 * e, 64 * e + 64)
                    nc.scalar.activation(dt[half, :], ldrow[half, e::2], ACT.Exp).then_inc(s.a_dt, 1)
                act.wait_ge(s.a_sin, 1)
                nc.scalar.activation(sn, k1, ACT.Sin).then_inc(s.a_out, 1)
                nc.scalar.activation(cs, k2, ACT.Sin).then_inc(s.a_out, 1)
                nc.scalar.activation(mag, x, ACT.Exp).then_inc(s.a_out, 1)
                nc.scalar.activation(r8, x, ACT.Exp, scale=float(S5L)).then_inc(s.a_out, 1)

            @block.vector
            def _(dve):
                step = Chain(dve, s.dve)
                nc.vector.memset(V.K, 0.0).then_inc(s.zeros, 1)
                nc.vector.memset(V.Kb, 0.0).then_inc(s.zeros, 1)
                dve.wait_ge(s.turned, 1)
                nc.vector.tensor_copy(are, pt[:, 0:DT])
                step(nc.vector.tensor_copy(aim, pt[:, DT:2 * DT]))
                dve.wait_ge(s.a_dt, 2)
                step(nc.vector.tensor_tensor(x, are, dt, ALU.mult))
                step(nc.vector.tensor_tensor(y, aim, dt, ALU.mult))
                for k, quarter in ((k1, 0.0), (k2, 0.25)):
                    step(nc.vector.tensor_scalar(w1, y, 1.0 / TWO_PI, quarter, ALU.mult, ALU.add))
                    step(nc.vector.tensor_scalar(w1, w1, MAGIC, None, ALU.add))
                    step(nc.vector.tensor_scalar(w1, w1, -MAGIC, None, ALU.add))
                    step(nc.vector.scalar_tensor_tensor(out=k, in0=w1, scalar=-PI_A, in1=y, op0=ALU.mult, op1=ALU.add))
                    step(nc.vector.scalar_tensor_tensor(out=k, in0=w1, scalar=-PI_B, in1=k, op0=ALU.mult, op1=ALU.add))
                    step(nc.vector.scalar_tensor_tensor(out=k, in0=w1, scalar=-PI_C, in1=k, op0=ALU.mult, op1=ALU.add))
                    if quarter:
                        step(nc.vector.tensor_scalar(k, k, math.pi / 2, None, ALU.add))
                    step(nc.vector.tensor_scalar(k, k, 3.1415925, -3.1415925, ALU.min, ALU.max))
                nc.vector.memset(V.pw[0][:, 0, :], 1.0)
                nc.vector.memset(V.pw[1][:, 0, :], 0.0).then_inc(s.a_sin, 1)
                dve.wait_ge(s.a_out, 4)
                nc.vector.tensor_tensor(V.pw[0][:, 1, :], mag, cs, ALU.mult)
                step(nc.vector.tensor_tensor(V.pw[1][:, 1, :], mag, sn, ALU.mult))
                pw = lambda a, b: tuple(v[:, a:b, :] for v in V.pw)
                one = lambda a, n: tuple(v[:, a:a + 1, :].broadcast_to([P, n, DT]) for v in V.pw)
                tmp = big[:, 0:4 * DT].rearrange("p (k n) -> p k n", n=DT)
                complex_times(step, nc, pw(2, 3), pw(1, 2), pw(1, 2), tmp[:, 0:1, :])
                complex_times(step, nc, pw(3, 5), pw(1, 3), one(2, 2), tmp[:, 0:2, :])
                complex_times(step, nc, pw(5, 9), pw(1, 5), one(4, 4), tmp)
                step(nc.vector.tensor_scalar(a1, V.pw[0][:, 1, :], -1.0, None, ALU.add))
                nc.vector.tensor_tensor(w1, are, are, ALU.mult)
                step(nc.vector.tensor_tensor(w2, aim, aim, ALU.mult))
                step(nc.vector.tensor_tensor(w1, w1, w2, ALU.add))
                step(nc.vector.reciprocal(w1, w1))
                step(nc.vector.tensor_tensor(w2, are, w1, ALU.mult))
                step(nc.vector.tensor_tensor(w3, aim, w1, ALU.mult))
                step(nc.vector.tensor_scalar(w3, w3, -1.0, None, ALU.mult))
                complex_times(step, nc, (q_re, q_im), (a1, V.pw[1][:, 1, :]), (w2, w3), n1)
                dve.wait_ge(s.in_b, 32)
                for d in range(2):
                    cut = slice(d * KT, (d + 1) * KT)
                    qb = tuple(v[:, cut].unsqueeze(2).broadcast_to([P, KT, S5P]) for v in (q_re, q_im))
                    complex_times(step, nc, tuple(v[:, cut, :] for v in V.bb), qb, br,
                                  big[:, 0:KT * S5P].rearrange("p (t q) -> p t q", q=S5P))
                dve.wait_ge(s.turned, 2)
                for n in range(2):
                    c = nc.vector.tensor_copy(cT[n], pt[:, 256 + n * P:256 + (n + 1) * P].rearrange(
                        "p (t q) -> p t q", q=S5P))
                step(c)
                for d in range(2):
                    for k in range(9):
                        r = k if d == 0 else 8 - k
                        cut = slice(d * KT, (d + 1) * KT)
                        out = tuple(v[:, cut, r * S5P:(r + 1) * S5P] for v in V.ca)
                        pk = tuple(v[:, k, cut].unsqueeze(2).broadcast_to([P, KT, S5P]) for v in V.pw)
                        t = big[:, 0:KT * S5P].rearrange("p (t q) -> p t q", q=S5P)
                        complex_times(step, nc, out, cT, pk, t)
                step(nc.vector.tensor_scalar(V.ca[1], V.ca[1], -1.0, None, ALU.mult))
                nc.vector.tensor_scalar(V.ca[0], V.ca[0], 1.0, None, ALU.mult).then_inc(s.ca, 1)
                for d in range(2):
                    for j in range(S5L):
                        k = 7 - j if d == 0 else j
                        cut = slice(d * KT, (d + 1) * KT)
                        out = tuple(v[:, cut, j * S5P:(j + 1) * S5P] for v in V.wv)
                        pk = tuple(v[:, k, cut].unsqueeze(2).broadcast_to([P, KT, S5P]) for v in V.pw)
                        t = big[:, 0:KT * S5P].rearrange("p (t q) -> p t q", q=S5P)
                        complex_times(step, nc, out, tuple(v[:, cut, :] for v in V.bb), pk, t)
                nc.vector.memset(w4, 0.0).then_inc(s.wv, 1)
                complex_times(step, nc, (v_re, v_im), (cs, sn), (cs, sn), w1)
                complex_times(step, nc, (u_re, u_im), (v_re, v_im), (v_re, v_im), w1)
                complex_times(step, nc, (v_re, v_im), (u_re, u_im), (u_re, u_im), w1)
                nc.vector.tensor_tensor(w1, v_re, v_re, ALU.mult)
                step(nc.vector.tensor_tensor(w2, v_im, v_im, ALU.mult))
                step(nc.vector.tensor_tensor(w1, w1, w2, ALU.add))
                step(nc.vector.tensor_scalar(w1, w1, -0.5, 1.5, ALU.mult, ALU.add))
                nc.vector.tensor_tensor(u_re, v_re, w1, ALU.mult)
                step(nc.vector.tensor_tensor(u_im, v_im, w1, ALU.mult))
                for d in range(2):
                    for b in range(4):
                        dve.wait_ge(s.mm, 4 * d + b + 1)
                        g0 = 8 * (b // 2) + b % 2
                        nc.vector.tensor_copy(V.T[d][0:16, g0:g0 + 7:2, :],
                                              pT[0:16, b, :].rearrange("p (g n) -> p g n", g=4))\
                            .then_inc((s.T0, s.T1)[d], 1)
                for n in range(8):
                    dve.wait_ge(s.wvd, n + 1)
                    ri, q = n // 4, n % 4
                    nc.vector.tensor_copy(V.wvT[ri][:, 4 * q:4 * q + 4, :],
                                          pw_ps[:, n % 2, :].rearrange("p (t n) -> p t n", t=4)).then_inc(s.tc, 1)
                dve.wait_ge(s.shift, 16 * S5L)
                dve.wait_ge(s.shift2, 16 * S5L)
                dve.wait_ge(s.turned, 3)
                nc.vector.tensor_copy(dcol, pt[:, 64:64 + S5G])
                step(nc.vector.tensor_tensor(V.K, V.K, V.Kb, ALU.add))
                for g in range(S5G):
                    nc.vector.scalar_tensor_tensor(out=V.K[:, g, :], in0=S.ident, scalar=dcol[:, g:g + 1],
                                                   in1=V.K[:, g, :], op0=ALU.mult, op1=ALU.add)

            @block.tensor
            def _(pe):
                pe.wait_ge(s.in_a, 32)
                for n in range(2):
                    t = pe.transpose(pt[:, DT * n:DT * (n + 1)], arow[n], S.ident[0:DT, 0:DT])
                t.then_inc(s.turned, 1)
                pe.wait_ge(s.in_c, 16 * 2 * KT)
                pe.wait_ge(s.dve, 1)
                for n in range(2):
                    t = pe.transpose(pt[:, 256 + n * P:256 + (n + 1) * P], crow[n], S.ident)
                t.then_inc(s.turned, 1)
                pe.wait_ge(s.ca, 1)
                pe.wait_ge(s.in_d, 16)
                pe.transpose(pt[:, 64:64 + S5G], drow.rearrange("g j p -> g (j p)"),
                             S.ident[0:S5G, 0:S5G]).then_inc(s.turned, 1)
                for d in range(2):
                    for b in range(4):
                        if d:
                            pe.wait_ge(s.T0, b + 1)
                        for i in range(4):
                            g = 8 * (b // 2) + 2 * i + b % 2
                            part, t = slice(64 * (g % 2), 64 * (g % 2) + 64), d * KT + g // 2
                            o = pT[0:16, b, i * P:(i + 1) * P]
                            first = 0 if d == 0 else 1
                            for ri in range(2):
                                mm = pe.matmul(o, V.bb[ri][part, t, :],
                                               V.ca[ri][part, t, first * S5P:first * S5P + P],
                                               start=(ri == 0), stop=(ri == 1))
                        mm.then_inc(s.mm, 1)
                pe.wait_ge(s.wv, 1)
                for n in range(8):
                    ri, q = n // 4, n % 4
                    if n >= 2:
                        pe.wait_ge(s.tc, n - 1)
                    for i in range(4):
                        t = pe.transpose(pw_ps[:, n % 2, i * P:(i + 1) * P], V.wv[ri][:, 4 * q + i, :], S.ident)
                    t.then_inc(s.wvd, 1)


def stage_s5(nc, I, S):
    V = s5_views(S)
    A = S.arena
    DT = 2 * KT
    NS = S5CC + S5C
    r8, (u_re, u_im) = S.s5_r8, S.s5_u
    g_re, g_im, w1, w2 = (A.view(H0 + 6 * T + i * NS, NS) for i in range(4))
    lv = A.view(H0 + 6 * T + 4 * NS, 2, DT)
    lw = A.view(H0 + 6 * T + 4 * NS + 2 * DT, 2, DT)
    big = A.view(H0, DT, 64)
    with ExitStack() as ctx:
        s = semaphores(nc, ctx, "s6", "dve turned ut v scanned out gelu turned2 table free")
        pu = psum(nc, ctx, "s6_u", 2, PSB)
        pv = psum(nc, ctx, "s6_v", 2, PSB)
        po = psum(nc, ctx, "s6_o", 4, PSB)
        with nc.Block() as block:
            @block.tensor
            def _(pe):
                for g in range(S5G):
                    if g >= 2:
                        pe.wait_ge(s.ut, g - 1)
                    pe.transpose(pu[:, g % 2, 0:S5C], S.u5[:, g, :, :].rearrange("c j p -> c (j p)"), S.ident)
                    pe.transpose(pu[:, g % 2, S5C:NS], S.u5c[0:S5CC, g, :, :].rearrange("c j p -> c (j p)"),
                                 S.ident[0:S5CC, 0:S5CC]).then_inc(s.turned, 1)
                pe.wait_ge(s.ut, S5G)
                for n in range(DT):
                    d, t = n // KT, n % KT
                    if n >= 2:
                        pe.wait_ge(s.scanned, n - 1)
                    for ri in range(2):
                        for e in range(2):
                            g = 2 * t + e
                            mm = pe.matmul(pv[64 * e:64 * e + 64, n % 2, ri * NS:(ri + 1) * NS],
                                           V.wvT[ri][:, n, 64 * e:64 * e + 64],
                                           V.UT[:, g, S5CC * d:S5CC * d + NS], start=True, stop=True)
                    mm.then_inc(s.v, 1)
                pe.wait_ge(s.table, 1)
                for b in range(4):
                    for i in range(4):
                        g = 8 * (b // 2) + 2 * i + b % 2
                        o = po[:, b, i * P:(i + 1) * P]
                        part = slice(64 * (g % 2), 64 * (g % 2) + 64)
                        pe.matmul(o, V.UT[:, g, S5CC:NS], V.K[:, g, :], start=True, stop=False)
                        for d in range(2):
                            t = d * KT + g // 2
                            first = S5P if d == 0 else 0
                            c0 = S5CC - 1 if d == 0 else 1
                            for ri in range(2):
                                mm = pe.matmul(o, V.st[ri][part, t, c0:c0 + S5C],
                                               V.ca[ri][part, t, first:first + P], start=False,
                                               stop=(d == 1 and ri == 1))
                    mm.then_inc(s.out, 1)
                pe.wait_ge(s.gelu, 4)
                for j in range(S5L):
                    if j >= 2:
                        pe.wait_ge(s.free, j - 1)
                    for c in range(2):
                        t = pe.transpose(pu[:, j % 2, c * P:(c + 1) * P], V.yc[:, j, c * P:(c + 1) * P], S.ident)
                    t.then_inc(s.turned2, 1)

            @block.scalar
            def _(act):
                for b in range(4):
                    act.wait_ge(s.out, b + 1)
                    g0 = 8 * (b // 2) + b % 2
                    nc.scalar.activation(
                        V.yc.rearrange("c j (g p) -> c g j p", g=S5G)[:, g0:g0 + 7:2, :, :],
                        po[:, b, :].rearrange("c (g j p) -> c g j p", g=4, j=S5L),
                        ACT.Gelu_apprx_tanh).then_inc(s.gelu, 1)

            @block.vector
            def _(dve):
                step = Chain(dve, s.dve)
                for g in range(S5G):
                    dve.wait_ge(s.turned, g + 1)
                    nc.vector.tensor_copy(V.UT[:, g, S5CC:S5CC + NS], pu[:, g % 2, 0:NS])
                    nc.vector.tensor_copy(V.UT[:, g, 0:S5CC], pu[:, g % 2, S5C:NS]).then_inc(s.ut, 1)
                tr, ti = V.tab
                nc.vector.memset(tr[:, :, 0:1], 1.0)
                nc.vector.memset(ti[:, :, 0:1], 0.0)
                nc.vector.tensor_copy(tr[:, :, 1:2], u_re.unsqueeze(2))
                nc.vector.tensor_scalar(ti[:, :, 1:2], u_im.unsqueeze(2), -1.0, None, ALU.mult)
                step(nc.vector.tensor_copy(lv[:, 0, :], u_re))
                step(nc.vector.tensor_scalar(lv[:, 1, :], u_im, -1.0, None, ALU.mult))
                n = 2
                a, b = lv, lw
                while n < NS:
                    complex_times(step, nc, (b[:, 0, :], b[:, 1, :]), (a[:, 0, :], a[:, 1, :]),
                                  (a[:, 0, :], a[:, 1, :]), g_re[:, 0:DT])
                    a, b = b, a
                    for c0 in range(0, min(n, NS - n), 64):
                        m = min(n - c0, NS - n - c0, 64)
                        up = tuple(a[:, ri, :].unsqueeze(2).broadcast_to([P, DT, m]) for ri in range(2))
                        complex_times(step, nc, tuple(v[:, :, n + c0:n + c0 + m] for v in V.tab),
                                      tuple(v[:, :, c0:c0 + m] for v in V.tab), up, big[:, :, 0:m])
                    n *= 2
                for n in range(DT):
                    d = n // KT
                    way = slice(None) if d == 0 else slice(None, None, -1)
                    tre, tim = tr[:, n, :][:, way], ti[:, n, :][:, way]
                    v_re, v_im = pv[:, n % 2, 0:NS], pv[:, n % 2, NS:2 * NS]
                    dve.wait_ge(s.v, n + 1)
                    nc.vector.tensor_tensor(w1, v_im, tim, ALU.mult)
                    nc.vector.tensor_tensor(w2, v_im, tre, ALU.mult)
                    nc.vector.tensor_tensor(g_re, v_re, tre, ALU.mult)
                    nc.vector.tensor_tensor(g_im, v_re, tim, ALU.mult).then_inc(s.scanned, 1)
                    dve.wait_ge(s.scanned, n + 1)
                    nc.vector.tensor_tensor(g_re, g_re, w1, ALU.subtract)
                    step(nc.vector.tensor_tensor(g_im, g_im, w2, ALU.add))
                    rate = r8[:, n:n + 1].broadcast_to([P, NS])
                    for g in (g_re, g_im):
                        c = nc.vector.tensor_tensor_scan(g[:, way], rate, g[:, way], 0.0, ALU.mult, ALU.add)
                    step(c)
                    nc.vector.tensor_tensor(w1, g_im, tim, ALU.mult)
                    nc.vector.tensor_tensor(w2, g_re, tim, ALU.mult)
                    nc.vector.tensor_tensor(V.st[0][:, n, :], g_re, tre, ALU.mult)
                    step(nc.vector.tensor_tensor(V.st[1][:, n, :], g_im, tre, ALU.mult))
                    nc.vector.tensor_tensor(V.st[0][:, n, :], V.st[0][:, n, :], w1, ALU.add)
                    step(nc.vector.tensor_tensor(V.st[1][:, n, :], V.st[1][:, n, :], w2, ALU.subtract))
                nc.vector.memset(lv[:, 0, 0:1], 0.0).then_inc(s.table, 1)
                ys = V.ys.rearrange("p c (k j) -> p c k j", j=S5L)
                for j in range(S5L):
                    dve.wait_ge(s.turned2, j + 1)
                    nc.vector.tensor_copy(ys[:, :, :, j], pu[:, j % 2, 0:256].rearrange("p (c k) -> p c k", c=2))\
                        .then_inc(s.free, 1)


def stage_s5_glu(nc, I, S):
    V = s5_views(S)
    A = S.arena
    gw = A.view(WR0, 2, W_MIX)
    sig = A.view(WR0 + 512, 2, T)
    with ExitStack() as ctx:
        s = semaphores(nc, ctx, "s7", "w done sig")
        ps = psum(nc, ctx, "s7_ps", 4, PSB)
        with nc.Block() as block:
            @block.sync
            def _(sp):
                sp.dma_start(gw, I["s5_glu_w"].rearrange("l (k p) n -> p (l k) n", p=P)).then_inc(s.w, 16)

            @block.tensor
            def _(pe):
                pe.wait_ge(s.w, 16)
                for n in range(4):
                    m, h = n // 2, n % 2
                    for k in range(2):
                        mm = pe.matmul(ps[:, n, :], gw[:, k, m * P:(m + 1) * P], V.ys[:, k, h * HALF:(h + 1) * HALF],
                                       start=(k == 0), stop=(k == 1))
                    mm.then_inc(s.done, 1)

            @block.scalar
            def _(act):
                for n in range(4):
                    m, h = n // 2, n % 2
                    act.wait_ge(s.done, n + 1)
                    nc.scalar.activation(sig[:, m, h * HALF:(h + 1) * HALF], ps[:, n, :], ACT.Sigmoid,
                                         bias=col(S, "s5_glu_b", m)).then_inc(s.sig, 1)

            @block.vector
            def _(dve):
                for m in range(2):
                    dve.wait_ge(s.sig, 2 * m + 2)
                    nc.vector.tensor_tensor(S.yT[:, 6 + m, :], V.ys[:, m, :], sig[:, m, :], ALU.mult)



def copy_stage(nc, name, dst, src):
    with ExitStack() as ctx:
        s = semaphores(nc, ctx, name, "copied")
        with nc.Block() as block:
            @block.sync
            def _(sp):
                sp.dma_start(dst, src).then_inc(s.copied, 16)
                sp.wait_ge(s.copied, 16)


def stage_keep_x(nc, I, S):
    copy_stage(nc, "keep", S.kept[0], S.arena.view(X0, TILE8))


def stage_back_x(nc, I, S):
    copy_stage(nc, "back", S.arena.view(X0, TILE8), S.kept[0])


def stage_w_out_1(nc, I, S):
    r = S.arena.view(Z0, KT, T)
    w = I["w_out"].rearrange("l (k p) n -> p (l k) n", p=P)

    def evac(dve, bank, m, h):
        cut = slice(h * HALF, (h + 1) * HALF)
        return dve.scalar_tensor_tensor(out=r[:, m, cut], in0=bank, scalar=S.mod[:, m + 16, 0:1],
                                        in1=S.xT[:, m, cut], op0=ALU.mult, op1=ALU.add)

    dense(nc, S, "wo", lambda m: w[:, :, bass.ts(m, P)], KT, KT, lambda k: S.yT[:, k, :], T, evac, Z0 + TILE8,
          evac_engine="vector")

    def final(act, k, h, cut):
        nc.scalar.activation(S.xT[:, k, cut], r[:, k, cut], ACT.Identity, bias=S.x_b[:, k:k + 1],
                             scale=S.x_w[:, k:k + 1])
        nc.scalar.activation(S.hT[:, k, cut], r[:, k, cut], ACT.Identity, bias=S.h_b[:, k:k + 1],
                             scale=S.h_w[:, k:k + 1])

    tmp = S.arena.view(Z0 + TILE8, KT, T)
    rs = S.arena.view(Z0 + 2 * TILE8, T)
    normalize(nc, S, "n1", lambda k: r[:, k, :], KT, D, LN_EPS, True, lambda k: tmp[:, k, :], rs, final)


def stage_ffn_in(nc, I, S):
    w = I["w_ffn_in"].rearrange("l (k p) n -> p (l k) n", p=P)
    with ExitStack() as ctx:
        s = semaphores(nc, ctx, "f1", "w0 w1 w2 w3 done silu free")
        ring = Z0 + FT * T
        slots = [S.arena.view(ring + i * KT * P, KT, P) for i in range(4)]
        tmp = [S.arena.view(ring + 4 * KT * P + i * HALF, HALF) for i in range(4)]
        loaded = [s.w0, s.w1, s.w2, s.w3]
        ps = psum(nc, ctx, "f1_ps", 8, PSB)
        def weights(m, j):
            return w[:, :, bass.ds(m * P + (j // 2) * P + (j % 2) * D_FF, P)]
        with nc.Block() as block:
            @block.sync
            def _(sp):
                for j in range(4):
                    sp.dma_start(slots[j], weights(0, j)).then_inc(loaded[j], 16)
                with sp.Fori(1, FT // 2) as i:
                    for j in range(4):
                        if j % 2 == 0:
                            sp.wait_ge(s.done, i * 4 + (j - 2))
                        sp.dma_start(slots[j], weights(i * 2, j)).then_inc(loaded[j], 16)

            @block.tensor
            def _(pe):
                with pe.Fori(0, FT // 2) as i:
                    for q in range(2):
                        pe.wait_ge(loaded[2 * q], i * 16 + 16)
                        pe.wait_ge(loaded[2 * q + 1], i * 16 + 16)
                        for h in range(2):
                            n = 2 * q + h
                            pe.wait_ge(s.free, i * 4 + (n + 1))
                            for e in range(2):
                                for k in range(KT):
                                    mm = pe.matmul(ps[:, 2 * n + e, :], slots[2 * q + e][:, k, :],
                                                   S.hT[:, k, h * HALF:(h + 1) * HALF],
                                                   start=(k == 0), stop=(k == KT - 1))
                            mm.then_inc(s.done, 1)

            @block.scalar
            def _(act):
                with act.Fori(0, FT // 2) as i:
                    for n in range(4):
                        act.wait_ge(s.done, i * 4 + (n + 1))
                        act.wait_ge(s.free, i * 4 + (n + 1))
                        nc.scalar.activation(tmp[n], ps[:, 2 * n, :], ACT.Silu).then_inc(s.silu, 1)

            @block.vector
            def _(dve):
                dve.sem_inc(s.free, 4)
                with dve.Fori(0, FT // 2) as i:
                    for n in range(4):
                        dve.wait_ge(s.silu, i * 4 + (n + 1))
                        nc.vector.tensor_tensor(S.hid[:, i * 2 + n // 2, (n % 2) * HALF:(n % 2 + 1) * HALF],
                                                tmp[n], ps[:, 2 * n + 1, :], ALU.mult).then_inc(s.free, 1)


def stage_ffn_out(nc, I, S):
    w = I["w_ffn_out"].rearrange("l (k p) n -> p (l k) n", p=P)
    r = S.hT
    with ExitStack() as ctx:
        s = semaphores(nc, ctx, "f2", "w0 w1 done free")
        slots = [S.arena.view(Z0 + FT * T + i * FT * P, FT, P) for i in range(2)]
        loaded = [s.w0, s.w1]
        ps = psum(nc, ctx, "f2_ps", 8, PSB)
        with nc.Block() as block:
            @block.sync
            def _(sp):
                for j in range(2):
                    sp.dma_start(slots[j], w[:, :, bass.ts(j, P)]).then_inc(loaded[j], 16)
                with sp.Fori(1, KT // 2) as i:
                    for j in range(2):
                        sp.wait_ge(s.done, i * 4 + (2 * j - 2))
                        sp.dma_start(slots[j], w[:, :, bass.ts(i * 2 + j, P)]).then_inc(loaded[j], 16)

            @block.tensor
            def _(pe):
                with pe.Fori(0, KT // 2) as i:
                    for j in range(2):
                        pe.wait_ge(loaded[j], i * 16 + 16)
                        for h in range(2):
                            pe.wait_ge(s.free, i * 4 + (2 * j + h + 1))
                            for k in range(FT):
                                mm = pe.matmul(ps[:, 2 * j + h, :], slots[j][:, k, :],
                                               S.hid[:, k, h * HALF:(h + 1) * HALF],
                                               start=(k == 0), stop=(k == FT - 1))
                            mm.then_inc(s.done, 1)

            @block.vector
            def _(dve):
                dve.sem_inc(s.free, 4)
                with dve.Fori(0, KT // 2) as i:
                    for n in range(4):
                        cut = slice((n % 2) * HALF, (n % 2 + 1) * HALF)
                        m = i * 2 + n // 2
                        dve.wait_ge(s.done, i * 4 + (n + 1))
                        nc.vector.scalar_tensor_tensor(out=r[:, m, cut], in0=ps[:, n, :],
                                                       scalar=S.mod[:, m + 40, 0:1], in1=S.xT[:, m, cut],
                                                       op0=ALU.mult, op1=ALU.add).then_inc(s.free, 1)

    def final(act, k, h, cut):
        nc.scalar.activation(S.xT[:, k, cut], r[:, k, cut], ACT.Identity, bias=col(S, "ln2_b", k),
                             scale=col(S, "ln2_w", k))

    tmp = S.arena.view(Z0, KT, T)
    rs = S.arena.view(Z0 + TILE8, T)
    normalize(nc, S, "n2", lambda k: r[:, k, :], KT, D, LN_EPS, True, lambda k: tmp[:, k, :], rs, final)



MA0, ML0 = X0, X0 + 4 * T
QK0 = Z0
ZA0 = QK0 + 8 * T
VB0 = ZA0 + 4 * T
FD0 = VB0 + NT * ATT_W
FX0 = FD0 + 256


def stage_keep_x2(nc, I, S):
    copy_stage(nc, "keep2", S.kept[1], S.arena.view(X0, TILE8))


def stage_rms(nc, I, S):
    def final(act, k, h, cut):
        nc.scalar.activation(S.hT[:, k, cut], S.xT[:, k, cut], ACT.Copy, scale=col(S, "norm_g_2", k))

    tmp = S.arena.view(Z0, KT, T)
    rs = S.arena.view(Z0 + TILE8, T)
    normalize(nc, S, "n3", lambda k: S.xT[:, k, :], KT, D, EPS, False, lambda k: tmp[:, k, :], rs, final)


def stage_project_att(nc, I, S):
    w = I["w_in_2"].rearrange("l (k p) n -> p (l k) n", p=P)
    qk = S.arena.view(QK0, 8, T)
    za = S.arena.view(ZA0, 4, T)
    dense(nc, S, "pq", lambda m: w[:, :, bass.ts(m, P)], 8, KT, lambda k: S.hT[:, k, :], T,
          lambda act, bank, m, h: act.activation(qk[:, m, h * HALF:(h + 1) * HALF], bank, ACT.Copy), FX0)
    dense(nc, S, "pz", lambda m: w[:, :, bass.ds(m * P + ZA_OFF, P)], 4, KT, lambda k: S.hT[:, k, :], T,
          lambda act, bank, m, h: act.activation(za[:, m, h * HALF:(h + 1) * HALF], bank, ACT.Silu), FX0)


def project_tokens(nc, S, name, w, parts, at, evac):
    with ExitStack() as ctx:
        s = semaphores(nc, ctx, name, "w done free")
        ps = psum(nc, ctx, f"{name}_ps", 8, PSB)
        views = []
        for _, n in parts:
            views.append(S.arena.view(at, KT, n))
            at += KT * n
        jobs = [(i, q) for i in range(NT) for q in range(len(parts))]
        with nc.Block() as block:
            @block.sync
            def _(sp):
                for (off, n), v in zip(parts, views):
                    sp.dma_start(v, w[:, :, off:off + n]).then_inc(s.w, 16)

            @block.tensor
            def _(pe):
                pe.wait_ge(s.w, 16 * len(parts))
                for n, (i, q) in enumerate(jobs):
                    if n >= 8:
                        pe.wait_ge(s.free, n - 7)
                    for k in range(KT):
                        mm = pe.matmul(ps[:, n % 8, 0:parts[q][1]], S.hT[:, k, i * P:(i + 1) * P],
                                       views[q][:, k, :], start=(k == 0), stop=(k == KT - 1))
                    mm.then_inc(s.done, 1)

            @block.scalar
            def _(act):
                for n, (i, q) in enumerate(jobs):
                    act.wait_ge(s.done, n + 1)
                    evac(nc.scalar, ps[:, n % 8, 0:parts[q][1]], i, q).then_inc(s.free, 1)


def stage_project_att_tokens(nc, I, S):
    w = I["w_in_2"].rearrange("l (k p) n -> p (l k) n", p=P)
    v = S.arena.view(VB0, NT, ATT_W)
    fd = S.arena.view(FD0, NT, ATT_H + SSD_H)

    def evac(act, bank, i, q):
        out = (v[:, i, :], fd[:, i, 0:ATT_H], fd[:, i, ATT_H:])[q]
        return act.activation(out, bank, ACT.Copy)

    project_tokens(nc, S, "pv", w, [(V_OFF, ATT_W), (F_OFF, ATT_H), (DT_OFF, SSD_H)], FX0, evac)


def stage_att_norm(nc, I, S):
    A = S.arena
    qk = A.view(QK0, 8, T)
    fd = A.view(FD0, NT, ATT_H + SSD_H)
    sq = A.view(FX0, 2, T)
    rs = A.view(FX0 + 2 * T, 2, T)
    e, ln, w, lf, c = (A.view(FX0 + 4 * T + 64 * i, NT, ATT_H) for i in range(5))
    fb = A.view(FX0 + 4 * T + 320, ATT_H)
    gq = A.view(FX0 + 4 * T + 330, 1)
    with ExitStack() as ctx:
        s = semaphores(nc, ctx, "an", "bias dve act exped lf sums turned squared mean eps root scaled c")
        pm = psum(nc, ctx, "an_m", 4, PSB)
        pc = psum(nc, ctx, "an_c", PSB)
        pt = psum(nc, ctx, "an_t", 2, PSB)
        with nc.Block() as block:
            @block.sync
            def _(sp):
                sp.dma_start(fb, I["forget_b_2"].broadcast_to([P, ATT_H])).then_inc(s.bias, 16)

            @block.scalar
            def _(act):
                act.wait_ge(s.act, 1)
                nc.scalar.activation(e, e, ACT.Exp).then_inc(s.exped, 1)
                act.wait_ge(s.exped, 1)
                nc.scalar.activation(ln, e, ACT.Ln, bias=1.0).then_inc(s.exped, 1)
                for m in range(8):
                    if m >= 2:
                        act.wait_ge(s.mean, 2 * (m - 1))
                    nc.scalar.activation(sq[:, m % 2, :], qk[:, m, :], ACT.Square).then_inc(s.squared, 1)
                    act.wait_ge(s.eps, m + 1)
                    nc.scalar.activation(rs[:, m % 2, :], rs[:, m % 2, :], ACT.Sqrt).then_inc(s.root, 1)

            @block.tensor
            def _(pe):
                pe.wait_ge(s.lf, 1)
                for i in range(NT):
                    o = pc[:, i * ATT_H:(i + 1) * ATT_H]
                    mm = pe.matmul(o, S.t_le, lf[:, i, :], start=True, stop=(i == 0))
                    for r in range(i):
                        mm = pe.matmul(o, S.ones, lf[:, r, :], start=False, stop=(r == i - 1))
                mm.then_inc(s.sums, 1)
                pe.wait_ge(s.c, 1)
                for i in range(NT):
                    t = pe.transpose(pt[0:ATT_H, i // 4, (i % 4) * P:(i % 4 + 1) * P], c[:, i, :], S.ident)
                t.then_inc(s.turned, 1)
                for m in range(8):
                    pe.wait_ge(s.squared, m + 1)
                    if m >= 2:
                        pe.wait_ge(s.eps, m - 1)
                    for h in range(2):
                        pe.matmul(pm[:, 2 * (m % 2) + h, :], S.blk, sq[:, m % 2, h * HALF:(h + 1) * HALF],
                                  start=True, stop=True).then_inc(s.mean, 1)

            @block.vector
            def _(dve):
                step = Chain(dve, s.dve)
                dve.wait_ge(s.bias, 16)
                f = fd[:, :, 0:ATT_H]
                step(nc.vector.tensor_tensor(f, f, fb.unsqueeze(1).broadcast_to([P, NT, ATT_H]), ALU.add))
                step(nc.vector.tensor_scalar(w, f, -1.0, None, ALU.mult))
                nc.vector.tensor_tensor(e, w, f, ALU.min).then_inc(s.act, 1)
                dve.wait_ge(s.exped, 2)
                log1p_tail(step, nc, e, ln, w, w)
                step(nc.vector.tensor_scalar(lf, f, 0.0, None, ALU.min))
                nc.vector.tensor_tensor(lf, lf, w, ALU.subtract).then_inc(s.lf, 1)
                nc.vector.tensor_scalar(gq, col(S, "q_norm_g_2"), ATT_HD ** -0.5, None, ALU.mult)
                dve.wait_ge(s.sums, 1)
                nc.vector.tensor_scalar(c, pc[:, 0:NT * ATT_H].rearrange("p (i h) -> p i h", h=ATT_H), -1.0, None,
                                        ALU.mult).then_inc(s.c, 1)
                dve.wait_ge(s.turned, 1)
                step(nc.vector.tensor_copy(S.crow, pt[0:ATT_H, :, :].rearrange("p a b -> p (a b)")))
                for m in range(8):
                    dve.wait_ge(s.mean, 2 * m + 2)
                    nc.vector.tensor_scalar(rs[:, m % 2, :],
                                            pm[:, 2 * (m % 2):2 * (m % 2) + 2, :].rearrange("p a b -> p (a b)"),
                                            EPS, None, ALU.add).then_inc(s.eps, 1)
                    dve.wait_ge(s.root, m + 1)
                    step(nc.vector.reciprocal(rs[:, m % 2, :], rs[:, m % 2, :]))
                    g = gq if m < 4 else col(S, "k_norm_g_2")
                    step(nc.vector.scalar_tensor_tensor(out=qk[:, m, :], in0=qk[:, m, :], scalar=g,
                                                        in1=rs[:, m % 2, :], op0=ALU.mult, op1=ALU.mult))


def stage_attention(nc, I, S):
    A = S.arena
    qk = A.view(QK0, 8, T)
    v = A.view(VB0, NT, ATT_W)
    cb = A.view(FX0, 2, T)
    cd = A.view(FX0 + 2 * T, 2, T)
    L = A.view(FX0 + 4 * T, 2, T)
    PT = A.view(FX0 + 6 * T, 2, T)
    y = A.view(FX0 + 8 * T, NT, ATT_W)
    assert FX0 + 12 * T <= SIZE - 100
    mx = A.view(FX0 + 12 * T, 2, 2)
    nm = A.view(FX0 + 12 * T + 4, 2, 1)
    sm = A.view(FX0 + 12 * T + 8, 2, 1)
    units = [(h, i) for h in range(ATT_H) for i in range(NT)]
    with ExitStack() as ctx:
        s = semaphores(nc, ctx, "at", "rows rowsc masked scores logits m exped turned copied pv out inv")
        pr = psum(nc, ctx, "at_s", 4, PSB)
        pt = psum(nc, ctx, "at_t", 2, PSB)
        po = psum(nc, ctx, "at_o", 2, PSB)
        with nc.Block() as block:
            @block.tensor
            def _(pe):
                def row(h):
                    if h:
                        pe.wait_ge(s.copied, NT * h)
                    for c in range(2):
                        mm = pe.matmul(pt[:, c, :], S.ident[0:ATT_H, h:h + 1].broadcast_to([ATT_H, P]),
                                       S.crow[:, c * HALF:(c + 1) * HALF], start=True, stop=True)
                    mm.then_inc(s.rows, 1)

                def scores(u):
                    h, i = units[u]
                    part = slice(64 * (h % 2), 64 * (h % 2) + 64)
                    if u >= 2:
                        pe.wait_ge(s.logits, u - 1)
                    n = (i + 1) * P
                    for c in range(0, n, HALF):
                        w = min(HALF, n - c)
                        mm = pe.matmul(pr[:, 2 * (u % 2) + c // HALF, 0:w], qk[part, h // 2, i * P:(i + 1) * P],
                                       qk[part, 4 + h // 2, c:c + w], start=True, stop=True)
                    mm.then_inc(s.scores, 1)

                def turn(u):
                    h, i = units[u]
                    pe.wait_ge(s.exped, u + 1)
                    if u:
                        pe.wait_ge(s.copied, u)
                    if i == 0:
                        pe.wait_ge(s.rowsc, h + 1)
                    for b in range(i + 1):
                        t = pe.transpose(pt[:, b // 4, (b % 4) * P:(b % 4 + 1) * P], L[:, u % 2, b * P:(b + 1) * P],
                                         S.ident)
                    t.then_inc(s.turned, 1)

                def values(u):
                    h, i = units[u]
                    pe.wait_ge(s.copied, u + 1)
                    if u >= 2:
                        pe.wait_ge(s.out, u - 1)
                    for b in range(i + 1):
                        mm = pe.matmul(po[:, u % 2, 0:ATT_HD], PT[:, u % 2, b * P:(b + 1) * P],
                                       v[:, b, h * ATT_HD:(h + 1) * ATT_HD], start=(b == 0), stop=(b == i))
                    mm.then_inc(s.pv, 1)

                U = len(units)
                for u in range(U + 2):
                    if u < U:
                        if units[u][1] == 0:
                            if u:
                                turn(u - 1)
                            row(units[u][0])
                        scores(u)
                        if units[u][1] == 0:
                            if u:
                                values(u - 1)
                            continue
                    if 1 <= u <= U:
                        turn(u - 1)
                        values(u - 1)

            @block.scalar
            def _(act):
                def row(h):
                    act.wait_ge(s.rows, h + 1)
                    if h >= 2:
                        act.wait_ge(s.logits, NT * (h - 1))
                    nc.scalar.activation(cb[:, h % 2, :], pt[:, :, :].rearrange("p a b -> p (a b)"), ACT.Copy)\
                        .then_inc(s.rowsc, 1)

                def copy(u):
                    h, i = units[u]
                    act.wait_ge(s.turned, u + 1)
                    if u >= 2:
                        act.wait_ge(s.pv, u - 1)
                    n = (i + 1) * P
                    nc.scalar.activation(PT[:, u % 2, 0:n], pt[:, :, :].rearrange("p a b -> p (a b)")[:, 0:n],
                                         ACT.Copy).then_inc(s.copied, 1)

                for u, (h, i) in enumerate(units):
                    if i == 0:
                        if u:
                            copy(u - 1)
                        row(h)
                    act.wait_ge(s.m, u + 1)
                    if u >= 2:
                        act.wait_ge(s.out, u - 1)
                    n = (i + 1) * P
                    nc.scalar.activation(L[:, u % 2, 0:n], L[:, u % 2, 0:n], ACT.Exp, bias=nm[:, u % 2, :],
                                         accum_out=sm[:, u % 2, :]).then_inc(s.exped, 1)
                    if u and i:
                        copy(u - 1)
                copy(len(units) - 1)

            @block.gpsimd
            def _(pool):
                for h in range(ATT_H):
                    pool.wait_ge(s.rowsc, h + 1)
                    if h >= 2:
                        pool.wait_ge(s.logits, NT * (h - 1))
                    pool.affine_select(out=cd[:, h % 2, :].rearrange("p (i s) -> p i s", s=P),
                                       in_=cb[:, h % 2, :].rearrange("p (i s) -> p i s", s=P),
                                       compare_op=ALU.is_ge, fill=-1e30, base=0, pattern=[[0, NT], [-1, P]],
                                       channel_multiplier=1).then_inc(s.masked, 1)

            @block.vector
            def _(dve):
                def finish(u):
                    h, i = units[u]
                    dve.wait_ge(s.exped, u + 1)
                    nc.vector.reciprocal(sm[:, u % 2, :], sm[:, u % 2, :]).then_inc(s.inv, 1)
                    dve.wait_ge(s.inv, u + 1)
                    dve.wait_ge(s.pv, u + 1)
                    nc.vector.tensor_scalar(y[:, i, h * ATT_HD:(h + 1) * ATT_HD], po[:, u % 2, 0:ATT_HD],
                                            sm[:, u % 2, :], None, ALU.mult).then_inc(s.out, 1)

                for u, (h, i) in enumerate(units):
                    dve.wait_ge(s.scores, u + 1)
                    dve.wait_ge(s.masked, h + 1)
                    if u >= 2:
                        dve.wait_ge(s.turned, u - 1)
                    sc = pr[:, 2 * (u % 2):2 * (u % 2) + 2, :].rearrange("p a b -> p (a b)")
                    n = i * P
                    if i:
                        nc.vector.tensor_tensor_reduce(L[:, u % 2, 0:n], sc[:, 0:n], cb[:, h % 2, 0:n], 1.0, -3.0e38,
                                                       ALU.add, ALU.max, mx[:, u % 2, 0:1])
                    else:
                        nc.vector.memset(mx[:, u % 2, 0:1], -3.0e38)
                    nc.vector.tensor_tensor_reduce(L[:, u % 2, n:n + P], sc[:, n:n + P], cd[:, h % 2, n:n + P], 1.0,
                                                   -3.0e38, ALU.add, ALU.max, mx[:, u % 2, 1:2]).then_inc(s.logits, 1)
                    dve.wait_ge(s.logits, u + 1)
                    nc.vector.tensor_reduce(nm[:, u % 2, :], mx[:, u % 2, :], AX, ALU.max, negate=True)\
                        .then_inc(s.m, 1)
                    if u:
                        finish(u - 1)
                finish(len(units) - 1)

    za = A.view(ZA0, 4, T)
    mix = A.view(MA0, 4, T)
    with ExitStack() as ctx:
        s = semaphores(nc, ctx, "ao", "turned out")
        ps = psum(nc, ctx, "ao_ps", 8, PSB)
        with nc.Block() as block:
            @block.tensor
            def _(pe):
                for n in range(8):
                    m, half = n // 2, n % 2
                    for i in range(4):
                        t = pe.transpose(ps[:, n, i * P:(i + 1) * P], y[:, 4 * half + i, m * P:(m + 1) * P], S.ident)
                    t.then_inc(s.turned, 1)

            @block.vector
            def _(dve):
                for n in range(8):
                    m, cut = n // 2, slice((n % 2) * HALF, (n % 2 + 1) * HALF)
                    dve.wait_ge(s.turned, n + 1)
                    nc.vector.tensor_tensor(mix[:, m, cut], ps[:, n, :], za[:, m, cut], ALU.mult)


def dense_conv(nc, S, name, weights, n_tiles, taps, bias, out, ring_at, pad_at):
    pads = [S.arena.view(pad_at + j * (T + 4), T + 4) for j in range(4)]
    with ExitStack() as ctx:
        s = semaphores(nc, ctx, name, "w0 w1 w2 w3 bank_free done copied conv taps zero")
        slots = [S.arena.view(ring_at + i * KT * P, KT, P) for i in range(4)]
        loaded = [s.w0, s.w1, s.w2, s.w3]
        ps = psum(nc, ctx, f"{name}_ps", 8, PSB)
        with nc.Block() as block:
            @block.sync
            def _(sp):
                for j in range(4):
                    sp.dma_start(slots[j], weights(j)).then_inc(loaded[j], 16)
                if n_tiles > 4:
                    with sp.Fori(1, n_tiles // 4) as i:
                        for j in range(4):
                            sp.wait_ge(s.done, i * 8 + (2 * j - 6))
                            sp.dma_start(slots[j], weights(i * 4 + j)).then_inc(loaded[j], 16)

            @block.tensor
            def _(pe):
                with pe.Fori(0, n_tiles // 4) as i:
                    for j in range(4):
                        pe.wait_ge(loaded[j], i * 16 + 16)
                        for h in range(2):
                            pe.wait_ge(s.bank_free, i * 8 + (2 * j + h + 1))
                            for k in range(KT):
                                mm = pe.matmul(ps[:, 2 * j + h, :], slots[j][:, k, :],
                                               S.hT[:, k, h * HALF:(h + 1) * HALF],
                                               start=(k == 0), stop=(k == KT - 1))
                            mm.then_inc(s.done, 1)

            @block.scalar
            def _(act):
                act.sem_inc(s.bank_free, 8)
                with act.Fori(0, n_tiles // 4) as i:
                    for j in range(4):
                        act.wait_ge(s.conv, i * 4 + (j + 1))
                        for h in range(2):
                            act.wait_ge(s.done, i * 8 + (2 * j + h + 1))
                            nc.scalar.activation(pads[j][:, 4 + h * HALF:4 + (h + 1) * HALF], ps[:, 2 * j + h, :],
                                                 ACT.Copy).then_inc(s.bank_free, 1)

            @block.vector
            def _(dve):
                for j in range(4):
                    nc.vector.memset(pads[j][:, 0:4], 0.0).then_inc(s.zero, 1)
                dve.wait_ge(s.zero, 4)
                dve.sem_inc(s.conv, 4)
                with dve.Fori(0, n_tiles // 4) as i:
                    for j in range(4):
                        m = i * 4 + j
                        dve.wait_ge(s.bank_free, i * 8 + (2 * j + 10))
                        o = out[:, m, :]
                        nc.vector.tensor_scalar(o, pads[j][:, 1:1 + T], taps(m, 0), bias(m), ALU.mult, ALU.add)\
                            .then_inc(s.taps, 1)
                        for w in range(1, TAPS):
                            dve.wait_ge(s.taps, i * 12 + (3 * j + w))
                            c = nc.vector.scalar_tensor_tensor(out=o, in0=pads[j][:, 1 + w:1 + w + T],
                                                               scalar=taps(m, w), in1=o, op0=ALU.mult, op1=ALU.add)
                            c.then_inc(s.taps if w < TAPS - 1 else s.conv, 1)


def taps_of(S, name, n_tiles):
    at, _ = COL[name]
    return lambda m, w: S.cols[:, bass.ds(m + (at + w * n_tiles), 1)]


def stage_lru(nc, I, S):
    A = S.arena
    w = I["w_in_2"].rearrange("l (k p) n -> p (l k) n", p=P)
    at = QK0
    xc, r, g, m2 = (A.view(at + i * 4 * T, 4, T) for i in range(4))
    assert at + 16 * T <= FD0
    z = A.view(FX0, 4, T)
    ring = FX0 + 4 * T
    bd = A.view(FX0 + 4 * T, 8, P)
    bat, _ = COL["lru_conv_b_2"]
    dense_conv(nc, S, "lc", lambda m: w[:, :, bass.ds(m * P + XL_OFF, P)], 4, taps_of(S, "lru_conv_w_2", 4),
               lambda m: S.cols[:, bass.ds(m + bat, 1)], xc, ring, ring + 4 * KT * P)
    dense(nc, S, "lz", lambda m: w[:, :, bass.ds(m * P + ZL_OFF, P)], 4, KT, lambda k: S.hT[:, k, :], T,
          lambda act, bank, m, h: act.activation(z[:, m, h * HALF:(h + 1) * HALF], bank, ACT.Silu), ring)
    e, ln, ww, cl = (A.view(FX0 + 6 * T + i * 4, 4) for i in range(4))
    mix = A.view(ML0, 4, T)
    with ExitStack() as ctx:
        s = semaphores(nc, ctx, "lr", "zero bd act exped rate dve mm gates sq a th root h")
        ps = psum(nc, ctx, "lr_ps", 8, PSB)
        with nc.Block() as block:
            @block.sync
            def _(sp):
                sp.wait_ge(s.zero, 1)
                for n, name in enumerate(("lru_w_a_2", "lru_w_x_2")):
                    for e2 in range(2):
                        sp.dma_start(bd[64 * e2:64 * e2 + 64, 4 * n:4 * n + 4, 64 * e2:64 * e2 + 64],
                                     I[name].rearrange("l (t e) d o -> e d (l t) o", e=2)[e2]).then_inc(s.bd, 16)

            @block.tensor
            def _(pe):
                pe.wait_ge(s.bd, 64)
                for n in range(16):
                    gate, m, h = n // 8, (n // 2) % 4, n % 2
                    if n >= 8:
                        pe.wait_ge(s.gates, n - 7)
                    pe.matmul(ps[:, n % 8, :], bd[:, 4 * gate + m, :], xc[:, m, h * HALF:(h + 1) * HALF],
                              start=True, stop=True).then_inc(s.mm, 1)

            @block.scalar
            def _(act):
                act.wait_ge(s.act, 1)
                nc.scalar.activation(e, e, ACT.Exp).then_inc(s.exped, 1)
                act.wait_ge(s.exped, 1)
                nc.scalar.activation(ln, e, ACT.Ln, bias=1.0).then_inc(s.exped, 1)
                for n in range(16):
                    gate, m, h = n // 8, (n // 2) % 4, n % 2
                    act.wait_ge(s.mm, n + 1)
                    nc.scalar.activation((r, g)[gate][:, m, h * HALF:(h + 1) * HALF], ps[:, n % 8, :], ACT.Sigmoid,
                                         bias=col(S, ("lru_b_a_2", "lru_b_x_2")[gate], m)).then_inc(s.gates, 1)
                act.wait_ge(s.rate, 1)
                act.wait_ge(s.gates, 16)
                for m in range(4):
                    nc.scalar.activation(m2[:, m, :], r[:, m, :], ACT.Tanh, scale=cl[:, m:m + 1]).then_inc(s.th, 1)
                act.wait_ge(s.th, 4)
                act.wait_ge(s.act, 2)
                for m in range(4):
                    nc.scalar.activation(r[:, m, :], r[:, m, :], ACT.Exp, scale=cl[:, m:m + 1]).then_inc(s.a, 1)
                for m in range(4):
                    act.wait_ge(s.sq, m + 1)
                    nc.scalar.activation(m2[:, m, :], m2[:, m, :], ACT.Sqrt).then_inc(s.root, 1)

            @block.vector
            def _(dve):
                step = Chain(dve, s.dve)
                nc.vector.memset(bd, 0.0).then_inc(s.zero, 1)
                lam = col(S, "lru_lambda_2", 0, 4)
                step(nc.vector.tensor_scalar(ww, lam, -1.0, None, ALU.mult))
                nc.vector.tensor_tensor(e, ww, lam, ALU.min).then_inc(s.act, 1)
                dve.wait_ge(s.exped, 2)
                log1p_tail(step, nc, e, ln, ww, ww)
                step(nc.vector.tensor_scalar(cl, lam, -1.0, 0.0, ALU.mult, ALU.max))
                step(nc.vector.tensor_tensor(cl, cl, ww, ALU.add))
                nc.vector.tensor_scalar(cl, cl, LRU_C, None, ALU.mult).then_inc(s.rate, 1)
                dve.wait_ge(s.th, 4)
                nc.vector.tensor_scalar(cl, cl, -1.0, None, ALU.mult).then_inc(s.act, 1)
                dve.wait_ge(s.gates, 16)
                for m in range(4):
                    k = nc.vector.tensor_tensor(g[:, m, :], g[:, m, :], xc[:, m, :], ALU.mult)
                step(k)
                for m in range(4):
                    dve.wait_ge(s.a, m + 1)
                    step(nc.vector.tensor_tensor(xc[:, m, :], r[:, m, :], r[:, m, :], ALU.mult))
                    nc.vector.scalar_tensor_tensor(out=m2[:, m, :], in0=xc[:, m, :], scalar=1.0, in1=m2[:, m, :],
                                                   op0=ALU.add, op1=ALU.mult).then_inc(s.sq, 1)
                for m in range(4):
                    dve.wait_ge(s.root, m + 1)
                    step(nc.vector.memset(m2[:, m, 0:1], 1.0))
                    step(nc.vector.tensor_tensor(g[:, m, :], g[:, m, :], m2[:, m, :], ALU.mult))
                    step(nc.vector.tensor_tensor_scan(m2[:, m, :], r[:, m, :], g[:, m, :], 0.0, ALU.mult, ALU.add))
                    nc.vector.tensor_tensor(mix[:, m, :], m2[:, m, :], z[:, m, :], ALU.mult)


ZS0 = Z0
XT0 = ZS0 + NT * SSD_W
BT0 = XT0 + NT * SSD_W
FE0 = BT0 + NT * SSD_G * SSD_N
XC0 = FE0 + 192
assert XC0 + 12 * T <= SIZE


def stage_keep_dt(nc, I, S):
    A = S.arena
    src, dst = A.view(FD0, 192), A.view(FE0, 192)
    assert FE0 >= FD0 + 192
    with ExitStack() as ctx:
        s = semaphores(nc, ctx, "kd", "moved")
        with nc.Block() as block:
            @block.vector
            def _(dve):
                nc.vector.tensor_copy(dst, src).then_inc(s.moved, 1)


def stage_project_ssd(nc, I, S):
    A = S.arena
    w = I["w_in_2"].rearrange("l (k p) n -> p (l k) n", p=P)
    xc = A.view(XC0, 12, T)
    bat, _ = COL["ssd_conv_b_2"]
    dense_conv(nc, S, "sc", lambda m: w[:, :, bass.ds(m * P + XBC_OFF, P)], 12, taps_of(S, "ssd_conv_w_2", 12),
               lambda m: S.cols[:, bass.ds(m + bat, 1)], xc, ZS0, ZS0 + 4 * KT * P)
    zs = A.view(ZS0, NT, SSD_W)
    for q in range(2):
        project_tokens(nc, S, f"sz{q}", w, [(ZS_OFF + q * HALF, HALF)], XT0,
                       lambda act, bank, i, _, q=q: act.activation(zs[:, i, q * HALF:(q + 1) * HALF], bank, ACT.Silu))
    xt = A.view(XT0, NT, SSD_W)
    bt = A.view(BT0, NT, SSD_G * SSD_N)
    with ExitStack() as ctx:
        s = semaphores(nc, ctx, "st", "silu turned free")
        ps = psum(nc, ctx, "st_ps", 4, PSB)
        jobs = [(m, h) for m in range(10) for h in range(2)]
        with nc.Block() as block:
            @block.scalar
            def _(act):
                for m in range(12):
                    nc.scalar.activation(xc[:, m, :], xc[:, m, :], ACT.Silu).then_inc(s.silu, 1)

            @block.tensor
            def _(pe):
                for n, (m, h) in enumerate(jobs):
                    pe.wait_ge(s.silu, m + 1)
                    if n >= 4:
                        pe.wait_ge(s.free, n - 3)
                    for i in range(4):
                        t = pe.transpose(ps[:, n % 4, i * P:(i + 1) * P],
                                         xc[:, m, (4 * h + i) * P:(4 * h + i + 1) * P], S.ident)
                    t.then_inc(s.turned, 1)

            @block.vector
            def _(dve):
                for n, (m, h) in enumerate(jobs):
                    dve.wait_ge(s.turned, n + 1)
                    dst = xt[:, 4 * h:4 * h + 4, m * P:(m + 1) * P] if m < 8 else \
                        bt[:, 4 * h:4 * h + 4, (m - 8) * P:(m - 7) * P]
                    nc.vector.tensor_copy(dst, ps[:, n % 4, :].rearrange("p (i n) -> p i n", i=4)).then_inc(s.free, 1)


def stage_ssd(nc, I, S):
    A = S.arena
    NC, HG = T // SSD_C, SSD_H // SSD_G
    zs = A.view(ZS0, NT, SSD_W)
    xt = A.view(XT0, NT, SSD_W)
    bt = A.view(BT0, NT, SSD_G * SSD_N)
    xc = A.view(XC0, 12, T)
    f = A.view(FE0, NT, ATT_H + SSD_H)[:, :, ATT_H:]
    at = XC0
    R = A.view(at, SSD_H, P)
    E = A.view(at + 2048, SSD_H, P)
    gm = A.view(at + 4096, SSD_G, P)
    xdt = A.view(at + 4352, SSD_W)
    xds = A.view(at + 5376, SSD_W)
    st = A.view(at + 6400, SSD_W)
    yy = A.view(C0, SSD_W)
    y2 = A.view(C0 + 1024, SSD_W)
    sm = at + 7424
    dtb, alog, dsk = (A.view(sm + 16 * i, SSD_H) for i in range(3))
    e, ln, ww, dt, adt = (A.view(sm + 48 + i * 128, NC, SSD_H) for i in range(5))
    assert sm + 48 + 640 <= at + 8 * T
    ex = [A.view(M_SMALL + 128 * i, NC, SSD_H) for i in range(2)]
    ex.append(A.view(M_IDENT + 7 * 128, NC, SSD_H))
    ea, ds, et = ex
    ms = A.view(M_SMALL + 256, 2)
    mix = S.hT
    with ExitStack() as ctx:
        s = semaphores(nc, ctx, "ss", "in_ act exped dve adt sums ea R G gm seg E M xdt xds Y off st_mm st upd y_ok sq ms root"
                                      " gated turned out n")
        pa = psum(nc, ctx, "ss_a", 4, PSB)
        pd = psum(nc, ctx, "ss_d", 2, PSB)
        po = psum(nc, ctx, "ss_o", 2, PSB)
        with nc.Block() as block:
            @block.sync
            def _(sp):
                for dst, name in ((dtb, "ssd_dt_bias_2"), (alog, "ssd_a_log_2"), (dsk, "ssd_d_2")):
                    sp.dma_start(dst, I[name].broadcast_to([P, SSD_H])).then_inc(s.in_, 16)

            @block.scalar
            def _(act):
                act.wait_ge(s.act, 1)
                nc.scalar.activation(e, e, ACT.Exp).then_inc(s.exped, 1)
                act.wait_ge(s.exped, 1)
                nc.scalar.activation(ln, e, ACT.Ln, bias=1.0).then_inc(s.exped, 1)
                act.wait_ge(s.in_, 48)
                nc.scalar.activation(alog, alog, ACT.Exp).then_inc(s.exped, 1)
                act.wait_ge(s.sums, 1)
                for n in range(3):
                    nc.scalar.activation(ex[n], pa[:, n, 0:128].rearrange("p (c h) -> p c h", h=SSD_H), ACT.Exp)\
                        .then_inc(s.ea, 1)
                for c in range(NC):
                    for q in range(4):
                        act.wait_ge(s.seg, 4 * c + q + 1)
                        if c:
                            act.wait_ge(s.Y, c)
                        nc.scalar.activation(E[:, 4 * q:4 * q + 4, :],
                                             pa[:, q, :].rearrange("p (h l) -> p h l", l=P), ACT.Exp)\
                            .then_inc(s.E, 1)
                    act.wait_ge(s.y_ok, c + 1)
                    for g in range(2):
                        nc.scalar.activation(y2[:, g * HALF:(g + 1) * HALF], yy[:, g * HALF:(g + 1) * HALF],
                                             ACT.Square, accum_out=ms[:, g:g + 1]).then_inc(s.sq, 1)
                    act.wait_ge(s.ms, c + 1)
                    nc.scalar.activation(ms, ms, ACT.Sqrt).then_inc(s.root, 1)

            @block.gpsimd
            def _(pool):
                pool.wait_ge(s.adt, 1)
                pool.wait_ge(s.ea, 3)
                for c in range(NC):
                    if c:
                        pool.wait_ge(s.seg, 4 * c)
                    pool.tensor_tensor(R, S.t_le.unsqueeze(1).broadcast_to([P, SSD_H, P]),
                                       adt[:, c, :].unsqueeze(2).broadcast_to([P, SSD_H, P]), ALU.mult)\
                        .then_inc(s.R, 1)
                    if c:
                        pool.wait_ge(s.st_mm, c)
                    pool.tensor_tensor(xdt.rearrange("p (h d) -> p h d", d=SSD_P),
                                       xt[:, c, :].rearrange("p (h d) -> p h d", d=SSD_P),
                                       dt[:, c, :].unsqueeze(2).broadcast_to([P, SSD_H, SSD_P]), ALU.mult)\
                        .then_inc(s.xdt, 1)
                    pool.wait_ge(s.xdt, c + 1)
                    pool.tensor_tensor(xds.rearrange("p (h d) -> p h d", d=SSD_P),
                                       xdt.rearrange("p (h d) -> p h d", d=SSD_P),
                                       ds[:, c, :].unsqueeze(2).broadcast_to([P, SSD_H, SSD_P]), ALU.mult)\
                        .then_inc(s.xds, 1)

            @block.tensor
            def _(pe):
                pe.wait_ge(s.adt, 1)
                for n, m in enumerate((S.t_le, S.t_gt, S.ones)):
                    mm = pe.matmul(pa[:, n, 0:128], m, adt.rearrange("p c h -> p (c h)"), start=True, stop=True)
                mm.then_inc(s.sums, 1)
                pe.wait_ge(s.ea, 3)
                for c in range(NC):
                    tok = slice(c * P, (c + 1) * P)
                    if c:
                        pe.wait_ge(s.upd, c)
                    for g in range(SSD_G):
                        mm = pe.matmul(po[:, 0, g * P:(g + 1) * P], xc[:, 8 + g, tok], xc[:, 10 + g, tok],
                                       start=True, stop=True)
                    mm.then_inc(s.G, 1)
                    pe.wait_ge(s.R, c + 1)
                    if c:
                        pe.wait_ge(s.out, c)
                    for q in range(4):
                        pe.matmul(pa[:, q, :], S.t_gt, R[:, 4 * q:4 * q + 4, :].rearrange("p h l -> p (h l)"),
                                  start=True, stop=True).then_inc(s.seg, 1)
                    pe.wait_ge(s.gm, c + 1)
                    if c:
                        for g in range(SSD_G):
                            mm = pe.matmul(po[:, g, :], xc[:, 10 + g, tok], st[:, g * HALF:(g + 1) * HALF],
                                           start=True, stop=True)
                        mm.then_inc(s.off, 1)
                    pe.wait_ge(s.M, c + 1)
                    pe.wait_ge(s.xdt, c + 1)
                    for h in range(SSD_H):
                        o = pd[:, h // HG, (h % HG) * SSD_P:(h % HG + 1) * SSD_P]
                        mm = pe.matmul(o, E[:, h, :], xdt[:, h * SSD_P:(h + 1) * SSD_P], start=True, stop=True)
                    mm.then_inc(s.Y, 1)
                    pe.wait_ge(s.xds, c + 1)
                    pe.wait_ge(s.n, c + 1)
                    for g in range(SSD_G):
                        mm = pe.matmul(po[:, g, :], bt[:, c, g * P:(g + 1) * P], xds[:, g * HALF:(g + 1) * HALF],
                                       start=True, stop=True)
                    mm.then_inc(s.st_mm, 1)
                    pe.wait_ge(s.gated, c + 1)
                    for k in range(8):
                        t = pe.transpose(pa[:, k // 4, (k % 4) * P:(k % 4 + 1) * P], yy[:, k * P:(k + 1) * P],
                                         S.ident)
                    t.then_inc(s.turned, 1)

            @block.vector
            def _(dve):
                step = Chain(dve, s.dve)
                dve.wait_ge(s.in_, 48)
                step(nc.vector.tensor_tensor(dt, f, dtb.unsqueeze(1).broadcast_to([P, NC, SSD_H]), ALU.add))
                step(nc.vector.tensor_scalar(ww, dt, -1.0, None, ALU.mult))
                nc.vector.tensor_tensor(e, ww, dt, ALU.min).then_inc(s.act, 1)
                dve.wait_ge(s.exped, 3)
                log1p_tail(step, nc, e, ln, ww, ww)
                step(nc.vector.tensor_scalar(dt, dt, 0.0, None, ALU.max))
                step(nc.vector.tensor_tensor(dt, dt, ww, ALU.add))
                step(nc.vector.tensor_scalar(alog, alog, -1.0, None, ALU.mult))
                nc.vector.tensor_tensor(adt, dt, alog.unsqueeze(1).broadcast_to([P, NC, SSD_H]), ALU.mult)\
                    .then_inc(s.adt, 1)
                bh = lambda v: v.unsqueeze(2).broadcast_to([P, SSD_H, SSD_P])
                hd = lambda v: v.rearrange("p (h d) -> p h d", d=SSD_P)
                for c in range(NC):
                    dve.wait_ge(s.G, c + 1)
                    nc.vector.tensor_tensor(gm, po[:, 0, 0:2 * P].rearrange("p (g l) -> p g l", l=P),
                                            S.t_le.unsqueeze(1).broadcast_to([P, SSD_G, P]), ALU.mult)\
                        .then_inc(s.gm, 1)
                    dve.wait_ge(s.gm, c + 1)
                    for g in range(SSD_G):
                        dve.wait_ge(s.E, 4 * c + 2 * g + 2)
                        k = nc.vector.tensor_tensor(E[:, g * HG:(g + 1) * HG, :], E[:, g * HG:(g + 1) * HG, :],
                                                    gm[:, g, :].unsqueeze(1).broadcast_to([P, HG, P]), ALU.mult)
                    k.then_inc(s.M, 1)
                    if c:
                        dve.wait_ge(s.turned, c)
                    step(nc.vector.tensor_tensor(hd(yy), hd(xt[:, c, :]), bh(dsk), ALU.mult))
                    if c:
                        dve.wait_ge(s.off, c)
                        dve.wait_ge(s.ms, c)
                        step(nc.vector.tensor_tensor(hd(y2), hd(po[:, :, :].rearrange("p a b -> p (a b)")),
                                                     bh(ea[:, c, :]), ALU.mult))
                        nc.vector.memset(ww[:, 0, 0:1], 0.0).then_inc(s.n, 1)
                        step(nc.vector.tensor_tensor(yy, yy, y2, ALU.add))
                    else:
                        nc.vector.memset(ww[:, 0, 0:1], 0.0).then_inc(s.n, 1)
                    dve.wait_ge(s.Y, c + 1)
                    step(nc.vector.tensor_tensor(yy, yy, pd[:, :, :].rearrange("p a b -> p (a b)"), ALU.add))
                    nc.vector.tensor_tensor(yy, yy, zs[:, c, :], ALU.mult).then_inc(s.y_ok, 1)
                    dve.wait_ge(s.st_mm, c + 1)
                    if c:
                        step(nc.vector.tensor_tensor(hd(st), hd(st), bh(et[:, c, :]), ALU.mult))
                        k = nc.vector.tensor_tensor(st, st, po[:, :, :].rearrange("p a b -> p (a b)"), ALU.add)
                    else:
                        k = nc.vector.tensor_copy(st, po[:, :, :].rearrange("p a b -> p (a b)"))
                    k.then_inc(s.upd, 1)
                    dve.wait_ge(s.sq, 2 * c + 2)
                    nc.vector.tensor_scalar(ms, ms, 1.0 / HALF, EPS, ALU.mult, ALU.add).then_inc(s.ms, 1)
                    dve.wait_ge(s.root, c + 1)
                    step(nc.vector.reciprocal(ms, ms))
                    for g in range(2):
                        k = nc.vector.tensor_scalar(yy[:, g * HALF:(g + 1) * HALF], yy[:, g * HALF:(g + 1) * HALF],
                                                    ms[:, g:g + 1], None, ALU.mult)
                    k.then_inc(s.gated, 1)
                    dve.wait_ge(s.turned, c + 1)
                    gn, _ = COL["ssd_norm_g_2"]
                    nc.vector.tensor_tensor(mix[:, :, c * P:(c + 1) * P],
                                            pa[:, 0:2, :].rearrange("p a (k t) -> p (a k) t", t=P),
                                            S.cols[:, gn:gn + 8].unsqueeze(2).broadcast_to([P, 8, P]), ALU.mult)\
                        .then_inc(s.out, 1)


def stage_out(nc, I, S):
    A = S.arena
    w = I["w_out_2"].rearrange("l (k p) n -> p (l k) n", p=P)
    wv = [A.view(Z0 + q * MT * HALF, MT, HALF) for q in range(2)]
    x2 = A.view(Z0 + MT * D, KT, T)
    ot = A.view(C0, 4, HALF)
    att, lru = A.view(MA0, 4, T), A.view(ML0, 4, T)
    def mix(k):
        return att[:, k, :] if k < 4 else S.hT[:, k - 4, :] if k < 12 else lru[:, k - 12, :]
    with ExitStack() as ctx:
        s = semaphores(nc, ctx, "fo", "x w0 w1 done copied o0 o1 o2 o3")
        sent = [s.o0, s.o1, s.o2, s.o3]
        ps = psum(nc, ctx, "fo_ps", 8, PSB)
        jobs = [(q, i) for q in range(2) for i in range(NT)]
        with nc.Block() as block:
            @block.sync
            def _(sp):
                for q in range(2):
                    sp.dma_start(wv[q], w[:, :, q * HALF:(q + 1) * HALF]).then_inc((s.w0, s.w1)[q], 16)
                    if q == 0:
                        sp.dma_start(x2, S.kept[1].rearrange("p (k t) -> p k t", t=T)).then_inc(s.x, 16)
                for n, (q, i) in enumerate(jobs):
                    sp.wait_ge(s.copied, n + 1)
                    sp.dma_start(S.out[0, i * P:(i + 1) * P, q * HALF:(q + 1) * HALF], ot[:, n % 4, :])\
                        .then_inc(sent[n % 4], 16)
                for n in range(4):
                    sp.wait_ge(sent[n], 16 * len(jobs) // 4)

            @block.tensor
            def _(pe):
                for n, (q, i) in enumerate(jobs):
                    pe.wait_ge((s.w0, s.w1)[q], 16)
                    pe.wait_ge(s.x, 16)
                    if n >= 8:
                        pe.wait_ge(s.copied, n - 7)
                    tok = slice(i * P, (i + 1) * P)
                    for k in range(MT):
                        mm = pe.matmul(ps[:, n % 8, :], mix(k)[:, tok], wv[q][:, k, :], start=(k == 0),
                                       stop=(k == MT - 1))
                        if k == 0:
                            for f in range(4):
                                pe.matmul(ps[:, n % 8, f * P:(f + 1) * P], x2[:, 4 * q + f, tok], S.ident,
                                          start=False, stop=False, skip_group_check=True)
                    mm.then_inc(s.done, 1)

            @block.scalar
            def _(act):
                for n, (q, i) in enumerate(jobs):
                    act.wait_ge(s.done, n + 1)
                    if n >= 4:
                        act.wait_ge(sent[n % 4], 16 * (n // 4))
                    nc.scalar.activation(ot[:, n % 4, :], ps[:, n % 8, :], ACT.Copy).then_inc(s.copied, 1)


def build(nc, I, out, upto=99, dumps=()):
    used_semaphores[0] = 0
    with ExitStack() as ctx:
        S = Views()
        arena = ctx.enter_context(nc.sbuf_tensor("arena", [P, SIZE], F32))
        A = S.arena = Arena(arena, SIZE)
        S.ident, S.ones, S.mean, S.t_le, S.t_ge, S.t_lt, S.t_gt, S.blk = (
            A.view(m, P) for m in (M_IDENT, M_ONES, M_MEAN, M_TLE, M_TGE, M_TLT, M_TGT, M_BLK))
        S.cols = A.view(M_COLS, N_COLS)
        S.mod = A.view(M_MOD, 48, 2)
        S.cs = A.view(M_CS, KT, 2)
        S.sc1 = A.view(M_SC1, KT, 2)
        S.sc2 = A.view(M_SC2, KT)
        S.small = A.view(M_SMALL, 300)
        S.x_w, S.x_b, S.h_w, S.h_b = (A.view(M_WX + 8 * i, KT) for i in range(4))
        S.xT = A.view(X0, KT, T)
        S.hT = A.view(H0, KT, T)
        S.ctxT = A.view(C0, KT, TC)
        S.yT = S.hT
        S.z = A.view(Z0, Z_TILES, T)
        S.kc = A.view(KC0, 2, TC)
        S.vt = A.view(VT0, (NT + NTC) * HEADS, HD + 1)
        S.gates = A.view(GT0, NT + NTC, 16)
        S.sv = A.view(SV0, NT, W_MIX)
        S.u5 = A.view(U50, S5G, S5L, S5P)
        S.u5c = A.view(U5C0, S5G, S5L, S5P)
        S.a = A.view(M_SMALL, NT + NTC, 8)
        S.expn = A.view(M_SMALL + 80, NT, 8)
        S.M = [A.view(H0 + d * T, T)[0:8, :] for d in range(2)]
        S.htok = A.view(Z0 + 10 * T, NT * HEADS, HD).rearrange("p (i h) d -> p i h d", h=HEADS)
        S.htmp = A.view(C0, 8, HD).rearrange("p (c j) d -> p c j d", c=2)
        S.hid = A.view(Z0, FT, T)
        S.crow = A.view(C0, T)[0:ATT_H, :]
        S.out = out
        S.kept = [nc.dram_tensor(f"kept_{i}", (P, TILE8), F32, kind="Internal").ap() for i in range(2)]
        for n, stage in enumerate(STAGES):
            if n < upto:
                stage(nc, I, S)
        for i, (d, at, n) in enumerate(dumps):
            with nc.semaphore(f"dump{i}") as sd, nc.Block() as block:
                @block.sync
                def _(sp):
                    sp.dma_start(d, A.view(at, n)).then_inc(sd, 16)
                    sp.wait_ge(sd, 16)


STAGES = [stage_constants, stage_keep_x, stage_project_1, stage_project_tokens_1, stage_conv, stage_sgu,
          stage_s5_params, stage_s5, stage_s5_glu, stage_mlstm_gates, stage_mlstm, stage_mlstm_out,
          stage_back_x, stage_w_out_1, stage_ffn_in, stage_ffn_out,
          stage_keep_x2, stage_rms, stage_project_att, stage_project_att_tokens, stage_att_norm, stage_attention,
          stage_lru, stage_keep_dt, stage_project_ssd, stage_ssd, stage_out]


_OUT = (1, T, D)


def kernel(**inputs):
    import numpy as _np
    import concourse.bacc as _bacc
    from concourse.bass_utils import run_bass_kernel_spmd as _run

    nc = _bacc.Bacc("TRN2", target_bir_lowering=False, num_devices=1)
    arrays, args = {}, {}
    for name, a in inputs.items():
        a = _np.ascontiguousarray(a)
        arrays[f"in_{name}"] = a
        args[name] = nc.dram_tensor(f"in_{name}", a.shape, F32, kind="ExternalInput").ap()
    out = nc.dram_tensor("out_0", _OUT, F32, kind="ExternalOutput").ap()
    build(nc, args, out)
    return _run(nc, [arrays], core_ids=[0]).results[0]["out_0"]
```

```python
import math
from contextlib import ExitStack, contextmanager

import concourse.bass as bass
from concourse import mybir

P = 128
F32 = mybir.dt.float32
ALU = mybir.AluOpType
ACT = mybir.ActivationFunctionType
AX = mybir.AxisListType.X
PSB = 512

D = 1024
KT = D // P
T = 1024
NT = T // P
HALF = 512
TC = 256
NTC = TC // P

W_MIX = D // 4
HEADS, HD = 4, 64
O_Q, O_K, O_V, O_O, O_G = 0, W_MIX, 2 * W_MIX, 3 * W_MIX, 4 * W_MIX
O_B = O_G + 4 * HEADS
O_C = O_B + 2 * W_MIX
O_D = O_C + 2 * W_MIX
P_IN = O_D + W_MIX
CONV_W, CONV_PAD, GRID = 31, 15, 64
ROWS = T // GRID
S5G, S5P, S5N = 16, 16, 64
S5L = 8
S5C = T // S5L
S5CC = TC // S5L
D_FF = -(-8 * D // (3 * 256)) * 256
FT = D_FF // P
ALPHA = 2.0 ** 0.25
LN_EPS = 1e-5
EPS = 1e-6

ATT_W, ATT_H, ATT_HD = 512, 8, 64
SSD_W, SSD_H, SSD_P, SSD_G, SSD_N, SSD_C = 1024, 16, 64, 2, 128, 128
SSD_CONV = SSD_W + 2 * SSD_G * SSD_N
LRU_W, LRU_B, LRU_BD, LRU_C = 512, 8, 64, 8.0
TAPS = 4
Q_OFF, K_OFF, V_OFF, ZA_OFF = 0, ATT_W, 2 * ATT_W, 3 * ATT_W
F_OFF = 4 * ATT_W
ZS_OFF = F_OFF + ATT_H
XBC_OFF = ZS_OFF + SSD_W
DT_OFF = XBC_OFF + SSD_CONV
XL_OFF = DT_OFF + SSD_H
ZL_OFF = XL_OFF + LRU_W
D_IN = ZL_OFF + LRU_W
MIX_W = 2 * D
MT = MIX_W // P


class Views:
    pass


class Named:

    def __init__(self, by_name):
        self.by_name = by_name

    def __getattr__(self, name):
        return self.by_name[name]


class Arena:

    def __init__(self, tensor, size):
        self.t, self.size, self.work = tensor, size, None

    def view(self, at, *shape, parts=P):
        n = math.prod(shape)
        assert at + n <= self.size, (at, shape)
        if at < X0:
            assert at + n <= X0
            v = self.t[0:parts, at:at + n]
        else:
            v = self.work[0:parts, at - X0:at - X0 + n]
        if len(shape) == 2:
            v = v.rearrange("p (a b) -> p a b", b=shape[1])
        elif len(shape) == 3:
            v = v.rearrange("p (a b c) -> p a b c", b=shape[1], c=shape[2])
        return v


PACKS = [
    [("b_mod", 48), ("ln1_w", 8), ("ln1_b", 8), ("ln2_w", 8), ("ln2_b", 8), ("norm_g_2", 8),
     ("mlstm_norm_w", 2), ("conv_b", 2), ("conv_ln_w", 2), ("conv_ln_b", 2), ("s5_glu_b", 2)],
    [("ssd_conv_w_2", 48), ("ssd_conv_b_2", 12), ("ssd_norm_g_2", 8), ("lru_conv_w_2", 16),
     ("lru_conv_b_2", 4), ("lru_b_a_2", 4), ("lru_b_x_2", 4), ("lru_lambda_2", 4)],
    [("conv_w", 62), ("c", 8), ("c_ctx", 8), ("q_norm_g_2", 1), ("k_norm_g_2", 1)],
]
COL = {}
_at = 0
for _p in PACKS:
    for _name, _n in _p:
        COL[_name] = (_at, _n)
        _at += _n
N_COLS = _at

SIZE = 52800
M_IDENT, M_ONES, M_MEAN, M_TLE, M_TGE, M_TLT, M_TGT, M_BLK = (128 * i for i in range(8))
M_COLS = 1024
M_MOD = M_COLS + N_COLS
M_CS = M_MOD + 96
M_SC1 = M_CS + 16
M_SC2 = M_SC1 + 16
M_WX = M_SC2 + 8
M_SMALL = M_WX + 32
BASE = 2048
assert M_SMALL + 300 < BASE
TILE8 = KT * T
H0 = BASE
X0 = H0 + TILE8
C0 = X0 + TILE8
Z0 = C0 + KT * TC
Z_TILES = 12
KC0 = Z0 + Z_TILES * T
VT0 = KC0 + 2 * TC
VC0 = VT0 + NT * HEADS * (HD + 1)
GT0 = VC0 + NTC * HEADS * (HD + 1)
SV0 = GT0 + (NT + NTC) * 16
U50 = SV0 + NT * W_MIX
U5C0 = U50 + 2048
WR0 = U5C0 + 2048
assert WR0 + 10368 <= SIZE, WR0


N_SEMAPHORES = 150
used_semaphores = [0]


def clear_if_used_up(nc, n):
    if used_semaphores[0] + n > N_SEMAPHORES:
        free = sorted(nc.released_uncleared_semaphores)
        with nc.Block() as block:
            @block.gpsimd
            def _(pool):
                first = free[0]
                for a, b in zip(free, free[1:] + [None]):
                    if b != a + 1:
                        pool.sem_clear(range(first, a + 1))
                        first = b
        used_semaphores[0] = 0


def semaphores(nc, S, ctx, prefix, names):
    n = len(names.split())
    if S.group is None:
        clear_if_used_up(nc, n)
    used_semaphores[0] += n
    return Named({n: ctx.enter_context(nc.semaphore(f"{prefix}_{n}")) for n in names.split()})


@contextmanager
def memory(S):
    if S.group is None:
        with ExitStack() as ctx:
            yield ctx
    else:
        yield S.group[0]


@contextmanager
def block_of(nc, S):
    if S.group is None:
        with nc.Block() as block:
            yield block
    else:
        yield S.group[1]


def beside(n_semaphores, *stages):
    def run(nc, I, S):
        with ExitStack() as ctx:
            clear_if_used_up(nc, n_semaphores)
            with nc.Block() as block:
                S.group = (ctx, block)
                before = used_semaphores[0]
                for stage in stages:
                    stage(nc, I, S)
                assert used_semaphores[0] - before <= n_semaphores
                S.group = None
    return run


def psum(nc, ctx, name, *shape):
    return ctx.enter_context(nc.psum_tensor(name, [P, *shape], F32))


def col(S, name, i=0, n=1, parts=slice(0, P)):
    at, _ = COL[name]
    return S.cols[parts, at + i:at + i + n]


MOD_N = 6 * D // HALF
MOD_H = 2 * D // HALF


class Modulation:

    def __init__(self, nc, S, ctx, name, first, last, ring, rows):
        self.nc, self.S, self.chunks, self.ring, self.rows = nc, S, list(range(first, last)), ring, rows
        self.n = len(self.chunks)
        slots = " ".join(f"w{i}" for i in range(len(ring)))
        self.s = semaphores(nc, S, ctx, name, slots + " done rowc turned")
        self.loaded = [self.s.by_name[f"w{i}"] for i in range(len(ring))]
        self.ps = psum(nc, ctx, f"{name}_ps", 2, PSB)
        self.turns = psum(nc, ctx, f"{name}_t", PSB)

    def load(self, engine, w, n):
        r = len(self.ring)
        if n >= r:
            engine.wait_ge(self.s.done, n - r + 1)
        m = self.chunks[n]
        engine.dma_start(self.ring[n % r], w[:, :, m * HALF:(m + 1) * HALF]).then_inc(self.loaded[n % r], 16)

    def products(self, pe):
        r, s = len(self.ring), self.s

        def turn(n):
            pe.wait_ge(s.rowc, n + 1)
            for j in range(4):
                at = 2 * (4 * n + j)
                t = pe.transpose(self.turns[:, at:at + 2], self.rows[n % 2][:, j * P:(j + 1) * P],
                                 self.S.ident[0:2, 0:2])
            t.then_inc(s.turned, 1)

        for n in range(self.n):
            pe.wait_ge(self.loaded[n % r], 16 * (n // r + 1))
            if n >= 2:
                pe.wait_ge(s.rowc, n - 1)
            for k in range(KT):
                mm = pe.matmul(self.ps[0:2, n % 2, :], self.S.cs[:, k, :], self.ring[n % r][:, k, :],
                               start=(k == 0), stop=(k == KT - 1))
            mm.then_inc(s.done, 1)
            if n:
                turn(n - 1)
        turn(self.n - 1)

    def finish(self, dve):
        s = self.s
        for n in range(self.n):
            dve.wait_ge(s.done, n + 1)
            if n >= 2:
                dve.wait_ge(s.turned, n - 1)
            self.nc.vector.tensor_copy(self.rows[n % 2], self.ps[0:2, n % 2, :]).then_inc(s.rowc, 1)
        dve.wait_ge(s.turned, self.n)
        at, _ = COL["b_mod"]
        a, m = 4 * self.chunks[0], 4 * self.n
        return self.nc.vector.tensor_tensor(
            self.S.mod[:, a:a + m, :], self.turns[:, 0:2 * m].rearrange("p (a b) -> p a b", b=2),
            self.S.cols[:, at + a:at + a + m].unsqueeze(2).broadcast_to([P, m, 2]), ALU.add)


def stage_constants(nc, I, S):
    with memory(S) as ctx:
        s = semaphores(nc, S, ctx, "c", "memset masks rows xin cin turned h_out x_out cols silu dve")
        A = S.arena
        xtok = A.view(Z0, NT, D)
        ctok = A.view(Z0 + NT * D, NTC, D)
        rows = A.view(Z0 + 10 * D, 3, P)
        ring = [A.view(Z0 + 11 * D + i * KT * HALF, KT, HALF) for i in range(4)]
        mod_rows = [A.view(Z0 + 28 * D + i * HALF, HALF)[0:2, :] for i in range(2)]
        md = Modulation(nc, S, ctx, "ca", 0, MOD_H, ring, mod_rows)
        B = 4
        ps = psum(nc, ctx, "c_turn", B, PSB)
        w_mod = I["w_mod"].rearrange("l (k p) n -> p (l k) n", p=P)
        turns = [(k, src, n0, n) for k in range(KT) for src, n0, n in ((xtok, 0, 4), (xtok, 4, 4), (ctok, 0, 2))]

        with block_of(nc, S) as block:
            @block.sync
            def _(sp):
                n = 0
                for p, pack in enumerate(PACKS):
                    at = 0
                    for name, k in pack:
                        a = I[name]
                        if name in ("q_norm_g_2", "k_norm_g_2"):
                            for half in range(2):
                                sp.dma_start(rows[at:at + 1, p, half * 64:half * 64 + 64], a).then_inc(s.rows, 16)
                                n += 1
                        else:
                            flat = {1: "a -> a", 2: "a b -> (a b)", 3: "a b c -> (a b c)"}[len(a.shape)]
                            v = (a.rearrange(flat) if len(a.shape) > 1 else a).rearrange("(r q) -> r q", q=P)
                            sp.dma_start(rows[at:at + k, p, :], v).then_inc(s.rows, 16)
                            n += 1
                        at += k
                S.n_rows = n
                sp.dma_start(xtok, I["x"].rearrange("b (i p) d -> p (b i) d", p=P)).then_inc(s.xin, 16)
                sp.dma_start(ctok, I["ctx"].rearrange("b (i p) d -> p (b i) d", p=P)).then_inc(s.cin, 16)

            @block.scalar
            def _(act):
                for n in range(md.n):
                    md.load(act, w_mod, n)
                act.wait_ge(s.cols, 3)
                nc.scalar.activation(S.cs[:, :, 0], col(S, "c", 0, 8), ACT.Silu).then_inc(s.silu, 1)
                nc.scalar.activation(S.cs[:, :, 1], col(S, "c_ctx", 0, 8), ACT.Silu).then_inc(s.silu, 1)
                for b, (k, src, n0, n) in enumerate(turns):
                    if src is xtok:
                        act.wait_ge(s.turned, 3 + b + 1)
                        nc.scalar.activation(S.xT[:, k, n0 * P:(n0 + n) * P], ps[:, (3 + b) % B, 0:n * P], ACT.Copy,
                                             scale=ALPHA).then_inc(s.x_out, 1)

            @block.gpsimd
            def _(pool):
                pool.memset(S.ident, 0.0).then_inc(s.memset, 1)
                for m in (S.ones, S.t_le, S.t_ge, S.t_lt, S.t_gt):
                    pool.memset(m, 1.0).then_inc(s.memset, 1)
                pool.memset(S.mean, 1.0 / D).then_inc(s.memset, 1)
                pool.wait_ge(s.memset, 7)
                pool.affine_select(out=S.ident, in_=S.ident, compare_op=ALU.not_equal, fill=1.0, base=0,
                                   pattern=[[-1, P]], channel_multiplier=1).then_inc(s.masks, 1)
                for m, sign, op in ((S.t_le, 1, ALU.is_ge), (S.t_ge, -1, ALU.is_ge),
                                    (S.t_lt, 1, ALU.is_gt), (S.t_gt, -1, ALU.is_gt)):
                    pool.affine_select(out=m, in_=m, compare_op=op, fill=0.0, base=0, pattern=[[sign, P]],
                                       channel_multiplier=-sign).then_inc(s.masks, 1)

            @block.tensor
            def _(pe):
                pe.wait_ge(s.masks, 5)
                pe.wait_ge(s.rows, 16 * S.n_rows)
                for p, pack in enumerate(PACKS):
                    k = sum(n for _, n in pack)
                    pe.transpose(ps[:, p, 0:k], rows[0:k, p, :], S.ident[0:k, 0:k]).then_inc(s.turned, 1)
                pe.wait_ge(s.silu, 2)
                md.products(pe)
                pe.wait_ge(s.xin, 16)
                pe.wait_ge(s.cin, 16)
                for b, (k, src, n0, n) in enumerate(turns):
                    old = b - B
                    if old >= 0:
                        pe.wait_ge(s.h_out, old + 1)
                    for i in range(n):
                        t = pe.transpose(ps[:, (3 + b) % B, i * P:(i + 1) * P],
                                         src[:, n0 + i, k * P:(k + 1) * P], S.ident)
                    t.then_inc(s.turned, 1)

            @block.vector
            def _(dve):
                nc.vector.memset(S.blk, 0.0).then_inc(s.dve, 1)
                dve.wait_ge(s.dve, 1)
                for half in (slice(0, 64), slice(64, 128)):
                    nc.vector.memset(S.blk[half, half], 1.0 / 64)
                at = 0
                for p, pack in enumerate(PACKS):
                    k = sum(n for _, n in pack)
                    dve.wait_ge(s.turned, p + 1)
                    nc.vector.tensor_copy(S.cols[:, at:at + k], ps[:, p, 0:k]).then_inc(s.cols, 1)
                    at += k
                dve.wait_ge(s.cols, 3)
                md.finish(dve).then_inc(s.dve, 1)
                dve.wait_ge(s.dve, 2)
                nc.vector.tensor_scalar(S.sc1, S.mod[:, 8:16, :], 1.0, None, ALU.add).then_inc(s.dve, 1)
                dve.wait_ge(s.dve, 3)
                for b, (k, src, n0, n) in enumerate(turns):
                    dve.wait_ge(s.turned, 3 + b + 1)
                    dve.wait_ge(s.x_out, sum(1 for t in turns[:b + 1] if t[1] is xtok))
                    if src is ctok:
                        dst, q = S.ctxT[:, k, :], 1
                    else:
                        dst, q = S.hT[:, k, n0 * P:(n0 + n) * P], 0
                    nc.vector.tensor_scalar(dst, ps[:, (3 + b) % B, 0:n * P], S.sc1[:, k, q:q + 1],
                                            S.mod[:, k, q:q + 1], ALU.mult, ALU.add).then_inc(s.h_out, 1)


def stage_mod_rest(nc, I, S):
    A = S.arena
    with memory(S) as ctx:
        s = semaphores(nc, S, ctx, "cc", "dve")
        ring = [A.view(KC0 + i * KT * HALF, KT, HALF) for i in range(2)] + [A.view(WR0 + 4 * KT * P, KT, HALF)]
        md = Modulation(nc, S, ctx, "cb", MOD_H, MOD_N, ring,
                        [A.view(WR0 + 8 * KT * P + i * HALF, HALF)[0:2, :] for i in range(2)])
        w_mod = I["w_mod"].rearrange("l (k p) n -> p (l k) n", p=P)
        with block_of(nc, S) as block:
            @block.sync
            def _(sp):
                for n in range(md.n):
                    md.load(sp, w_mod, n)

            @block.tensor
            def _(pe):
                md.products(pe)

            @block.vector
            def _(dve):
                md.finish(dve).then_inc(s.dve, 1)
                dve.wait_ge(s.dve, 1)
                nc.vector.tensor_scalar(S.sc2, S.mod[:, 32:40, 0], 1.0, None, ALU.add).then_inc(s.dve, 1)
                w, b = col(S, "ln1_w", 0, KT), col(S, "ln1_b", 0, KT)
                nc.vector.tensor_scalar(S.x_w, w, ALPHA, None, ALU.mult)
                nc.vector.tensor_scalar(S.x_b, b, ALPHA, None, ALU.mult)
                dve.wait_ge(s.dve, 2)
                nc.vector.tensor_tensor(S.h_w, w, S.sc2, ALU.mult)
                nc.vector.tensor_tensor(S.h_b, b, S.sc2, ALU.mult).then_inc(s.dve, 1)
                dve.wait_ge(s.dve, 3)
                nc.vector.tensor_tensor(S.h_b, S.h_b, S.mod[:, 24:32, 0], ALU.add)


def dense(nc, S, name, weights, n_tiles, kt, moving, width, evac, ring_at, evac_engine="scalar",
          irregular=False, banks=8):
    halves = max(1, width // HALF)
    w = min(width, HALF)
    assert n_tiles % 4 == 0
    with memory(S) as ctx:
        s = semaphores(nc, S, ctx, name, "w0 w1 w2 w3 bank_free done")
        slots = [S.arena.view(ring_at + i * kt * P, kt, P) for i in range(4)]
        loaded = [s.w0, s.w1, s.w2, s.w3]
        ps = psum(nc, ctx, f"{name}_ps", banks, PSB)
        with block_of(nc, S) as block:
            @block.sync
            def _(sp):
                for j in range(4):
                    sp.dma_start(slots[j], weights(j)).then_inc(loaded[j], 16)
                if irregular:
                    for m in range(4, n_tiles):
                        sp.wait_ge(s.done, halves * (m - 3))
                        sp.dma_start(slots[m % 4], weights(m)).then_inc(loaded[m % 4], 16)
                elif n_tiles > 4:
                    with sp.Fori(1, n_tiles // 4) as i:
                        for j in range(4):
                            sp.wait_ge(s.done, i * (4 * halves) + halves * (j - 3))
                            sp.dma_start(slots[j], weights(i * 4 + j)).then_inc(loaded[j], 16)

            @block.tensor
            def _(pe):
                with pe.Fori(0, n_tiles // 4) as i:
                    for j in range(4):
                        pe.wait_ge(loaded[j], i * 16 + 16)
                        for h in range(halves):
                            pe.wait_ge(s.bank_free, i * (4 * halves) + (halves * j + h + 1))
                            for k in range(kt):
                                mm = pe.matmul(ps[:, (2 * j + h) % banks, 0:w], slots[j][:, k, :],
                                               moving(k)[:, h * w:(h + 1) * w],
                                               start=(k == 0), stop=(k == kt - 1))
                            mm.then_inc(s.done, 1)
    
            def copy_out(engine, e):
                e.sem_inc(s.bank_free, banks // 2 * halves)
                if irregular:
                    for m in range(n_tiles):
                        for h in range(halves):
                            e.wait_ge(s.done, halves * m + h + 1)
                            evac(engine, ps[:, (2 * (m % 4) + h) % banks, 0:w], m, h).then_inc(s.bank_free, 1)
                    return
                with e.Fori(0, n_tiles // 4) as i:
                    for j in range(4):
                        for h in range(halves):
                            e.wait_ge(s.done, i * (4 * halves) + (halves * j + h + 1))
                            evac(engine, ps[:, (2 * j + h) % banks, 0:w], i * 4 + j, h).then_inc(s.bank_free, 1)

            if evac_engine == "scalar":
                @block.scalar
                def _(act):
                    copy_out(nc.scalar, act)
            else:
                @block.vector
                def _(dve):
                    copy_out(nc.vector, dve)
    return s


class Chain:

    def __init__(self, engine, sem):
        self.engine, self.sem, self.n = engine, sem, 0

    def __call__(self, ins):
        ins.then_inc(self.sem, 1)
        self.n += 1
        self.engine.wait_ge(self.sem, self.n)


def stage_project_1(nc, I, S):
    w = I["w_in"].rearrange("l (k p) n -> p (l k) n", p=P)
    first = [O_Q, O_Q + P, O_K, O_K + P, O_O, O_O + P, O_B, O_B + P] + [O_C + i * P for i in range(4)]
    funcs = [ACT.Copy] * 4 + [ACT.Sigmoid] * 2 + [ACT.Gelu_apprx_tanh] * 2 + [ACT.Copy] * 2 + [ACT.Sigmoid] * 2

    def evac(act, bank, m, h):
        return act.activation(S.z[:, m, h * HALF:(h + 1) * HALF], bank, funcs[m])

    dense(nc, S, "p1", lambda m: w[:, :, first[m]:first[m] + P], Z_TILES, KT, lambda k: S.hT[:, k, :], T, evac,
          WR0, irregular=True, banks=4)


def stage_project_tokens_1(nc, I, S):
    A = S.arena
    n_tok = W_MIX + 16 + W_MIX
    wt = A.view(WR0, KT, n_tok)
    wd = A.view(WR0 + KT * n_tok, KT, W_MIX)
    wk = A.view(WR0 + KT * (n_tok + W_MIX), KT, W_MIX)
    w = I["w_in"].rearrange("l (k p) n -> p (l k) n", p=P)
    jobs = []
    for i in range(NT):
        tok = slice(i * P, (i + 1) * P)
        jobs.append((lambda k, tok=tok: S.hT[:, k, tok], lambda k: wt[:, k, 0:272], P, 272, "vg", i))
        jobs.append((lambda k, tok=tok: S.hT[:, k, tok], lambda k: wt[:, k, 272:528], P, 256, "sv", i))
    for i in range(NTC):
        tok = slice(i * P, (i + 1) * P)
        jobs.append((lambda k, tok=tok: S.ctxT[:, k, tok], lambda k: wt[:, k, 0:272], P, 272, "vg", NT + i))
    for j in range(S5L):
        jobs.append((lambda k, j=j: S.hT[:, k, j::S5L], lambda k: wd[:, k, :], P, 256, "s5", j))
    for j in range(S5L):
        jobs.append((lambda k, j=j: S.ctxT[:, k, j::S5L], lambda k: wd[:, k, :], S5CC, 256, "s5c", j))
    for m in range(2):
        jobs.append((lambda k, m=m: wk[:, k, m * P:(m + 1) * P], lambda k: S.ctxT[:, k, :], P, TC, "kc", m))
    with memory(S) as ctx:
        s = semaphores(nc, S, ctx, "t1", "wt wd wk done free")
        ps = psum(nc, ctx, "t1_ps", 4, PSB)
        with block_of(nc, S) as block:
            @block.sync
            def _(sp):
                for a, b, off, n in ((0, 256, O_V, 256), (256, 272, O_G, 16), (272, 528, O_B + W_MIX, 256)):
                    sp.dma_start(wt[:, :, a:b], w[:, :, off:off + n]).then_inc(s.wt, 16)
                sp.dma_start(wd, w[:, :, O_D:O_D + W_MIX]).then_inc(s.wd, 16)
                sp.dma_start(wk, w[:, :, O_K:O_K + W_MIX]).then_inc(s.wk, 16)

            @block.tensor
            def _(pe):
                pe.wait_ge(s.wt, 48)
                for n, (sta, mov, rows, cols, kind, _) in enumerate(jobs):
                    if n == 2 * NT + NTC:
                        pe.wait_ge(s.wd, 16)
                    if kind == "kc":
                        pe.wait_ge(s.wk, 16)
                    if n >= 4:
                        pe.wait_ge(s.free, n - 3)
                    for k in range(KT):
                        mm = pe.matmul(ps[0:rows, n % 4, 0:cols], sta(k), mov(k), start=(k == 0), stop=(k == KT - 1))
                    mm.then_inc(s.done, 1)

            @block.vector
            def _(dve):
                nc.vector.memset(S.vt[:, :, HD:HD + 1], 1.0)

            @block.scalar
            def _(act):
                for n, (_, _, rows, cols, kind, i) in enumerate(jobs):
                    act.wait_ge(s.done, n + 1)
                    b = ps[0:rows, n % 4, 0:cols]
                    if kind == "sv":
                        c = nc.scalar.activation(S.sv[:, i, :], b, ACT.Gelu_apprx_tanh)
                    elif kind == "vg":
                        nc.scalar.activation(S.vt[:, i * HEADS:(i + 1) * HEADS, 0:HD],
                                             b[:, 0:256].rearrange("p (h d) -> p h d", h=HEADS), ACT.Copy)
                        c = nc.scalar.activation(S.gates[:, i, :], b[:, 256:272], ACT.Copy)
                    elif kind == "s5":
                        c = nc.scalar.activation(S.u5[:, :, i, :], b.rearrange("p (g q) -> p g q", g=S5G), ACT.Copy)
                    elif kind == "s5c":
                        c = nc.scalar.activation(S.u5c[0:rows, :, i, :], b.rearrange("p (g q) -> p g q", g=S5G),
                                                 ACT.Copy)
                    else:
                        c = nc.scalar.activation(S.kc[:, i, :], b, ACT.Copy)
                    c.then_inc(s.free, 1)


def normalize(nc, S, name, src, n_tiles, count, eps, center, tmp, rs, final, source=None,
              scale_after=None, final_dve=None):
    with memory(S) as ctx:
        s = semaphores(nc, S, ctx, name, "sums centered squared var root inverse scaled")
        ps = psum(nc, ctx, f"{name}_ps", 4, PSB)
        cut = [slice(0, HALF), slice(HALF, T)]
        with block_of(nc, S) as block:
            @block.tensor
            def _(pe):
                if source:
                    pe.wait_ge(*source)
                for h in range(2):
                    if center:
                        for k in range(n_tiles):
                            mm = pe.matmul(ps[:, h, :], S.ones, src(k)[:, cut[h]], start=(k == 0),
                                           stop=(k == n_tiles - 1))
                        mm.then_inc(s.sums, 1)
                for h in range(2):
                    pe.wait_ge(s.squared, n_tiles * (h + 1))
                    for k in range(n_tiles):
                        mm = pe.matmul(ps[:, 2 + h, :], S.ones, tmp(k)[:, cut[h]], start=(k == 0),
                                       stop=(k == n_tiles - 1))
                    mm.then_inc(s.var, 1)

            @block.vector
            def _(dve):
                if center:
                    for h in range(2):
                        dve.wait_ge(s.sums, h + 1)
                        for k in range(n_tiles):
                            nc.vector.scalar_tensor_tensor(out=src(k)[:, cut[h]], in0=ps[:, h, :],
                                                           scalar=-1.0 / count, in1=src(k)[:, cut[h]],
                                                           op0=ALU.mult, op1=ALU.add).then_inc(s.centered, 1)
                for h in range(2):
                    dve.wait_ge(s.var, h + 1)
                    nc.vector.tensor_scalar(rs[:, cut[h]], ps[:, 2 + h, :], 1.0 / count, eps, ALU.mult, ALU.add)\
                        .then_inc(s.root, 1)
                    dve.wait_ge(s.inverse, h + 1)
                    nc.vector.reciprocal(rs[:, cut[h]], rs[:, cut[h]]).then_inc(s.scaled, 1)
                    dve.wait_ge(s.scaled, (n_tiles + 1) * h + 1)
                    if scale_after:
                        dve.wait_ge(*scale_after)
                    for k in range(n_tiles):
                        nc.vector.tensor_tensor(src(k)[:, cut[h]], src(k)[:, cut[h]], rs[:, cut[h]], ALU.mult)\
                            .then_inc(s.scaled, 1)
                if final_dve:
                    for h in range(2):
                        for k in range(n_tiles):
                            dve.wait_ge(s.scaled, (n_tiles + 1) * h + k + 2)
                            final_dve(k, h, cut[h])

            @block.scalar
            def _(act):
                for h in range(2):
                    for k in range(n_tiles):
                        if center:
                            act.wait_ge(s.centered, n_tiles * h + k + 1)
                        nc.scalar.activation(tmp(k)[:, cut[h]], src(k)[:, cut[h]], ACT.Square)\
                            .then_inc(s.squared, 1)
                for h in range(2):
                    act.wait_ge(s.root, h + 1)
                    nc.scalar.activation(rs[:, cut[h]], rs[:, cut[h]], ACT.Sqrt).then_inc(s.inverse, 1)
                for h in range(2):
                    for k in range(n_tiles):
                        act.wait_ge(s.scaled, (n_tiles + 1) * h + k + 2)
                        final(act, k, h, cut[h])


def stage_conv(nc, I, S):
    pad = S.arena.view(X0, 2 * ROWS, GRID + 2 * CONV_PAD)
    acc = S.arena.view(X0 + 2 * ROWS * (GRID + 2 * CONV_PAD), 2, T)
    tmp = S.arena.view(X0 + 2 * ROWS * (GRID + 2 * CONV_PAD) + 2 * T, 3, T)
    with memory(S) as ctx:
        s = semaphores(nc, S, ctx, "cv", "pads taps")
        with block_of(nc, S) as block:
            @block.vector
            def _(dve):
                nc.vector.memset(pad[:, :, 0:CONV_PAD], 0.0).then_inc(s.pads, 1)
                nc.vector.memset(pad[:, :, CONV_PAD + GRID:], 0.0).then_inc(s.pads, 1)
                for c in range(2):
                    nc.vector.tensor_tensor(pad[:, c * ROWS:(c + 1) * ROWS, CONV_PAD:CONV_PAD + GRID],
                                            S.z[:, 8 + c, :].rearrange("p (r t) -> p r t", r=ROWS),
                                            S.z[:, 10 + c, :].rearrange("p (r t) -> p r t", r=ROWS),
                                            ALU.mult).then_inc(s.pads, 1)
                dve.wait_ge(s.pads, 4)
                for w in range(CONV_W):
                    for c in range(2):
                        src = pad[:, c * ROWS:(c + 1) * ROWS, w:w + GRID]
                        a = acc[:, c, :].rearrange("p (r t) -> p r t", r=ROWS)
                        if w == 0:
                            nc.vector.tensor_scalar(a, src, col(S, "conv_w", c), col(S, "conv_b", c), ALU.mult,
                                                    ALU.add).then_inc(s.taps, 1)
                        else:
                            dve.wait_ge(s.taps, 2 * (w - 1) + c + 1)
                            nc.vector.scalar_tensor_tensor(out=a, in0=src, scalar=col(S, "conv_w", 2 * w + c),
                                                           in1=a, op0=ALU.mult, op1=ALU.add).then_inc(s.taps, 1)

    def final(act, k, h, cut):
        nc.scalar.activation(S.yT[:, 4 + k, cut], acc[:, k, cut], ACT.Silu, bias=col(S, "conv_ln_b", k),
                             scale=col(S, "conv_ln_w", k))

    normalize(nc, S, "cn", lambda k: acc[:, k, :], 2, W_MIX, LN_EPS, True, lambda k: tmp[:, k, :], tmp[:, 2, :],
              final, source=(s.taps, 2 * CONV_W))


def stage_sgu(nc, I, S):
    A = S.arena
    G, GD = 4, 64
    ws = A.view(WR0, G, P)
    wsT = A.view(WR0 + 512, G, P)
    bs = A.view(WR0 + 1024, G, P)
    lnw = A.view(WR0 + 1536, W_MIX)
    lnb = A.view(WR0 + 1792, W_MIX)
    st = A.view(WR0 + 2048, NT, 6)
    mv = A.view(WR0 + 2100, NT, 2)
    rs = A.view(WR0 + 2120, NT)
    with memory(S) as ctx:
        s = semaphores(nc, S, ctx, "sg", "ws rows dve root normed wT wTc done")
        pw = psum(nc, ctx, "sg_w", PSB)
        po = psum(nc, ctx, "sg_o", 4, PSB)
        with block_of(nc, S) as block:
            @block.sync
            def _(sp):
                sp.dma_start(ws, I["sgu_w"].rearrange("l g t s -> t (l g) s")).then_inc(s.ws, 16)
                sp.dma_start(bs[0:1, :, :], I["sgu_b"]).then_inc(s.rows, 16)
                sp.dma_start(lnw, I["sgu_ln_w"].broadcast_to([P, W_MIX])).then_inc(s.rows, 16)
                sp.dma_start(lnb, I["sgu_ln_b"].broadcast_to([P, W_MIX])).then_inc(s.rows, 16)

            @block.vector
            def _(dve):
                step = Chain(dve, s.dve)
                for i in range(NT):
                    c = nc.vector.bn_stats(st[:, i, :], S.sv[:, i, :])
                step(c)
                for i in range(NT):
                    c = nc.vector.bn_aggr(mv[:, i, :], st[:, i, :])
                step(c)
                nc.vector.tensor_scalar(rs, mv[:, :, 1], LN_EPS, None, ALU.add).then_inc(s.root, 1)
                dve.wait_ge(s.ws, 16)
                dve.wait_ge(s.wT, 1)
                nc.vector.tensor_copy(wsT, pw[:, :].rearrange("p (g t) -> p g t", g=G)).then_inc(s.wTc, 1)
                dve.wait_ge(s.root, 2)
                step(nc.vector.reciprocal(rs, rs))
                for i in range(NT):
                    c = nc.vector.tensor_scalar(S.sv[:, i, :], S.sv[:, i, :], mv[:, i, 0:1], rs[:, i:i + 1],
                                                ALU.subtract, ALU.mult)
                step(c)
                dve.wait_ge(s.rows, 48)
                step(nc.vector.tensor_tensor(S.sv, S.sv, lnw.unsqueeze(1).broadcast_to([P, NT, W_MIX]), ALU.mult))
                nc.vector.tensor_tensor(S.sv, S.sv, lnb.unsqueeze(1).broadcast_to([P, NT, W_MIX]), ALU.add)\
                    .then_inc(s.normed, 1)
                for n in range(4):
                    c, h = n // 2, n % 2
                    cut = slice(h * HALF, (h + 1) * HALF)
                    dve.wait_ge(s.done, n + 1)
                    nc.vector.tensor_tensor(S.yT[:, 2 + c, cut], po[:, n, :], S.z[:, 6 + c, cut], ALU.mult)

            @block.scalar
            def _(act):
                act.wait_ge(s.root, 1)
                nc.scalar.activation(rs, rs, ACT.Sqrt).then_inc(s.root, 1)

            @block.tensor
            def _(pe):
                pe.wait_ge(s.ws, 16)
                for g in range(G):
                    t = pe.transpose(pw[:, g * P:(g + 1) * P], ws[:, g, :], S.ident)
                t.then_inc(s.wT, 1)
                pe.wait_ge(s.rows, 48)
                pe.wait_ge(s.wTc, 1)
                pe.wait_ge(s.normed, 1)
                for n in range(4):
                    c, h = n // 2, n % 2
                    for i in range(4):
                        for e in range(2):
                            g, o = 2 * c + e, po[e * GD:(e + 1) * GD, n, i * P:(i + 1) * P]
                            pe.matmul(o, S.ones[0:1, 0:GD], bs[0:1, g, :], start=True, stop=False)
                            mm = pe.matmul(o, S.sv[:, 4 * h + i, g * GD:(g + 1) * GD], wsT[:, g, :],
                                           start=False, stop=True)
                    mm.then_inc(s.done, 1)



def log1p_tail(step, nc, e, ln, w, out_t):
    step(nc.vector.tensor_scalar(w, e, -0.25, 1.0 / 3.0, ALU.mult, ALU.add))
    step(nc.vector.tensor_tensor(w, w, e, ALU.mult))
    step(nc.vector.tensor_scalar(w, w, -0.5, None, ALU.add))
    step(nc.vector.tensor_tensor(w, w, e, ALU.mult))
    step(nc.vector.tensor_scalar(w, w, 1.0, None, ALU.add))
    step(nc.vector.tensor_tensor(w, w, e, ALU.mult))
    step(nc.vector.tensor_tensor(w, w, ln, ALU.subtract))
    step(nc.vector.tensor_scalar(e, e, 1.0 / 128.0, None, ALU.is_lt))
    step(nc.vector.tensor_tensor(w, w, e, ALU.mult))
    step(nc.vector.tensor_tensor(out_t, w, ln, ALU.add))


def stage_mlstm_gates(nc, I, S):
    A = S.arena
    N = NT + NTC
    bias = A.view(WR0, 16)
    fg = A.view(WR0 + 16, N, 8)
    e, ln, w = (A.view(WR0 + 96 + 80 * i, N, 8) for i in range(3))
    lf = A.view(WR0 + 336, N, 8)
    rows = A.view(C0, N * P)[0:8, :]
    first = A.view(WR0 + 500, 1)[0:8, :]
    with memory(S) as ctx:
        s = semaphores(nc, S, ctx, "mg", "bias dve act exped lf sums a turned max Mt")
        pb = psum(nc, ctx, "mg_b", PSB)
        pt = psum(nc, ctx, "mg_t", 3, PSB)
        pm = psum(nc, ctx, "mg_m", PSB)
        b = pb[:, 0:80].rearrange("p (i n) -> p i n", n=8)
        with block_of(nc, S) as block:
            @block.sync
            def _(sp):
                sp.dma_start(bias, I["mlstm_gate_bias"].broadcast_to([P, 16])).then_inc(s.bias, 16)

            @block.vector
            def _(dve):
                step = Chain(dve, s.dve)
                dve.wait_ge(s.bias, 16)
                g = S.gates.rearrange("p i (d k h) -> p i d k h", d=2, k=2)
                step(nc.vector.tensor_tensor(S.gates, S.gates, bias.unsqueeze(1).broadcast_to([P, N, 16]), ALU.add))
                for d in range(2):
                    c = nc.vector.tensor_copy(fg[:, :, 4 * d:4 * d + 4], g[:, :, d, 1, :])
                step(c)
                step(nc.vector.tensor_scalar(w, fg, -1.0, None, ALU.mult))
                nc.vector.tensor_tensor(e, w, fg, ALU.min).then_inc(s.act, 1)
                dve.wait_ge(s.exped, 2)
                log1p_tail(step, nc, e, ln, w, w)
                step(nc.vector.tensor_scalar(fg, fg, 0.0, None, ALU.min))
                nc.vector.tensor_tensor(lf, fg, w, ALU.subtract).then_inc(s.lf, 1)
                dve.wait_ge(s.sums, 1)
                for d in range(2):
                    nc.vector.tensor_tensor(S.a[:, 0:NT, 4 * d:4 * d + 4], g[:, 0:NT, d, 0, :],
                                            b[:, 0:NT, 4 * d:4 * d + 4], ALU.subtract).then_inc(s.a, 1)
                    nc.vector.tensor_tensor(S.a[:, NT:N, 4 * d:4 * d + 4], g[:, NT:N, d, 0, :],
                                            b[:, NT:N, 4 * d:4 * d + 4], ALU.add).then_inc(s.a, 1)
                dve.wait_ge(s.turned, 1)
                for i in range(3):
                    n = 512 if i < 2 else 256
                    c = nc.vector.tensor_copy(rows[:, 512 * i:512 * i + n], pt[0:8, i, 0:n])
                step(c)
                step(nc.vector.tensor_reduce(first, rows[:, T:], AX, ALU.max))
                toks = rows[:, 0:T]
                nc.vector.tensor_tensor_scan(S.M[0][:, :], toks, toks, first, ALU.max, ALU.max).then_inc(s.max, 1)
                nc.vector.tensor_tensor_scan(S.M[1][:, ::-1], toks[:, ::-1], toks[:, ::-1], first, ALU.max,
                                             ALU.max).then_inc(s.max, 1)
                dve.wait_ge(s.Mt, 1)
                for d in range(2):
                    v = pm[:, 64 * d:64 * d + 64].rearrange("p (i n) -> p i n", n=8)[:, :, 4 * d:4 * d + 4]
                    c = nc.vector.tensor_copy(S.expn[:, :, 4 * d:4 * d + 4], v)
                step(c)
                nc.vector.tensor_tensor(S.expn, S.expn, b[:, 0:NT, :], ALU.add).then_inc(s.act, 1)
                for d in range(2):
                    nc.vector.tensor_scalar(S.M[d][:, :], S.M[d][:, :], -1.0, None, ALU.mult)

            @block.scalar
            def _(act):
                act.wait_ge(s.act, 1)
                nc.scalar.activation(e, e, ACT.Exp).then_inc(s.exped, 1)
                act.wait_ge(s.exped, 1)
                nc.scalar.activation(ln, e, ACT.Ln, bias=1.0).then_inc(s.exped, 1)
                act.wait_ge(s.act, 2)
                nc.scalar.activation(S.expn, S.expn, ACT.Exp, scale=-1.0)

            @block.tensor
            def _(pe):
                pe.wait_ge(s.lf, 1)
                for d in range(2):
                    cut = slice(4 * d, 4 * d + 4)
                    for tiles, own, before in ((range(NT), S.t_le if d == 0 else S.t_ge, d == 0),
                                               (range(NT, N), S.t_gt if d == 0 else S.t_lt, d == 1)):
                        for i in tiles:
                            others = [r for r in tiles if (r < i if before else r > i)]
                            mm = pe.matmul(b[:, i, cut], own, lf[:, i, cut], start=True, stop=not others)
                            for r in others:
                                mm = pe.matmul(b[:, i, cut], S.ones, lf[:, r, cut], start=False,
                                               stop=(r == others[-1]))
                mm.then_inc(s.sums, 1)
                pe.wait_ge(s.a, 4)
                for i in range(N):
                    t = pe.transpose(pt[0:8, i // 4, (i % 4) * P:(i % 4 + 1) * P], S.a[:, i, :], S.ident)
                t.then_inc(s.turned, 1)
                pe.wait_ge(s.max, 2)
                for d in range(2):
                    for i in range(NT):
                        t = pe.transpose(pm[:, 64 * d + 8 * i:64 * d + 8 * i + 8],
                                         S.M[d][:, i * P:(i + 1) * P], S.ident[0:8, 0:8])
                t.then_inc(s.Mt, 1)


def stage_mlstm(nc, I, S):
    A = S.arena
    N = NT + NTC
    order = [NT, NT + 1] + list(range(NT))
    def span(d, i):
        if i >= NT:
            return 0, T
        return (i * P, T) if d == 0 else (0, (i + 1) * P)
    NM = A.view(SV0, 2 * HEADS, T)
    W = A.view(Z0 + 6 * T, 2, 2, T)
    DS = 3
    Db = A.view(SV0 + 8 * T, DS, 2, T)
    sums = A.view(SV0 + 14 * T, 2, 2, 260)
    den = A.view(M_SMALL + 150, NT)
    with memory(S) as ctx:
        s = semaphores(nc, S, ctx, "ml", "rows rowsc scores e0 e1 m0 m1 w pv dve out")
        pS = psum(nc, ctx, "ml_s", 4, PSB)
        pO = psum(nc, ctx, "ml_o", 4, PSB)
        tiles = [(h, o, i) for h in range(HEADS) for o, i in enumerate(order)]
        with block_of(nc, S) as block:
            @block.tensor
            def _(pe):
                for u in range(2 * HEADS):
                    h, d = u // 2, u % 2
                    if u >= 2:
                        pe.wait_ge(s.rowsc, u - 1)
                    for c in range(2):
                        n = 4 * d + h
                        mm = pe.matmul(pS[:, 2 * (u % 2) + c, :], S.ident[0:8, n:n + 1].broadcast_to([8, P]),
                                       S.M[d][:, c * HALF:(c + 1) * HALF], start=True, stop=True)
                    mm.then_inc(s.rows, 1)

                def scores(t):
                    h, o, i = tiles[t]
                    part = slice(64 * (h % 2), 64 * (h % 2) + 64)
                    if t >= 2:
                        pe.wait_ge(s.w, 2 * (t - 1))
                    else:
                        pe.wait_ge(s.rowsc, 2 * HEADS - 1 + t)
                    key = (S.kc[part, h // 2, (i - NT) * P:(i - NT + 1) * P] if i >= NT else
                           S.z[part, 2 + h // 2, i * P:(i + 1) * P])
                    for c in range(2):
                        mm = pe.matmul(pS[:, 2 * (t % 2) + c, :], key,
                                       S.z[part, h // 2, c * HALF:(c + 1) * HALF], start=True, stop=True)
                    mm.then_inc(s.scores, 1)

                scores(0)
                for t, (h, o, i) in enumerate(tiles):
                    if t + 1 < len(tiles):
                        scores(t + 1)
                    for d in range(2):
                        pe.wait_ge(s.w, 2 * t + d + 1)
                        if o == 0 and h:
                            pe.wait_ge(s.out, 2 * (h - 1) + d + 1)
                        a, b = span(d, i)
                        for j in range(a // P, b // P):
                            last = j if d == 0 else NT - 1
                            mm = pe.matmul(pO[:, 2 * d + j // 4, (j % 4) * 65:(j % 4) * 65 + 65],
                                           W[:, t % 2, d, j * P:(j + 1) * P], S.vt[:, i * HEADS + h, :],
                                           start=(o == 0 and j % 4 == 0),
                                           stop=(i == last and j % 4 == 3))
                        mm.then_inc(s.pv, 1)

            @block.scalar
            def _(act):
                for u in range(2 * HEADS):
                    act.wait_ge(s.rows, u + 1)
                    nc.scalar.activation(NM[:, u, :],
                                         pS[:, 2 * (u % 2):2 * (u % 2) + 2, :].rearrange("p a b -> p (a b)"),
                                         ACT.Copy).then_inc(s.rowsc, 1)
                act.wait_ge(s.rowsc, 2 * HEADS)
                for t, (h, o, i) in enumerate(tiles):
                    if t >= DS:
                        act.wait_ge(s.w, 2 * (t - DS + 1))
                    for d in range(2):
                        a, b = span(d, i)
                        nc.scalar.activation(Db[:, t % DS, d, a:b], NM[:, 2 * h + d, a:b], ACT.Exp,
                                             bias=S.a[:, i, 4 * d + h:4 * d + h + 1])\
                            .then_inc((s.e0, s.e1)[d], 1)

            @block.gpsimd
            def _(pool):
                for t, (h, o, i) in enumerate(tiles):
                    if i >= NT:
                        continue
                    for d in range(2):
                        pool.wait_ge((s.e0, s.e1)[d], t + 1)
                        blk = Db[:, t % DS, d, i * P:(i + 1) * P]
                        sign = 1 if d == 0 else -1
                        pool.affine_select(out=blk, in_=blk, compare_op=ALU.is_ge, fill=0.0, base=0,
                                           pattern=[[sign, P]], channel_multiplier=-sign)\
                            .then_inc((s.m0, s.m1)[d], 1)

            @block.vector
            def _(dve):
                step = Chain(dve, s.dve)

                def read_out(h):
                    for d in range(2):
                        dve.wait_ge(s.pv, 2 * N * h + 2 * N - 1 + d)
                        nc.vector.tensor_copy(sums[:, d, :, :], pO[:, 2 * d:2 * d + 2, 0:260]).then_inc(s.out, 1)

                def divide(h):
                    for d in range(2):
                        dve.wait_ge(s.out, 2 * h + d + 1)
                        o = sums[:, d, :, :].rearrange("p c (j d) -> p (c j) d", d=65)
                        step(nc.vector.scalar_tensor_tensor(out=den, in0=o[:, :, 64], scalar=-1.0, in1=o[:, :, 64],
                                                            op0=ALU.mult, op1=ALU.max))
                        step(nc.vector.tensor_tensor(den, den, S.expn[:, :, 4 * d + h], ALU.max))
                        step(nc.vector.reciprocal(den, den))
                        rb = den.unsqueeze(2).broadcast_to([P, NT, HD])
                        hv = S.htok[:, :, h, :]
                        if d == 0:
                            step(nc.vector.tensor_tensor(hv, o[:, :, 0:64], rb, ALU.mult))
                        else:
                            tmp = S.htmp.rearrange("p c j d -> p (c j) d")
                            step(nc.vector.tensor_tensor(tmp, o[:, :, 0:64], rb, ALU.mult))
                            step(nc.vector.tensor_tensor(hv, hv, tmp, ALU.add))

                for t, (h, o, i) in enumerate(tiles):
                    dve.wait_ge(s.scores, t + 1)
                    for d in range(2):
                        a, b = span(d, i)
                        if i >= NT:
                            dve.wait_ge((s.e0, s.e1)[d], t + 1)
                        else:
                            dve.wait_ge((s.m0, s.m1)[d], NT * h + i + 1)
                        if t >= 2:
                            dve.wait_ge(s.pv, 2 * (t - 2) + d + 1)
                        sc = pS[:, 2 * (t % 2):2 * (t % 2) + 2, :].rearrange("p a b -> p (a b)")
                        nc.vector.scalar_tensor_tensor(out=W[:, t % 2, d, a:b], in0=sc[:, a:b],
                                                       scalar=HD ** -0.5, in1=Db[:, t % DS, d, a:b],
                                                       op0=ALU.mult, op1=ALU.mult).then_inc(s.w, 1)
                    if h and o == 0:
                        read_out(h - 1)
                    if h and o == 2:
                        divide(h - 1)
                read_out(HEADS - 1)
                divide(HEADS - 1)


def stage_mlstm_out(nc, I, S):
    A = S.arena
    h = S.htok
    NH = NT * HEADS
    flat = h.rearrange("p i h d -> p (i h) d")
    sq = A.view(SV0, NH, HD)
    mu = A.view(WR0 + 4096, NH)
    rs = A.view(WR0 + 4200, NH)
    with memory(S) as ctx:
        s = semaphores(nc, S, ctx, "mo", "dve root turned out")
        ps = psum(nc, ctx, "mo_ps", 4, PSB)
        with block_of(nc, S) as block:
            @block.vector
            def _(dve):
                step = Chain(dve, s.dve)
                step(nc.vector.tensor_reduce(mu, flat, AX, ALU.add))
                step(nc.vector.tensor_scalar(mu, mu, 1.0 / HD, None, ALU.mult))
                step(nc.vector.tensor_tensor(flat, flat, mu.unsqueeze(2).broadcast_to([P, NH, HD]), ALU.subtract))
                step(nc.vector.tensor_tensor(sq, flat, flat, ALU.mult))
                step(nc.vector.tensor_reduce(rs, sq, AX, ALU.add))
                nc.vector.tensor_scalar(rs, rs, 1.0 / HD, LN_EPS, ALU.mult, ALU.add).then_inc(s.root, 1)
                dve.wait_ge(s.root, 2)
                step(nc.vector.reciprocal(rs, rs))
                step(nc.vector.tensor_tensor(flat, flat, rs.unsqueeze(2).broadcast_to([P, NH, HD]), ALU.mult))
                for n in range(4):
                    c, half = n // 2, n % 2
                    cut = slice(half * HALF, (half + 1) * HALF)
                    dve.wait_ge(s.turned, n + 1)
                    nc.vector.scalar_tensor_tensor(out=S.yT[:, c, cut], in0=ps[:, n, :],
                                                   scalar=col(S, "mlstm_norm_w", c), in1=S.z[:, 4 + c, cut],
                                                   op0=ALU.mult, op1=ALU.mult)

            @block.scalar
            def _(act):
                act.wait_ge(s.root, 1)
                nc.scalar.activation(rs, rs, ACT.Sqrt).then_inc(s.root, 1)

            @block.tensor
            def _(pe):
                pe.wait_ge(s.dve, 7)
                for n in range(4):
                    c, half = n // 2, n % 2
                    for i in range(4):
                        t = pe.transpose(ps[:, n, i * P:(i + 1) * P],
                                         h[:, 4 * half + i, 2 * c:2 * c + 2, :].rearrange("p h d -> p (h d)"),
                                         S.ident)
                    t.then_inc(s.turned, 1)



TWO_PI = 2.0 * math.pi
PI_A = 6.28125
PI_B = 0.0019350051879882812
PI_C = TWO_PI - PI_A - PI_B
MAGIC = 12582912.0


def complex_times(step, nc, out, a, b, tmp):
    (o_re, o_im), (a_re, a_im), (b_re, b_im) = out, a, b
    nc.vector.tensor_tensor(tmp, a_im, b_im, ALU.mult)
    step(nc.vector.tensor_tensor(o_re, a_re, b_re, ALU.mult))
    step(nc.vector.tensor_tensor(o_re, o_re, tmp, ALU.subtract))
    nc.vector.tensor_tensor(tmp, a_im, b_re, ALU.mult)
    step(nc.vector.tensor_tensor(o_im, a_re, b_im, ALU.mult))
    step(nc.vector.tensor_tensor(o_im, o_im, tmp, ALU.add))


def s5_views(S):
    A = S.arena
    V = Views()
    DT = 2 * KT
    z = Z0 + 6 * T
    V.ca = [A.view(z + i * DT * 9 * S5P, DT, 9 * S5P) for i in range(2)]
    z += 2 * DT * 9 * S5P
    V.bb = [A.view(z + i * DT * S5P, DT, S5P) for i in range(2)]
    z += 2 * DT * S5P
    V.pw = [A.view(z + i * DT * 9, 9, DT) for i in range(2)]
    z += 2 * DT * 9
    V.p = [A.view(z + i * DT, DT) for i in range(24)]
    z += 24 * DT
    assert z <= Z0 + 12 * T
    V.K = A.view(SV0, S5G, P)
    V.wvT = [A.view(WR0 + i * 2048, DT, P) for i in range(2)]
    V.wv = [A.view(WR0 + 4096 + i * 2048, DT, S5L * S5P) for i in range(2)]
    V.tab = [A.view(WR0 + 4096 + i * 2560, DT, S5CC + S5C) for i in range(2)]
    V.T = [A.view(H0, S5G, P), A.view(C0, S5G, P)]
    V.Kb = A.view(H0 + 6 * T, S5G, P)
    V.UT = A.view(X0, S5G, S5C + 2 * S5CC)
    V.st = [A.view(X0 + 3072 + i * 2560, DT, S5CC + S5C) for i in range(2)]
    V.yc = A.view(H0, S5L, W_MIX)
    V.ys = A.view(C0, 2, T)
    return V


def stage_s5_params(nc, I, S):
    V = s5_views(S)
    A = S.arena
    DT = 2 * KT
    ld, dt, are, aim, x, y, k1, k2, mag, cs, sn, a1, n1, q_re, q_im, w1, w2, w3, u_re, u_im, v_re, v_im, r8, w4 = V.p
    S.s5_r8, S.s5_u = r8, (u_re, u_im)
    br = [A.view(X0 + i * 128, KT, S5P) for i in range(2)]
    crow = [A.view(X0 + 256 + i * P, P) for i in range(2)]
    cT = [A.view(X0 + 512 + i * P, KT, S5P) for i in range(2)]
    arow = [A.view(X0 + 768 + i * P, P)[0:DT, :] for i in range(2)]
    dcol = A.view(X0 + 1024, S5G)
    ldrow = A.view(X0 + 1040, 2 * DT)
    drow = A.view(X0 + 1100, S5L, S5P)[0:S5G, :, :]
    big = A.view(X0 + 2048, DT * 9 * S5P)
    with memory(S) as ctx:
        s = semaphores(nc, S, ctx, "s5", "in_a in_dt in_b in_c in_d turned dve a_dt a_sin a_out zeros shift T0 T1 ca wv wvd tc done"
                                      " shift2 mm")
        pt = psum(nc, ctx, "s5_t", PSB)
        pT = psum(nc, ctx, "s5_T", 4, PSB)
        pw_ps = psum(nc, ctx, "s5_w", 2, PSB)
        with block_of(nc, S) as block:
            @block.sync
            def _(sp):
                for n, name in enumerate(("s5_a_re", "s5_a_im")):
                    sp.dma_start(arow[n], I[name].rearrange("l d (t e) n -> (l d t) (e n)", e=2)).then_inc(s.in_a, 16)
                sp.dma_start(ldrow, I["s5_log_dt"].rearrange("l d g -> l (d g)").broadcast_to([P, 2 * DT]))\
                    .then_inc(s.in_dt, 16)
                for n, name in enumerate(("s5_b_re", "s5_b_im")):
                    sp.dma_start(br[n], I[name].rearrange("l (t e) n p -> (e n) (l t) p", e=2)).then_inc(s.in_b, 16)
                for n, name in enumerate(("s5_c_re", "s5_c_im")):
                    for t in range(KT):
                        sp.dma_start(crow[n][16 * t:16 * t + 16, :].rearrange("p (e n) -> p e n", e=2),
                                     I[name][0, 2 * t:2 * t + 2].rearrange("e p n -> p e n")).then_inc(s.in_c, 16)
                sp.dma_start(drow, I["s5_d"].rearrange("l (g p) -> g l p", p=S5P).broadcast_to([S5G, S5L, S5P]))\
                    .then_inc(s.in_d, 16)
                for d in range(2):
                    sp.wait_ge(s.zeros, 2)
                    sp.wait_ge((s.T0, s.T1)[d], 4)
                    for j in range(S5L):
                        if d == 0:
                            dst, src = V.K[16 * j:16 * j + 16, :, 16 * j:P], V.T[0][0:16, :, 0:P - 16 * j]
                        else:
                            dst, src = V.Kb[16 * j:16 * j + 16, :, 0:16 * j + 16], V.T[1][0:16, :, 16 * (7 - j):P]
                        sp.dma_start(dst, src).then_inc((s.shift, s.shift2)[d], 16)

            @block.scalar
            def _(act):
                act.wait_ge(s.in_dt, 16)
                for e in range(2):
                    half = slice(64 * e, 64 * e + 64)
                    nc.scalar.activation(dt[half, :], ldrow[half, e::2], ACT.Exp).then_inc(s.a_dt, 1)
                act.wait_ge(s.a_sin, 1)
                nc.scalar.activation(sn, k1, ACT.Sin).then_inc(s.a_out, 1)
                nc.scalar.activation(cs, k2, ACT.Sin).then_inc(s.a_out, 1)
                nc.scalar.activation(mag, x, ACT.Exp).then_inc(s.a_out, 1)
                nc.scalar.activation(r8, x, ACT.Exp, scale=float(S5L)).then_inc(s.a_out, 1)

            @block.vector
            def _(dve):
                step = Chain(dve, s.dve)
                nc.vector.memset(V.K, 0.0).then_inc(s.zeros, 1)
                nc.vector.memset(V.Kb, 0.0).then_inc(s.zeros, 1)
                dve.wait_ge(s.turned, 1)
                nc.vector.tensor_copy(are, pt[:, 0:DT])
                step(nc.vector.tensor_copy(aim, pt[:, DT:2 * DT]))
                dve.wait_ge(s.a_dt, 2)
                step(nc.vector.tensor_tensor(x, are, dt, ALU.mult))
                step(nc.vector.tensor_tensor(y, aim, dt, ALU.mult))
                for k, quarter in ((k1, 0.0), (k2, 0.25)):
                    step(nc.vector.tensor_scalar(w1, y, 1.0 / TWO_PI, quarter, ALU.mult, ALU.add))
                    step(nc.vector.tensor_scalar(w1, w1, MAGIC, None, ALU.add))
                    step(nc.vector.tensor_scalar(w1, w1, -MAGIC, None, ALU.add))
                    step(nc.vector.scalar_tensor_tensor(out=k, in0=w1, scalar=-PI_A, in1=y, op0=ALU.mult, op1=ALU.add))
                    step(nc.vector.scalar_tensor_tensor(out=k, in0=w1, scalar=-PI_B, in1=k, op0=ALU.mult, op1=ALU.add))
                    step(nc.vector.scalar_tensor_tensor(out=k, in0=w1, scalar=-PI_C, in1=k, op0=ALU.mult, op1=ALU.add))
                    if quarter:
                        step(nc.vector.tensor_scalar(k, k, math.pi / 2, None, ALU.add))
                    step(nc.vector.tensor_scalar(k, k, 3.1415925, -3.1415925, ALU.min, ALU.max))
                nc.vector.memset(V.pw[0][:, 0, :], 1.0)
                nc.vector.memset(V.pw[1][:, 0, :], 0.0).then_inc(s.a_sin, 1)
                dve.wait_ge(s.a_out, 4)
                nc.vector.tensor_tensor(V.pw[0][:, 1, :], mag, cs, ALU.mult)
                step(nc.vector.tensor_tensor(V.pw[1][:, 1, :], mag, sn, ALU.mult))
                pw = lambda a, b: tuple(v[:, a:b, :] for v in V.pw)
                one = lambda a, n: tuple(v[:, a:a + 1, :].broadcast_to([P, n, DT]) for v in V.pw)
                tmp = big[:, 0:4 * DT].rearrange("p (k n) -> p k n", n=DT)
                complex_times(step, nc, pw(2, 3), pw(1, 2), pw(1, 2), tmp[:, 0:1, :])
                complex_times(step, nc, pw(3, 5), pw(1, 3), one(2, 2), tmp[:, 0:2, :])
                complex_times(step, nc, pw(5, 9), pw(1, 5), one(4, 4), tmp)
                step(nc.vector.tensor_scalar(a1, V.pw[0][:, 1, :], -1.0, None, ALU.add))
                nc.vector.tensor_tensor(w1, are, are, ALU.mult)
                step(nc.vector.tensor_tensor(w2, aim, aim, ALU.mult))
                step(nc.vector.tensor_tensor(w1, w1, w2, ALU.add))
                step(nc.vector.reciprocal(w1, w1))
                step(nc.vector.tensor_tensor(w2, are, w1, ALU.mult))
                step(nc.vector.tensor_tensor(w3, aim, w1, ALU.mult))
                step(nc.vector.tensor_scalar(w3, w3, -1.0, None, ALU.mult))
                complex_times(step, nc, (q_re, q_im), (a1, V.pw[1][:, 1, :]), (w2, w3), n1)
                dve.wait_ge(s.in_b, 32)
                for d in range(2):
                    cut = slice(d * KT, (d + 1) * KT)
                    qb = tuple(v[:, cut].unsqueeze(2).broadcast_to([P, KT, S5P]) for v in (q_re, q_im))
                    complex_times(step, nc, tuple(v[:, cut, :] for v in V.bb), qb, br,
                                  big[:, 0:KT * S5P].rearrange("p (t q) -> p t q", q=S5P))
                dve.wait_ge(s.turned, 2)
                for n in range(2):
                    c = nc.vector.tensor_copy(cT[n], pt[:, 256 + n * P:256 + (n + 1) * P].rearrange(
                        "p (t q) -> p t q", q=S5P))
                step(c)
                for d in range(2):
                    for k in range(9):
                        r = k if d == 0 else 8 - k
                        cut = slice(d * KT, (d + 1) * KT)
                        out = tuple(v[:, cut, r * S5P:(r + 1) * S5P] for v in V.ca)
                        pk = tuple(v[:, k, cut].unsqueeze(2).broadcast_to([P, KT, S5P]) for v in V.pw)
                        t = big[:, 0:KT * S5P].rearrange("p (t q) -> p t q", q=S5P)
                        complex_times(step, nc, out, cT, pk, t)
                step(nc.vector.tensor_scalar(V.ca[1], V.ca[1], -1.0, None, ALU.mult))
                nc.vector.tensor_scalar(V.ca[0], V.ca[0], 1.0, None, ALU.mult).then_inc(s.ca, 1)
                for d in range(2):
                    for j in range(S5L):
                        k = 7 - j if d == 0 else j
                        cut = slice(d * KT, (d + 1) * KT)
                        out = tuple(v[:, cut, j * S5P:(j + 1) * S5P] for v in V.wv)
                        pk = tuple(v[:, k, cut].unsqueeze(2).broadcast_to([P, KT, S5P]) for v in V.pw)
                        t = big[:, 0:KT * S5P].rearrange("p (t q) -> p t q", q=S5P)
                        complex_times(step, nc, out, tuple(v[:, cut, :] for v in V.bb), pk, t)
                nc.vector.memset(w4, 0.0).then_inc(s.wv, 1)
                complex_times(step, nc, (v_re, v_im), (cs, sn), (cs, sn), w1)
                complex_times(step, nc, (u_re, u_im), (v_re, v_im), (v_re, v_im), w1)
                complex_times(step, nc, (v_re, v_im), (u_re, u_im), (u_re, u_im), w1)
                nc.vector.tensor_tensor(w1, v_re, v_re, ALU.mult)
                step(nc.vector.tensor_tensor(w2, v_im, v_im, ALU.mult))
                step(nc.vector.tensor_tensor(w1, w1, w2, ALU.add))
                step(nc.vector.tensor_scalar(w1, w1, -0.5, 1.5, ALU.mult, ALU.add))
                nc.vector.tensor_tensor(u_re, v_re, w1, ALU.mult)
                step(nc.vector.tensor_tensor(u_im, v_im, w1, ALU.mult))
                for d in range(2):
                    for b in range(4):
                        dve.wait_ge(s.mm, 4 * d + b + 1)
                        g0 = 8 * (b // 2) + b % 2
                        nc.vector.tensor_copy(V.T[d][0:16, g0:g0 + 7:2, :],
                                              pT[0:16, b, :].rearrange("p (g n) -> p g n", g=4))\
                            .then_inc((s.T0, s.T1)[d], 1)
                for n in range(8):
                    dve.wait_ge(s.wvd, n + 1)
                    ri, q = n // 4, n % 4
                    nc.vector.tensor_copy(V.wvT[ri][:, 4 * q:4 * q + 4, :],
                                          pw_ps[:, n % 2, :].rearrange("p (t n) -> p t n", t=4)).then_inc(s.tc, 1)
                dve.wait_ge(s.shift, 16 * S5L)
                dve.wait_ge(s.shift2, 16 * S5L)
                dve.wait_ge(s.turned, 3)
                nc.vector.tensor_copy(dcol, pt[:, 64:64 + S5G])
                step(nc.vector.tensor_tensor(V.K, V.K, V.Kb, ALU.add))
                for g in range(S5G):
                    nc.vector.scalar_tensor_tensor(out=V.K[:, g, :], in0=S.ident, scalar=dcol[:, g:g + 1],
                                                   in1=V.K[:, g, :], op0=ALU.mult, op1=ALU.add)

            @block.tensor
            def _(pe):
                pe.wait_ge(s.in_a, 32)
                for n in range(2):
                    t = pe.transpose(pt[:, DT * n:DT * (n + 1)], arow[n], S.ident[0:DT, 0:DT])
                t.then_inc(s.turned, 1)
                pe.wait_ge(s.in_c, 16 * 2 * KT)
                pe.wait_ge(s.dve, 1)
                for n in range(2):
                    t = pe.transpose(pt[:, 256 + n * P:256 + (n + 1) * P], crow[n], S.ident)
                t.then_inc(s.turned, 1)
                pe.wait_ge(s.ca, 1)
                pe.wait_ge(s.in_d, 16)
                pe.transpose(pt[:, 64:64 + S5G], drow.rearrange("g j p -> g (j p)"),
                             S.ident[0:S5G, 0:S5G]).then_inc(s.turned, 1)
                for d in range(2):
                    for b in range(4):
                        if d:
                            pe.wait_ge(s.T0, b + 1)
                        for i in range(4):
                            g = 8 * (b // 2) + 2 * i + b % 2
                            part, t = slice(64 * (g % 2), 64 * (g % 2) + 64), d * KT + g // 2
                            o = pT[0:16, b, i * P:(i + 1) * P]
                            first = 0 if d == 0 else 1
                            for ri in range(2):
                                mm = pe.matmul(o, V.bb[ri][part, t, :],
                                               V.ca[ri][part, t, first * S5P:first * S5P + P],
                                               start=(ri == 0), stop=(ri == 1))
                        mm.then_inc(s.mm, 1)
                pe.wait_ge(s.wv, 1)
                for n in range(8):
                    ri, q = n // 4, n % 4
                    if n >= 2:
                        pe.wait_ge(s.tc, n - 1)
                    for i in range(4):
                        t = pe.transpose(pw_ps[:, n % 2, i * P:(i + 1) * P], V.wv[ri][:, 4 * q + i, :], S.ident)
                    t.then_inc(s.wvd, 1)


def stage_s5(nc, I, S):
    V = s5_views(S)
    A = S.arena
    DT = 2 * KT
    NS = S5CC + S5C
    r8, (u_re, u_im) = S.s5_r8, S.s5_u
    g_re, g_im, w1, w2 = (A.view(H0 + 6 * T + i * NS, NS) for i in range(4))
    lv = A.view(H0 + 6 * T + 4 * NS, 2, DT)
    lw = A.view(H0 + 6 * T + 4 * NS + 2 * DT, 2, DT)
    big = A.view(H0, DT, 64)
    with memory(S) as ctx:
        s = semaphores(nc, S, ctx, "s6", "dve turned ut v scanned out gelu turned2 table free")
        pu = psum(nc, ctx, "s6_u", 2, PSB)
        pv = psum(nc, ctx, "s6_v", 2, PSB)
        po = psum(nc, ctx, "s6_o", 4, PSB)
        with block_of(nc, S) as block:
            @block.tensor
            def _(pe):
                for g in range(S5G):
                    if g >= 2:
                        pe.wait_ge(s.ut, g - 1)
                    pe.transpose(pu[:, g % 2, 0:S5C], S.u5[:, g, :, :].rearrange("c j p -> c (j p)"), S.ident)
                    pe.transpose(pu[:, g % 2, S5C:NS], S.u5c[0:S5CC, g, :, :].rearrange("c j p -> c (j p)"),
                                 S.ident[0:S5CC, 0:S5CC]).then_inc(s.turned, 1)
                pe.wait_ge(s.ut, S5G)
                for n in range(DT):
                    d, t = n // KT, n % KT
                    if n >= 2:
                        pe.wait_ge(s.scanned, n - 1)
                    for ri in range(2):
                        for e in range(2):
                            g = 2 * t + e
                            mm = pe.matmul(pv[64 * e:64 * e + 64, n % 2, ri * NS:(ri + 1) * NS],
                                           V.wvT[ri][:, n, 64 * e:64 * e + 64],
                                           V.UT[:, g, S5CC * d:S5CC * d + NS], start=True, stop=True)
                    mm.then_inc(s.v, 1)
                pe.wait_ge(s.table, 1)
                for b in range(4):
                    for i in range(4):
                        g = 8 * (b // 2) + 2 * i + b % 2
                        o = po[:, b, i * P:(i + 1) * P]
                        part = slice(64 * (g % 2), 64 * (g % 2) + 64)
                        pe.matmul(o, V.UT[:, g, S5CC:NS], V.K[:, g, :], start=True, stop=False)
                        for d in range(2):
                            t = d * KT + g // 2
                            first = S5P if d == 0 else 0
                            c0 = S5CC - 1 if d == 0 else 1
                            for ri in range(2):
                                mm = pe.matmul(o, V.st[ri][part, t, c0:c0 + S5C],
                                               V.ca[ri][part, t, first:first + P], start=False,
                                               stop=(d == 1 and ri == 1))
                    mm.then_inc(s.out, 1)
                pe.wait_ge(s.gelu, 4)
                for j in range(S5L):
                    if j >= 2:
                        pe.wait_ge(s.free, j - 1)
                    for c in range(2):
                        t = pe.transpose(pu[:, j % 2, c * P:(c + 1) * P], V.yc[:, j, c * P:(c + 1) * P], S.ident)
                    t.then_inc(s.turned2, 1)

            @block.scalar
            def _(act):
                for b in range(4):
                    act.wait_ge(s.out, b + 1)
                    g0 = 8 * (b // 2) + b % 2
                    nc.scalar.activation(
                        V.yc.rearrange("c j (g p) -> c g j p", g=S5G)[:, g0:g0 + 7:2, :, :],
                        po[:, b, :].rearrange("c (g j p) -> c g j p", g=4, j=S5L),
                        ACT.Gelu_apprx_tanh).then_inc(s.gelu, 1)

            @block.vector
            def _(dve):
                step = Chain(dve, s.dve)
                for g in range(S5G):
                    dve.wait_ge(s.turned, g + 1)
                    nc.vector.tensor_copy(V.UT[:, g, S5CC:S5CC + NS], pu[:, g % 2, 0:NS])
                    nc.vector.tensor_copy(V.UT[:, g, 0:S5CC], pu[:, g % 2, S5C:NS]).then_inc(s.ut, 1)
                tr, ti = V.tab
                nc.vector.memset(tr[:, :, 0:1], 1.0)
                nc.vector.memset(ti[:, :, 0:1], 0.0)
                nc.vector.tensor_copy(tr[:, :, 1:2], u_re.unsqueeze(2))
                nc.vector.tensor_scalar(ti[:, :, 1:2], u_im.unsqueeze(2), -1.0, None, ALU.mult)
                step(nc.vector.tensor_copy(lv[:, 0, :], u_re))
                step(nc.vector.tensor_scalar(lv[:, 1, :], u_im, -1.0, None, ALU.mult))
                n = 2
                a, b = lv, lw
                while n < NS:
                    complex_times(step, nc, (b[:, 0, :], b[:, 1, :]), (a[:, 0, :], a[:, 1, :]),
                                  (a[:, 0, :], a[:, 1, :]), g_re[:, 0:DT])
                    a, b = b, a
                    for c0 in range(0, min(n, NS - n), 64):
                        m = min(n - c0, NS - n - c0, 64)
                        up = tuple(a[:, ri, :].unsqueeze(2).broadcast_to([P, DT, m]) for ri in range(2))
                        complex_times(step, nc, tuple(v[:, :, n + c0:n + c0 + m] for v in V.tab),
                                      tuple(v[:, :, c0:c0 + m] for v in V.tab), up, big[:, :, 0:m])
                    n *= 2
                for n in range(DT):
                    d = n // KT
                    way = slice(None) if d == 0 else slice(None, None, -1)
                    tre, tim = tr[:, n, :][:, way], ti[:, n, :][:, way]
                    v_re, v_im = pv[:, n % 2, 0:NS], pv[:, n % 2, NS:2 * NS]
                    dve.wait_ge(s.v, n + 1)
                    nc.vector.tensor_tensor(w1, v_im, tim, ALU.mult)
                    nc.vector.tensor_tensor(w2, v_im, tre, ALU.mult)
                    nc.vector.tensor_tensor(g_re, v_re, tre, ALU.mult)
                    nc.vector.tensor_tensor(g_im, v_re, tim, ALU.mult).then_inc(s.scanned, 1)
                    dve.wait_ge(s.scanned, n + 1)
                    nc.vector.tensor_tensor(g_re, g_re, w1, ALU.subtract)
                    step(nc.vector.tensor_tensor(g_im, g_im, w2, ALU.add))
                    rate = r8[:, n:n + 1].broadcast_to([P, NS])
                    for g in (g_re, g_im):
                        c = nc.vector.tensor_tensor_scan(g[:, way], rate, g[:, way], 0.0, ALU.mult, ALU.add)
                    step(c)
                    nc.vector.tensor_tensor(w1, g_im, tim, ALU.mult)
                    nc.vector.tensor_tensor(w2, g_re, tim, ALU.mult)
                    nc.vector.tensor_tensor(V.st[0][:, n, :], g_re, tre, ALU.mult)
                    step(nc.vector.tensor_tensor(V.st[1][:, n, :], g_im, tre, ALU.mult))
                    nc.vector.tensor_tensor(V.st[0][:, n, :], V.st[0][:, n, :], w1, ALU.add)
                    step(nc.vector.tensor_tensor(V.st[1][:, n, :], V.st[1][:, n, :], w2, ALU.subtract))
                nc.vector.memset(lv[:, 0, 0:1], 0.0).then_inc(s.table, 1)
                ys = V.ys.rearrange("p c (k j) -> p c k j", j=S5L)
                for j in range(S5L):
                    dve.wait_ge(s.turned2, j + 1)
                    nc.vector.tensor_copy(ys[:, :, :, j], pu[:, j % 2, 0:256].rearrange("p (c k) -> p c k", c=2))\
                        .then_inc(s.free, 1)


def stage_s5_glu(nc, I, S):
    V = s5_views(S)
    A = S.arena
    gw = A.view(WR0, 2, W_MIX)
    sig = A.view(WR0 + 512, 2, T)
    with memory(S) as ctx:
        s = semaphores(nc, S, ctx, "s7", "w done sig")
        ps = psum(nc, ctx, "s7_ps", 4, PSB)
        with block_of(nc, S) as block:
            @block.sync
            def _(sp):
                sp.dma_start(gw, I["s5_glu_w"].rearrange("l (k p) n -> p (l k) n", p=P)).then_inc(s.w, 16)

            @block.tensor
            def _(pe):
                pe.wait_ge(s.w, 16)
                for n in range(4):
                    m, h = n // 2, n % 2
                    for k in range(2):
                        mm = pe.matmul(ps[:, n, :], gw[:, k, m * P:(m + 1) * P], V.ys[:, k, h * HALF:(h + 1) * HALF],
                                       start=(k == 0), stop=(k == 1))
                    mm.then_inc(s.done, 1)

            @block.scalar
            def _(act):
                for n in range(4):
                    m, h = n // 2, n % 2
                    act.wait_ge(s.done, n + 1)
                    nc.scalar.activation(sig[:, m, h * HALF:(h + 1) * HALF], ps[:, n, :], ACT.Sigmoid,
                                         bias=col(S, "s5_glu_b", m)).then_inc(s.sig, 1)

            @block.vector
            def _(dve):
                for m in range(2):
                    dve.wait_ge(s.sig, 2 * m + 2)
                    nc.vector.tensor_tensor(S.yT[:, 6 + m, :], V.ys[:, m, :], sig[:, m, :], ALU.mult)



def copy_stage(nc, S, name, dst, src):
    with memory(S) as ctx:
        s = semaphores(nc, S, ctx, name, "copied")
        with block_of(nc, S) as block:
            @block.sync
            def _(sp):
                sp.dma_start(dst, src).then_inc(s.copied, 16)
                sp.wait_ge(s.copied, 16)


def stage_keep_x(nc, I, S):
    copy_stage(nc, S, "keep", S.kept[0], S.arena.view(X0, TILE8))


def stage_back_x(nc, I, S):
    copy_stage(nc, S, "back", S.arena.view(X0, TILE8), S.kept[0])


def stage_w_out_1(nc, I, S):
    r = S.arena.view(Z0, KT, T)
    w = I["w_out"].rearrange("l (k p) n -> p (l k) n", p=P)

    def evac(dve, bank, m, h):
        cut = slice(h * HALF, (h + 1) * HALF)
        return dve.scalar_tensor_tensor(out=r[:, m, cut], in0=bank, scalar=S.mod[:, m + 16, 0:1],
                                        in1=S.xT[:, m, cut], op0=ALU.mult, op1=ALU.add)

    dn = dense(nc, S, "wo", lambda m: w[:, :, bass.ts(m, P)], KT, KT, lambda k: S.yT[:, k, :], T, evac, Z0 + TILE8,
               evac_engine="vector", banks=4)
    with memory(S) as ctx:
        s = semaphores(nc, S, ctx, "kx", "x sent")

        def final(act, k, h, cut):
            nc.scalar.activation(S.hT[:, k, cut], r[:, k, cut], ACT.Identity, bias=S.h_b[:, k:k + 1],
                                 scale=S.h_w[:, k:k + 1])

        def final_x(k, h, cut):
            nc.vector.tensor_scalar(S.xT[:, k, cut], r[:, k, cut], S.x_w[:, k:k + 1], S.x_b[:, k:k + 1], ALU.mult,
                                    ALU.add).then_inc(s.x, 1)

        tmp = S.arena.view(Z0 + TILE8, KT, T)
        rs = S.arena.view(Z0 + 2 * TILE8, T)
        normalize(nc, S, "n1", lambda k: r[:, k, :], KT, D, LN_EPS, True, lambda k: tmp[:, k, :], rs, final,
                  source=(dn.bank_free, 4 + 2 * KT), final_dve=final_x)
        with block_of(nc, S) as block:
            @block.sync
            def _(sp):
                for h in range(2):
                    cut = slice(h * HALF, (h + 1) * HALF)
                    sp.wait_ge(s.x, KT * (h + 1))
                    sp.dma_start(S.kept[0].rearrange("p (k t) -> p k t", t=T)[:, :, cut], S.xT[:, :, cut])\
                        .then_inc(s.sent, 16)
                sp.wait_ge(s.sent, 32)


FR = mybir.dt.float32r
KH = FT // 2
PIECES_IN, PIECES_OUT = 2 * FT, 2 * KT
PIECES = PIECES_IN + PIECES_OUT


def ffn_memory(nc, ctx, S):
    E = ctx.enter_context
    S.h_part = E(nc.sbuf_tensor("h_part", [P, 2, KT, HALF], FR))
    S.hid_part = E(nc.sbuf_tensor("hid_part", [P, 2, FT, HALF], FR))
    S.w_part = E(nc.sbuf_tensor("w_part", [P, 2, 2, KH, P], FR))
    S.w_raw = E(nc.sbuf_tensor("w_raw", [P, 2, KH, P], F32))
    S.gate = E(nc.sbuf_tensor("gate", [P, 2, HALF], F32))
    S.hid = E(nc.sbuf_tensor("hid", [P, 2, HALF], F32))
    S.x_in = E(nc.sbuf_tensor("x_in", [P, 2, HALF], F32))


def stage_ffn(nc, I, S):
    w_in = I["w_ffn_in"].rearrange("l (k p) n -> p (l k) n", p=P)
    w_out = I["w_ffn_out"].rearrange("l (k p) n -> p (l k) n", p=P)
    kept = S.kept[0].rearrange("p (k t) -> p k t", t=T)
    r = S.hT
    f32 = lambda v: v.bitcast(F32)
    with memory(S) as ctx:
        s = semaphores(nc, S, ctx, "ff", "raw0 raw1 x0 x1 h_hi h_lo hi lo used silu mult hid_hi hid_lo out")
        raw, xs = (s.raw0, s.raw1), (s.x0, s.x1)
        pi = psum(nc, ctx, "ff_in", 4, PSB)
        po = psum(nc, ctx, "ff_out", 2, PSB)

        def pairs(engine, n, body):
            body(0, 0, True)
            body(1, 1, False)
            with engine.Fori(1, n // 2) as i:
                for q in range(2):
                    body(i * 2 + q, q, False)

        with block_of(nc, S) as block:
            @block.sync
            def _(sp):
                for half in range(2):
                    base = PIECES * half
                    with sp.Fori(0, FT // 2) as i:
                        for j in range(4):
                            sp.wait_ge(s.lo, i * 4 + (base + j + 1))
                            sp.dma_start(S.w_raw[:, j % 2, 0:KT, :],
                                         w_in[:, :, bass.ds(i * (2 * P) + (j // 2 * P + j % 2 * D_FF), P)])\
                                .then_inc(raw[j % 2], 16)
                    with sp.Fori(0, KT // 2) as i:
                        for j in range(4):
                            sp.wait_ge(s.lo, i * 4 + (base + PIECES_IN + j + 1))
                            sp.dma_start(S.w_raw[:, j % 2, :, :],
                                         w_out[:, j % 2 * KH:(j % 2 + 1) * KH, bass.ds(i * (2 * P) + j // 2 * P, P)])\
                                .then_inc(raw[j % 2], 16)
                            if j % 2:
                                q = j // 2
                                sp.wait_ge(s.out, i * 2 + (KT * half + q + 1))
                                sp.dma_start(S.x_in[:, q, :], kept[:, bass.ds(i * 2 + q, 1),
                                                                   half * HALF:(half + 1) * HALF]
                                             .rearrange("p a t -> p (a t)")).then_inc(xs[q], 16)

            @block.tensor
            def _(pe):
                pe.sem_inc(s.used, 2)

                def three(bank, slot, kt, moving, first, last):
                    for k in range(kt):
                        for n, (a, b) in enumerate(((0, 0), (0, 1), (1, 0))):
                            mm = pe.matmul(bank, S.w_part[:, slot, a, k, :], moving(b, k),
                                           start=(first and k == 0 and n == 0),
                                           stop=(last and k == kt - 1 and n == 2))
                    mm.then_inc(s.used, 1)

                for half in range(2):
                    base = PIECES * half
                    pe.wait_ge(s.h_lo, KT * (half + 1))
                    with pe.Fori(0, FT // 2) as i:
                        for j in range(4):
                            pe.wait_ge(s.lo, i * 4 + (base + j + 3))
                            pe.wait_ge(s.mult, i * 2 + (FT * half + j // 2 + 1))
                            three(pi[:, j, :], j % 2, KT, lambda b, k: S.h_part[:, b, k, :], True, True)
                    pe.wait_ge(s.hid_lo, FT * (half + 1))
                    with pe.Fori(0, KT // 2) as i:
                        for j in range(4):
                            pe.wait_ge(s.lo, i * 4 + (base + PIECES_IN + j + 3))
                            pe.wait_ge(s.out, i * 2 + (KT * half + j // 2 + 1))
                            three(po[:, j // 2, :], j % 2, KH, lambda b, k: S.hid_part[:, b, j % 2 * KH + k, :],
                                  j % 2 == 0, j % 2 == 1)

            @block.scalar
            def _(act):
                for half in range(2):
                    base = PIECES * half
                    cut = slice(half * HALF, (half + 1) * HALF)
                    if half:
                        act.wait_ge(s.used, PIECES_IN + 2)
                    for k in range(KT):
                        nc.scalar.activation(S.h_part[:, 0, k, :], S.hT[:, k, cut], ACT.Copy).then_inc(s.h_hi, 1)

                    def hi(n, slot, kt):
                        act.wait_ge(raw[slot], (n - slot) * 8 + (base * 8 + 16))
                        act.wait_ge(s.used, n + (base + 1))
                        nc.scalar.activation(S.w_part[:, slot, 0, 0:kt, :], S.w_raw[:, slot, 0:kt, :], ACT.Copy)\
                            .then_inc(s.hi, 1)

                    def silu(p, q):
                        act.wait_ge(s.used, p * 2 + (base + 3))
                        act.wait_ge(s.mult, p + (FT * half + 1))
                        nc.scalar.activation(S.gate[:, q, :], pi[:, 2 * q, :], ACT.Silu).then_inc(s.silu, 1)

                    def hid_hi(p, q):
                        act.wait_ge(s.mult, p + (FT * half + 3))
                        nc.scalar.activation(S.hid_part[:, 0, p, :], S.hid[:, q, :], ACT.Copy).then_inc(s.hid_hi, 1)

                    def step_in(p, q, first):
                        hi(p * 2, 0, KT)
                        if not first:
                            silu(p - 1, 1 - q)
                        hi(p * 2 + 1, 1, KT)
                        if not first:
                            hid_hi(p - 1, 1 - q)
                    pairs(act, FT, step_in)
                    hi(PIECES_IN, 0, KH)
                    silu(FT - 1, 1)
                    hid_hi(FT - 1, 1)
                    hi(PIECES_IN + 1, 1, KH)

                    def step_out(m, q, first):
                        if not first:
                            hi(m * 2 + PIECES_IN, 0, KH)
                            hi(m * 2 + (PIECES_IN + 1), 1, KH)
                    pairs(act, KT, step_out)

            @block.vector
            def _(dve):
                dve.sem_inc(s.lo, 2)
                dve.sem_inc(s.mult, 2)
                dve.sem_inc(s.out, 2)
                for half in range(2):
                    base = PIECES * half
                    cut = slice(half * HALF, (half + 1) * HALF)
                    for k in range(KT):
                        dve.wait_ge(s.h_hi, KT * half + k + 1)
                        nc.vector.tensor_tensor(S.h_part[:, 1, k, :], S.hT[:, k, cut], f32(S.h_part[:, 0, k, :]),
                                                ALU.subtract).then_inc(s.h_lo, 1)

                    def lo(n, slot, kt):
                        dve.wait_ge(s.hi, n + (base + 1))
                        nc.vector.tensor_tensor(S.w_part[:, slot, 1, 0:kt, :], S.w_raw[:, slot, 0:kt, :],
                                                f32(S.w_part[:, slot, 0, 0:kt, :]), ALU.subtract).then_inc(s.lo, 1)

                    def mult(p, q):
                        dve.wait_ge(s.silu, p + (FT * half + 1))
                        dve.wait_ge(s.used, p * 2 + (base + 4))
                        nc.vector.tensor_tensor(S.hid[:, q, :], S.gate[:, q, :], pi[:, 2 * q + 1, :], ALU.mult)\
                            .then_inc(s.mult, 1)

                    def hid_lo(p, q):
                        dve.wait_ge(s.hid_hi, p + (FT * half + 1))
                        nc.vector.tensor_tensor(S.hid_part[:, 1, p, :], S.hid[:, q, :], f32(S.hid_part[:, 0, p, :]),
                                                ALU.subtract).then_inc(s.hid_lo, 1)

                    def out(m, q):
                        dve.wait_ge(xs[q], (m - q) * 8 + (KT * half * 8 + 16))
                        dve.wait_ge(s.used, m * 2 + (base + PIECES_IN + 4))
                        nc.vector.scalar_tensor_tensor(out=r[:, m, cut], in0=po[:, q, :],
                                                       scalar=S.mod[:, m + 40, 0:1], in1=S.x_in[:, q, :],
                                                       op0=ALU.mult, op1=ALU.add).then_inc(s.out, 1)

                    def step_in(p, q, first):
                        lo(p * 2, 0, KT)
                        if not first:
                            mult(p - 1, 1 - q)
                        lo(p * 2 + 1, 1, KT)
                        if not first:
                            hid_lo(p - 1, 1 - q)
                    pairs(dve, FT, step_in)
                    lo(PIECES_IN, 0, KH)
                    mult(FT - 1, 1)
                    hid_lo(FT - 1, 1)
                    lo(PIECES_IN + 1, 1, KH)

                    def step_out(m, q, first):
                        if not first:
                            lo(m * 2 + PIECES_IN, 0, KH)
                            out(m - 1, 1 - q)
                            lo(m * 2 + (PIECES_IN + 1), 1, KH)
                    pairs(dve, KT, step_out)
                    out(KT - 1, 1)


def stage_norm_2(nc, I, S):
    r = S.hT

    def final(act, k, h, cut):
        nc.scalar.activation(S.xT[:, k, cut], r[:, k, cut], ACT.Identity, bias=col(S, "ln2_b", k),
                             scale=col(S, "ln2_w", k))

    tmp = S.arena.view(Z0, KT, T)
    rs = S.arena.view(Z0 + TILE8, T)
    normalize(nc, S, "n2", lambda k: r[:, k, :], KT, D, LN_EPS, True, lambda k: tmp[:, k, :], rs, final)


MA0, ML0 = X0, X0 + 4 * T
QK0 = Z0
ZA0 = QK0 + 8 * T
VB0 = ZA0 + 4 * T
FD0 = VB0 + NT * ATT_W
FX0 = FD0 + 256


def stage_rms(nc, I, S):
    def final(act, k, h, cut):
        nc.scalar.activation(S.hT[:, k, cut], S.xT[:, k, cut], ACT.Copy, scale=col(S, "norm_g_2", k))

    tmp = S.arena.view(Z0, KT, T)
    rs = S.arena.view(Z0 + TILE8, T)
    with memory(S) as ctx:
        s = semaphores(nc, S, ctx, "keep2", "kept")
        with block_of(nc, S) as block:
            @block.sync
            def _(sp):
                sp.dma_start(S.kept[1], S.arena.view(X0, TILE8)).then_inc(s.kept, 16)
                sp.wait_ge(s.kept, 16)
    normalize(nc, S, "n3", lambda k: S.xT[:, k, :], KT, D, EPS, False, lambda k: tmp[:, k, :], rs, final,
              scale_after=(s.kept, 16))


def stage_forget(nc, I, S):
    A = S.arena
    w = I["w_in_2"].rearrange("l (k p) n -> p (l k) n", p=P)
    R = ATT_H + SSD_H
    wf = A.view(FX0 + 12 * T, KT, R)
    fd = A.view(X0, T)[0:R, :]
    f = fd[0:ATT_H, :]
    e, ln, ww = (A.view(X0 + i * T, T)[0:ATT_H, :] for i in range(1, 4))
    fb = A.view(X0 + 4 * T, 1)[0:ATT_H, :]
    tok = A.view(FD0, NT, R)
    with memory(S) as ctx:
        s = semaphores(nc, S, ctx, "fg", "w bias done rows turned dve act exped")
        ps = psum(nc, ctx, "fg_ps", 2, PSB)
        with block_of(nc, S) as block:
            @block.sync
            def _(sp):
                sp.dma_start(wf[:, :, 0:ATT_H], w[:, :, F_OFF:F_OFF + ATT_H]).then_inc(s.w, 16)
                sp.dma_start(wf[:, :, ATT_H:], w[:, :, DT_OFF:DT_OFF + SSD_H]).then_inc(s.w, 16)
                sp.dma_start(fb, I["forget_b_2"].rearrange("l h -> h l")).then_inc(s.bias, 16)

            @block.tensor
            def _(pe):
                pe.wait_ge(s.w, 32)
                for h in range(2):
                    for k in range(KT):
                        mm = pe.matmul(ps[0:R, h, :], wf[:, k, :], S.hT[:, k, h * HALF:(h + 1) * HALF],
                                       start=(k == 0), stop=(k == KT - 1))
                    mm.then_inc(s.done, 1)
                pe.wait_ge(s.rows, 2)
                for i in range(NT):
                    t = pe.transpose(ps[:, 0, R * i:R * i + R], fd[:, i * P:(i + 1) * P], S.ident[0:R, 0:R])
                t.then_inc(s.turned, 1)

            @block.scalar
            def _(act):
                for h in range(2):
                    act.wait_ge(s.done, h + 1)
                    nc.scalar.activation(fd[:, h * HALF:(h + 1) * HALF], ps[0:R, h, :], ACT.Copy).then_inc(s.rows, 1)
                act.wait_ge(s.act, 1)
                nc.scalar.activation(e, e, ACT.Exp).then_inc(s.exped, 1)
                act.wait_ge(s.exped, 1)
                nc.scalar.activation(ln, e, ACT.Ln, bias=1.0).then_inc(s.exped, 1)

            @block.vector
            def _(dve):
                step = Chain(dve, s.dve)
                dve.wait_ge(s.turned, 1)
                nc.vector.tensor_copy(tok, ps[:, 0, 0:NT * R].rearrange("p (i n) -> p i n", n=R))
                dve.wait_ge(s.bias, 16)
                step(nc.vector.tensor_scalar(f, f, fb, None, ALU.add))
                step(nc.vector.tensor_scalar(ww, f, -1.0, None, ALU.mult))
                nc.vector.tensor_tensor(e, ww, f, ALU.min).then_inc(s.act, 1)
                dve.wait_ge(s.exped, 2)
                log1p_tail(step, nc, e, ln, ww, ww)
                step(nc.vector.tensor_scalar(f, f, 0.0, None, ALU.min))
                step(nc.vector.tensor_tensor(ww, ww, f, ALU.subtract))
                step(nc.vector.memset(e, 1.0))
                nc.vector.tensor_tensor_scan(S.crow, e, ww, 0.0, ALU.mult, ALU.add)


def stage_project_att(nc, I, S):
    w = I["w_in_2"].rearrange("l (k p) n -> p (l k) n", p=P)
    first = [m * P for m in range(8)] + [ZA_OFF + m * P for m in range(4)]
    out = S.arena.view(QK0, 12, T)
    dense(nc, S, "pq", lambda m: w[:, :, first[m]:first[m] + P], 12, KT, lambda k: S.hT[:, k, :], T,
          lambda act, bank, m, h: act.activation(out[:, m, h * HALF:(h + 1) * HALF], bank,
                                                 ACT.Copy if m < 8 else ACT.Silu),
          FX0, irregular=True, banks=2)


def project_tokens(nc, S, name, w, parts, at, evac, banks=8, room=None):
    with memory(S) as ctx:
        s = semaphores(nc, S, ctx, name, "w0 w1 done free")
        ps = psum(nc, ctx, f"{name}_ps", banks, PSB)
        views = []
        for _, n in parts:
            views.append(S.arena.view(at, KT, n))
            at += KT * n
        jobs = [(i, q) for q in range(len(parts)) for i in range(NT)]
        with block_of(nc, S) as block:
            @block.sync
            def _(sp):
                for (off, n), v, loaded in zip(parts, views, (s.w0, s.w1)):
                    sp.dma_start(v, w[:, :, off:off + n]).then_inc(loaded, 16)

            @block.tensor
            def _(pe):
                for n, (i, q) in enumerate(jobs):
                    pe.wait_ge((s.w0, s.w1)[q], 16)
                    if n >= banks:
                        pe.wait_ge(s.free, n - banks + 1)
                    for k in range(KT):
                        mm = pe.matmul(ps[:, n % banks, 0:parts[q][1]], S.hT[:, k, i * P:(i + 1) * P],
                                       views[q][:, k, :], start=(k == 0), stop=(k == KT - 1))
                    mm.then_inc(s.done, 1)

            @block.scalar
            def _(act):
                if room:
                    act.wait_ge(*room)
                for n, (i, q) in enumerate(jobs):
                    act.wait_ge(s.done, n + 1)
                    evac(nc.scalar, ps[:, n % banks, 0:parts[q][1]], i, q).then_inc(s.free, 1)


def stage_att_values(nc, I, S):
    A = S.arena
    w = I["w_in_2"].rearrange("l (k p) n -> p (l k) n", p=P)
    qk = A.view(QK0, 8, T)
    v = A.view(VB0, NT, ATT_W)
    wv = A.view(FX0 + 4 * T, KT, ATT_W)
    sq = A.view(FX0 + 8 * T, 2, T)
    rs = A.view(FX0 + 10 * T, 2, T)
    gq = A.view(X0 + 5 * T, 1)
    with memory(S) as ctx:
        s = semaphores(nc, S, ctx, "av", "w done free squared mean eps root dve")
        ps = psum(nc, ctx, "av_ps", 2, PSB)
        pm = psum(nc, ctx, "av_m", 2, PSB)
        with block_of(nc, S) as block:
            @block.sync
            def _(sp):
                sp.dma_start(wv, w[:, :, V_OFF:V_OFF + ATT_W]).then_inc(s.w, 16)

            @block.scalar
            def _(act):
                def square(m):
                    if m >= 2:
                        act.wait_ge(s.mean, m - 1)
                    nc.scalar.activation(sq[:, m % 2, :], qk[:, m, :], ACT.Square).then_inc(s.squared, 1)

                square(0)
                for i in range(NT):
                    if i + 1 < NT:
                        square(i + 1)
                    act.wait_ge(s.done, i + 1)
                    nc.scalar.activation(v[:, i, :], ps[:, i % 2, :], ACT.Copy).then_inc(s.free, 1)
                    act.wait_ge(s.eps, i + 1)
                    nc.scalar.activation(rs[:, i % 2, :], rs[:, i % 2, :], ACT.Sqrt).then_inc(s.root, 1)

            @block.tensor
            def _(pe):
                pe.wait_ge(s.w, 16)
                for i in range(NT):
                    if i >= 2:
                        pe.wait_ge(s.free, i - 1)
                    for k in range(KT):
                        mm = pe.matmul(ps[:, i % 2, :], S.hT[:, k, i * P:(i + 1) * P], wv[:, k, :],
                                       start=(k == 0), stop=(k == KT - 1))
                    mm.then_inc(s.done, 1)
                    pe.wait_ge(s.squared, i + 1)
                    if i:
                        pe.wait_ge(s.eps, i)
                    for h in range(2):
                        mm = pe.matmul(pm[:, h, :], S.blk, sq[:, i % 2, h * HALF:(h + 1) * HALF],
                                       start=True, stop=True)
                    mm.then_inc(s.mean, 1)

            @block.vector
            def _(dve):
                step = Chain(dve, s.dve)
                step(nc.vector.tensor_scalar(gq, col(S, "q_norm_g_2"), ATT_HD ** -0.5, None, ALU.mult))
                for m in range(8):
                    dve.wait_ge(s.mean, m + 1)
                    nc.vector.tensor_scalar(rs[:, m % 2, :], pm[:, :, :].rearrange("p a b -> p (a b)"),
                                            EPS, None, ALU.add).then_inc(s.eps, 1)
                    dve.wait_ge(s.root, m + 1)
                    step(nc.vector.reciprocal(rs[:, m % 2, :], rs[:, m % 2, :]))
                    g = gq if m < 4 else col(S, "k_norm_g_2")
                    step(nc.vector.scalar_tensor_tensor(out=qk[:, m, :], in0=qk[:, m, :], scalar=g,
                                                        in1=rs[:, m % 2, :], op0=ALU.mult, op1=ALU.mult))


def stage_attention(nc, I, S):
    A = S.arena
    LS = 4
    qk = A.view(QK0, 8, T)
    v = A.view(VB0, NT, ATT_W)
    cb = A.view(FX0, 2, T)
    cd = A.view(FX0 + 2 * T, 2, T)
    y = A.view(FX0 + 4 * T, NT, ATT_W)
    PT = A.view(FX0 + 8 * T, 2, T)
    L = A.view(FX0 + 10 * T, LS, T)
    assert FX0 + (10 + LS) * T <= SIZE - 100
    mx = A.view(FX0 + (10 + LS) * T, LS, 2)
    nm = A.view(FX0 + (10 + LS) * T + 20, LS, 1)
    sm = A.view(FX0 + (10 + LS) * T + 40, LS, 1)
    units = [(h, i) for h in range(ATT_H) for i in range(NT)]
    with memory(S) as ctx:
        s = semaphores(nc, S, ctx, "at", "rows rowsc masked scores logits m exped turned copied pv out inv")
        pr = psum(nc, ctx, "at_s", 4, PSB)
        pt = psum(nc, ctx, "at_t", 2, PSB)
        po = psum(nc, ctx, "at_o", 2, PSB)
        with block_of(nc, S) as block:
            @block.tensor
            def _(pe):
                def row(h):
                    if h:
                        pe.wait_ge(s.copied, NT * h - 2)
                    for c in range(2):
                        mm = pe.matmul(pt[:, c, :], S.ident[0:ATT_H, h:h + 1].broadcast_to([ATT_H, P]),
                                       S.crow[:, c * HALF:(c + 1) * HALF], start=True, stop=True)
                    mm.then_inc(s.rows, 1)

                def scores(u):
                    h, i = units[u]
                    part = slice(64 * (h % 2), 64 * (h % 2) + 64)
                    if u >= 2:
                        pe.wait_ge(s.logits, u - 1)
                    n = (i + 1) * P
                    for c in range(0, n, HALF):
                        w = min(HALF, n - c)
                        mm = pe.matmul(pr[:, 2 * (u % 2) + c // HALF, 0:w], qk[part, h // 2, i * P:(i + 1) * P],
                                       qk[part, 4 + h // 2, c:c + w], start=True, stop=True)
                    mm.then_inc(s.scores, 1)

                def turn(u):
                    h, i = units[u]
                    pe.wait_ge(s.exped, u + 1)
                    if u:
                        pe.wait_ge(s.copied, u)
                    if i == NT - 2 and h + 1 < ATT_H or u == 0:
                        pe.wait_ge(s.rowsc, h + 2 if u else 1)
                    for b in range(i + 1):
                        t = pe.transpose(pt[:, b // 4, (b % 4) * P:(b % 4 + 1) * P], L[:, u % LS, b * P:(b + 1) * P],
                                         S.ident)
                    t.then_inc(s.turned, 1)

                def values(u):
                    h, i = units[u]
                    pe.wait_ge(s.copied, u + 1)
                    if u >= 2:
                        pe.wait_ge(s.out, u - 1)
                    for b in range(i + 1):
                        mm = pe.matmul(po[:, u % 2, 0:ATT_HD], PT[:, u % 2, b * P:(b + 1) * P],
                                       v[:, b, h * ATT_HD:(h + 1) * ATT_HD], start=(b == 0), stop=(b == i))
                    mm.then_inc(s.pv, 1)

                U = len(units)
                for u in range(U + 3):
                    if u < U:
                        if units[u][1] == 0:
                            row(units[u][0])
                        scores(u)
                    if 2 <= u < U + 2:
                        turn(u - 2)
                    if u >= 3:
                        values(u - 3)

            @block.scalar
            def _(act):
                def row(h):
                    act.wait_ge(s.rows, h + 1)
                    if h >= 2:
                        act.wait_ge(s.logits, NT * (h - 1))
                    nc.scalar.activation(cb[:, h % 2, :], pt[:, :, :].rearrange("p a b -> p (a b)"), ACT.Copy)\
                        .then_inc(s.rowsc, 1)

                def copy(u):
                    h, i = units[u]
                    act.wait_ge(s.turned, u + 1)
                    if u >= 2:
                        act.wait_ge(s.pv, u - 1)
                    n = (i + 1) * P
                    nc.scalar.activation(PT[:, u % 2, 0:n], pt[:, :, :].rearrange("p a b -> p (a b)")[:, 0:n],
                                         ACT.Copy).then_inc(s.copied, 1)

                for u, (h, i) in enumerate(units):
                    if i == 0:
                        row(h)
                    act.wait_ge(s.m, u + 1)
                    if u >= LS:
                        act.wait_ge(s.out, u - LS + 1)
                    n = (i + 1) * P
                    nc.scalar.activation(L[:, u % LS, 0:n], L[:, u % LS, 0:n], ACT.Exp, bias=nm[:, u % LS, :],
                                         accum_out=sm[:, u % LS, :]).then_inc(s.exped, 1)
                    if u >= 2:
                        copy(u - 2)
                copy(len(units) - 2)
                copy(len(units) - 1)

            @block.gpsimd
            def _(pool):
                for h in range(ATT_H):
                    pool.wait_ge(s.rowsc, h + 1)
                    if h >= 2:
                        pool.wait_ge(s.logits, NT * (h - 1))
                    pool.affine_select(out=cd[:, h % 2, :].rearrange("p (i s) -> p i s", s=P),
                                       in_=cb[:, h % 2, :].rearrange("p (i s) -> p i s", s=P),
                                       compare_op=ALU.is_ge, fill=-1e30, base=0, pattern=[[0, NT], [-1, P]],
                                       channel_multiplier=1).then_inc(s.masked, 1)

            @block.vector
            def _(dve):
                def finish(u):
                    h, i = units[u]
                    dve.wait_ge(s.exped, u + 1)
                    nc.vector.reciprocal(sm[:, u % LS, :], sm[:, u % LS, :]).then_inc(s.inv, 1)
                    dve.wait_ge(s.inv, u + 1)
                    dve.wait_ge(s.pv, u + 1)
                    nc.vector.tensor_scalar(y[:, i, h * ATT_HD:(h + 1) * ATT_HD], po[:, u % 2, 0:ATT_HD],
                                            sm[:, u % LS, :], None, ALU.mult).then_inc(s.out, 1)

                for u, (h, i) in enumerate(units):
                    dve.wait_ge(s.scores, u + 1)
                    dve.wait_ge(s.masked, h + 1)
                    if u >= LS:
                        dve.wait_ge(s.turned, u - LS + 1)
                    sc = pr[:, 2 * (u % 2):2 * (u % 2) + 2, :].rearrange("p a b -> p (a b)")
                    n = i * P
                    if i:
                        nc.vector.tensor_tensor_reduce(L[:, u % LS, 0:n], sc[:, 0:n], cb[:, h % 2, 0:n], 1.0, -3.0e38,
                                                       ALU.add, ALU.max, mx[:, u % LS, 0:1])
                    else:
                        nc.vector.memset(mx[:, u % LS, 0:1], -3.0e38)
                    nc.vector.tensor_tensor_reduce(L[:, u % LS, n:n + P], sc[:, n:n + P], cd[:, h % 2, n:n + P], 1.0,
                                                   -3.0e38, ALU.add, ALU.max, mx[:, u % LS, 1:2]).then_inc(s.logits, 1)
                    dve.wait_ge(s.logits, u + 1)
                    nc.vector.tensor_reduce(nm[:, u % LS, :], mx[:, u % LS, :], AX, ALU.max, negate=True)\
                        .then_inc(s.m, 1)
                    if u >= 3:
                        finish(u - 3)
                for u in range(len(units) - 3, len(units)):
                    finish(u)

    za = A.view(ZA0, 4, T)
    mix = A.view(MA0, 4, T)
    with memory(S) as ctx:
        s = semaphores(nc, S, ctx, "ao", "turned out")
        ps = psum(nc, ctx, "ao_ps", 8, PSB)
        with block_of(nc, S) as block:
            @block.tensor
            def _(pe):
                for n in range(8):
                    m, half = n // 2, n % 2
                    for i in range(4):
                        t = pe.transpose(ps[:, n, i * P:(i + 1) * P], y[:, 4 * half + i, m * P:(m + 1) * P], S.ident)
                    t.then_inc(s.turned, 1)

            @block.vector
            def _(dve):
                for n in range(8):
                    m, cut = n // 2, slice((n % 2) * HALF, (n % 2 + 1) * HALF)
                    dve.wait_ge(s.turned, n + 1)
                    nc.vector.tensor_tensor(mix[:, m, cut], ps[:, n, :], za[:, m, cut], ALU.mult)


def dense_conv(nc, S, name, weights, n_tiles, taps, bias, out, ring_at, pads_at, banks=8):
    pads = [S.arena.view(at, T + 4) for at in pads_at]
    with memory(S) as ctx:
        s = semaphores(nc, S, ctx, name, "w0 w1 w2 w3 bank_free done copied conv taps zero")
        slots = [S.arena.view(ring_at + i * KT * P, KT, P) for i in range(4)]
        loaded = [s.w0, s.w1, s.w2, s.w3]
        ps = psum(nc, ctx, f"{name}_ps", banks, PSB)
        with block_of(nc, S) as block:
            @block.sync
            def _(sp):
                for j in range(4):
                    sp.dma_start(slots[j], weights(j)).then_inc(loaded[j], 16)
                if n_tiles > 4:
                    with sp.Fori(1, n_tiles // 4) as i:
                        for j in range(4):
                            sp.wait_ge(s.done, i * 8 + (2 * j - 6))
                            sp.dma_start(slots[j], weights(i * 4 + j)).then_inc(loaded[j], 16)

            @block.tensor
            def _(pe):
                with pe.Fori(0, n_tiles // 4) as i:
                    for j in range(4):
                        pe.wait_ge(loaded[j], i * 16 + 16)
                        for h in range(2):
                            pe.wait_ge(s.bank_free, i * 8 + (2 * j + h + 1))
                            for k in range(KT):
                                mm = pe.matmul(ps[:, (2 * j + h) % banks, :], slots[j][:, k, :],
                                               S.hT[:, k, h * HALF:(h + 1) * HALF],
                                               start=(k == 0), stop=(k == KT - 1))
                            mm.then_inc(s.done, 1)

            @block.scalar
            def _(act):
                act.sem_inc(s.bank_free, banks)
                with act.Fori(0, n_tiles // 4) as i:
                    for j in range(4):
                        act.wait_ge(s.conv, i * 4 + (j + 1))
                        for h in range(2):
                            act.wait_ge(s.done, i * 8 + (2 * j + h + 1))
                            nc.scalar.activation(pads[j][:, 4 + h * HALF:4 + (h + 1) * HALF], ps[:, (2 * j + h) % banks, :],
                                                 ACT.Copy).then_inc(s.bank_free, 1)

            @block.vector
            def _(dve):
                for j in range(4):
                    nc.vector.memset(pads[j][:, 0:4], 0.0).then_inc(s.zero, 1)
                dve.wait_ge(s.zero, 4)
                dve.sem_inc(s.conv, 4)
                with dve.Fori(0, n_tiles // 4) as i:
                    for j in range(4):
                        m = i * 4 + j
                        dve.wait_ge(s.bank_free, i * 8 + (2 * j + 2 + banks))
                        o = out[:, m, :]
                        nc.vector.tensor_scalar(o, pads[j][:, 1:1 + T], taps(m, 0), bias(m), ALU.mult, ALU.add)\
                            .then_inc(s.taps, 1)
                        for w in range(1, TAPS):
                            dve.wait_ge(s.taps, i * 12 + (3 * j + w))
                            c = nc.vector.scalar_tensor_tensor(out=o, in0=pads[j][:, 1 + w:1 + w + T],
                                                               scalar=taps(m, w), in1=o, op0=ALU.mult, op1=ALU.add)
                            c.then_inc(s.taps if w < TAPS - 1 else s.conv, 1)
    return s


def taps_of(S, name, n_tiles):
    at, _ = COL[name]
    return lambda m, w: S.cols[:, bass.ds(m + (at + w * n_tiles), 1)]


def stage_lru(nc, I, S):
    A = S.arena
    w = I["w_in_2"].rearrange("l (k p) n -> p (l k) n", p=P)
    at = QK0
    xc, r, g, m2 = (A.view(at + i * 4 * T, 4, T) for i in range(4))
    assert at + 16 * T <= FD0
    z = A.view(FX0, 4, T)
    ring = FX0 + 4 * T
    bd = A.view(FX0 + 13 * T, 8, P)
    e, ln, ww, cl = (A.view(FX0 + 14 * T + i * 4, 4) for i in range(4))
    mix = A.view(ML0, 4, T)
    wz = A.view(ML0, KT, LRU_W)
    bat, _ = COL["lru_conv_b_2"]
    with memory(S) as ctx:
        s = semaphores(nc, S, ctx, "lr", "zero bd wz zmm z act exped rate dve mm gates sq a th root h")
        ps = psum(nc, ctx, "lr_ps", 2, PSB)
        pz = psum(nc, ctx, "lr_z", 4, PSB)
        with block_of(nc, S) as block:
            @block.scalar
            def _(act):
                act.dma_start(wz, w[:, :, ZL_OFF:ZL_OFF + LRU_W]).then_inc(s.wz, 16)

            @block.vector
            def _(dve):
                nc.vector.memset(bd, 0.0).then_inc(s.zero, 1)
        cv = dense_conv(nc, S, "lc", lambda m: w[:, :, bass.ds(m * P + XL_OFF, P)], 4, taps_of(S, "lru_conv_w_2", 4),
                        lambda m: S.cols[:, bass.ds(m + bat, 1)], xc, ring,
                        [ring + 4 * KT * P + j * (T + 4) for j in range(4)], banks=2)
        with block_of(nc, S) as block:
            @block.sync
            def _(sp):
                sp.wait_ge(s.zero, 1)
                for n, name in enumerate(("lru_w_a_2", "lru_w_x_2")):
                    for e2 in range(2):
                        sp.dma_start(bd[64 * e2:64 * e2 + 64, 4 * n:4 * n + 4, 64 * e2:64 * e2 + 64],
                                     I[name].rearrange("l (t e) d o -> e d (l t) o", e=2)[e2]).then_inc(s.bd, 16)

            @block.tensor
            def _(pe):
                pe.wait_ge(s.bd, 64)
                for n in range(16):
                    gate, m, h = n // 8, (n // 2) % 4, n % 2
                    if n < 8:
                        pe.wait_ge(cv.conv, 4 + m + 1)
                    if n >= 2:
                        pe.wait_ge(s.gates, n - 1)
                    pe.matmul(ps[:, n % 2, :], bd[:, 4 * gate + m, :], xc[:, m, h * HALF:(h + 1) * HALF],
                              start=True, stop=True).then_inc(s.mm, 1)
                pe.wait_ge(s.wz, 16)
                for n in range(8):
                    m, h = n // 2, n % 2
                    if n >= 4:
                        pe.wait_ge(s.z, n - 3)
                    for k in range(KT):
                        mm = pe.matmul(pz[:, n % 4, :], wz[:, k, m * P:(m + 1) * P], S.hT[:, k, h * HALF:(h + 1) * HALF],
                                       start=(k == 0), stop=(k == KT - 1))
                    mm.then_inc(s.zmm, 1)

            @block.scalar
            def _(act):
                def silu_z(m):
                    for n in (2 * m, 2 * m + 1):
                        act.wait_ge(s.zmm, n + 1)
                        nc.scalar.activation(z[:, m, (n % 2) * HALF:(n % 2 + 1) * HALF], pz[:, n % 4, :], ACT.Silu)\
                            .then_inc(s.z, 1)

                act.wait_ge(s.act, 1)
                nc.scalar.activation(e, e, ACT.Exp).then_inc(s.exped, 1)
                act.wait_ge(s.exped, 1)
                nc.scalar.activation(ln, e, ACT.Ln, bias=1.0).then_inc(s.exped, 1)
                for n in range(16):
                    gate, m, h = n // 8, (n // 2) % 4, n % 2
                    act.wait_ge(s.mm, n + 1)
                    nc.scalar.activation((r, g)[gate][:, m, h * HALF:(h + 1) * HALF], ps[:, n % 2, :], ACT.Sigmoid,
                                         bias=col(S, ("lru_b_a_2", "lru_b_x_2")[gate], m)).then_inc(s.gates, 1)
                act.wait_ge(s.rate, 1)
                act.wait_ge(s.gates, 16)
                for m in range(4):
                    nc.scalar.activation(m2[:, m, :], r[:, m, :], ACT.Tanh, scale=cl[:, m:m + 1]).then_inc(s.th, 1)
                silu_z(0)
                act.wait_ge(s.th, 4)
                act.wait_ge(s.act, 2)
                for m in range(4):
                    nc.scalar.activation(r[:, m, :], r[:, m, :], ACT.Exp, scale=cl[:, m:m + 1]).then_inc(s.a, 1)
                silu_z(1)
                for m in range(4):
                    act.wait_ge(s.sq, m + 1)
                    nc.scalar.activation(m2[:, m, :], m2[:, m, :], ACT.Sqrt).then_inc(s.root, 1)
                silu_z(2)
                silu_z(3)

            @block.vector
            def _(dve):
                step = Chain(dve, s.dve)
                lam = col(S, "lru_lambda_2", 0, 4)
                step(nc.vector.tensor_scalar(ww, lam, -1.0, None, ALU.mult))
                nc.vector.tensor_tensor(e, ww, lam, ALU.min).then_inc(s.act, 1)
                dve.wait_ge(s.exped, 2)
                log1p_tail(step, nc, e, ln, ww, ww)
                step(nc.vector.tensor_scalar(cl, lam, -1.0, 0.0, ALU.mult, ALU.max))
                step(nc.vector.tensor_tensor(cl, cl, ww, ALU.add))
                nc.vector.tensor_scalar(cl, cl, LRU_C, None, ALU.mult).then_inc(s.rate, 1)
                dve.wait_ge(s.th, 4)
                nc.vector.tensor_scalar(cl, cl, -1.0, None, ALU.mult).then_inc(s.act, 1)
                dve.wait_ge(s.gates, 16)
                for m in range(4):
                    k = nc.vector.tensor_tensor(g[:, m, :], g[:, m, :], xc[:, m, :], ALU.mult)
                step(k)
                for m in range(4):
                    dve.wait_ge(s.a, m + 1)
                    step(nc.vector.tensor_tensor(xc[:, m, :], r[:, m, :], r[:, m, :], ALU.mult))
                    nc.vector.scalar_tensor_tensor(out=m2[:, m, :], in0=xc[:, m, :], scalar=1.0, in1=m2[:, m, :],
                                                   op0=ALU.add, op1=ALU.mult).then_inc(s.sq, 1)
                for m in range(4):
                    dve.wait_ge(s.root, m + 1)
                    step(nc.vector.memset(m2[:, m, 0:1], 1.0))
                    step(nc.vector.tensor_tensor(g[:, m, :], g[:, m, :], m2[:, m, :], ALU.mult))
                    step(nc.vector.tensor_tensor_scan(m2[:, m, :], r[:, m, :], g[:, m, :], 0.0, ALU.mult, ALU.add))
                dve.wait_ge(s.z, 8)
                for m in range(4):
                    nc.vector.tensor_tensor(mix[:, m, :], m2[:, m, :], z[:, m, :], ALU.mult)


ZS0 = Z0
XT0 = ZS0 + NT * SSD_W
BT0 = XT0 + NT * SSD_W
FE0 = BT0 + NT * SSD_G * SSD_N
XC0 = FE0 + 192
assert XC0 + 13 * T + 4 <= SIZE


def stage_keep_dt(nc, I, S):
    A = S.arena
    src, dst = A.view(FD0, 192), A.view(FE0, 192)
    assert FE0 >= FD0 + 192
    with memory(S) as ctx:
        s = semaphores(nc, S, ctx, "kd", "moved")
        with block_of(nc, S) as block:
            @block.vector
            def _(dve):
                nc.vector.tensor_copy(dst, src).then_inc(s.moved, 1)


def stage_project_ssd(nc, I, S):
    A = S.arena
    w = I["w_in_2"].rearrange("l (k p) n -> p (l k) n", p=P)
    xc = A.view(XC0, 12, T)
    bat, _ = COL["ssd_conv_b_2"]
    cv = dense_conv(nc, S, "sc", lambda m: w[:, :, bass.ds(m * P + XBC_OFF, P)], 12, taps_of(S, "ssd_conv_w_2", 12),
               lambda m: S.cols[:, bass.ds(m + bat, 1)], xc, ZS0,
                    [ZS0 + 4 * KT * P + j * (T + 4) for j in range(3)] + [XC0 + 12 * T], banks=4)
    zs = A.view(ZS0, NT, SSD_W)
    project_tokens(nc, S, "sz", w, [(ZS_OFF + q * HALF, HALF) for q in range(2)], XT0,
                   lambda act, bank, i, q: act.activation(zs[:, i, q * HALF:(q + 1) * HALF], bank, ACT.Silu),
                   banks=2, room=(cv.conv, 4 + 12))
    xt = A.view(XT0, NT, SSD_W)
    bt = A.view(BT0, NT, SSD_G * SSD_N)
    with memory(S) as ctx:
        s = semaphores(nc, S, ctx, "st", "silu turned free")
        ps = psum(nc, ctx, "st_ps", 2, PSB)
        jobs = [(m, h) for m in range(10) for h in range(2)]
        with block_of(nc, S) as block:
            @block.scalar
            def _(act):
                for m in range(12):
                    nc.scalar.activation(xc[:, m, :], xc[:, m, :], ACT.Silu).then_inc(s.silu, 1)

            @block.tensor
            def _(pe):
                for n, (m, h) in enumerate(jobs):
                    pe.wait_ge(s.silu, m + 1)
                    if n >= 2:
                        pe.wait_ge(s.free, n - 1)
                    for i in range(4):
                        t = pe.transpose(ps[:, n % 2, i * P:(i + 1) * P],
                                         xc[:, m, (4 * h + i) * P:(4 * h + i + 1) * P], S.ident)
                    t.then_inc(s.turned, 1)

            @block.vector
            def _(dve):
                for n, (m, h) in enumerate(jobs):
                    dve.wait_ge(s.turned, n + 1)
                    dst = xt[:, 4 * h:4 * h + 4, m * P:(m + 1) * P] if m < 8 else \
                        bt[:, 4 * h:4 * h + 4, (m - 8) * P:(m - 7) * P]
                    nc.vector.tensor_copy(dst, ps[:, n % 2, :].rearrange("p (i n) -> p i n", i=4)).then_inc(s.free, 1)


def stage_ssd(nc, I, S):
    A = S.arena
    NC, HG = T // SSD_C, SSD_H // SSD_G
    zs = A.view(ZS0, NT, SSD_W)
    xt = A.view(XT0, NT, SSD_W)
    bt = A.view(BT0, NT, SSD_G * SSD_N)
    xc = A.view(XC0, 12, T)
    f = A.view(FE0, NT, ATT_H + SSD_H)[:, :, ATT_H:]
    at = XC0
    R = A.view(at, SSD_H, P)
    E = A.view(at + 2048, SSD_H, P)
    gm = A.view(at + 4096, SSD_G, P)
    xdt = A.view(at + 4352, SSD_W)
    xds = A.view(at + 5376, SSD_W)
    st = A.view(at + 6400, SSD_W)
    yy = A.view(C0, SSD_W)
    y2 = A.view(C0 + 1024, SSD_W)
    sm = at + 7424
    dtb, alog, dsk = (A.view(sm + 16 * i, SSD_H) for i in range(3))
    e, ln, ww, dt, adt = (A.view(sm + 48 + i * 128, NC, SSD_H) for i in range(5))
    assert sm + 48 + 640 <= at + 8 * T
    ex = [A.view(M_SMALL + 128 * i, NC, SSD_H) for i in range(2)]
    ex.append(A.view(M_IDENT + 7 * 128, NC, SSD_H))
    ea, ds, et = ex
    ms = A.view(M_SMALL + 256, 2)
    mix = S.hT
    with memory(S) as ctx:
        s = semaphores(nc, S, ctx, "ss", "in_ act exped dve adt sums ea R G gm seg E M xdt xds Y off st_mm st upd y_ok sq ms root"
                                      " gated turned out n")
        pa = psum(nc, ctx, "ss_a", 4, PSB)
        pd = psum(nc, ctx, "ss_d", 2, PSB)
        po = psum(nc, ctx, "ss_o", 2, PSB)
        with block_of(nc, S) as block:
            @block.sync
            def _(sp):
                for dst, name in ((dtb, "ssd_dt_bias_2"), (alog, "ssd_a_log_2"), (dsk, "ssd_d_2")):
                    sp.dma_start(dst, I[name].broadcast_to([P, SSD_H])).then_inc(s.in_, 16)

            @block.scalar
            def _(act):
                act.wait_ge(s.act, 1)
                nc.scalar.activation(e, e, ACT.Exp).then_inc(s.exped, 1)
                act.wait_ge(s.exped, 1)
                nc.scalar.activation(ln, e, ACT.Ln, bias=1.0).then_inc(s.exped, 1)
                act.wait_ge(s.in_, 48)
                nc.scalar.activation(alog, alog, ACT.Exp).then_inc(s.exped, 1)
                act.wait_ge(s.sums, 1)
                for n in range(3):
                    nc.scalar.activation(ex[n], pa[:, n, 0:128].rearrange("p (c h) -> p c h", h=SSD_H), ACT.Exp)\
                        .then_inc(s.ea, 1)
                for c in range(NC):
                    for q in range(4):
                        act.wait_ge(s.seg, 4 * c + q + 1)
                        if c:
                            act.wait_ge(s.Y, c)
                        nc.scalar.activation(E[:, 4 * q:4 * q + 4, :],
                                             pa[:, q, :].rearrange("p (h l) -> p h l", l=P), ACT.Exp)\
                            .then_inc(s.E, 1)
                    act.wait_ge(s.y_ok, c + 1)
                    for g in range(2):
                        nc.scalar.activation(y2[:, g * HALF:(g + 1) * HALF], yy[:, g * HALF:(g + 1) * HALF],
                                             ACT.Square, accum_out=ms[:, g:g + 1]).then_inc(s.sq, 1)
                    act.wait_ge(s.ms, c + 1)
                    nc.scalar.activation(ms, ms, ACT.Sqrt).then_inc(s.root, 1)

            @block.gpsimd
            def _(pool):
                pool.wait_ge(s.adt, 1)
                pool.wait_ge(s.ea, 3)
                for c in range(NC):
                    if c:
                        pool.wait_ge(s.seg, 4 * c)
                    pool.tensor_tensor(R, S.t_le.unsqueeze(1).broadcast_to([P, SSD_H, P]),
                                       adt[:, c, :].unsqueeze(2).broadcast_to([P, SSD_H, P]), ALU.mult)\
                        .then_inc(s.R, 1)
                    if c:
                        pool.wait_ge(s.st_mm, c)
                    pool.tensor_tensor(xdt.rearrange("p (h d) -> p h d", d=SSD_P),
                                       xt[:, c, :].rearrange("p (h d) -> p h d", d=SSD_P),
                                       dt[:, c, :].unsqueeze(2).broadcast_to([P, SSD_H, SSD_P]), ALU.mult)\
                        .then_inc(s.xdt, 1)
                    pool.wait_ge(s.xdt, c + 1)
                    pool.tensor_tensor(xds.rearrange("p (h d) -> p h d", d=SSD_P),
                                       xdt.rearrange("p (h d) -> p h d", d=SSD_P),
                                       ds[:, c, :].unsqueeze(2).broadcast_to([P, SSD_H, SSD_P]), ALU.mult)\
                        .then_inc(s.xds, 1)

            @block.tensor
            def _(pe):
                pe.wait_ge(s.adt, 1)
                for n, m in enumerate((S.t_le, S.t_gt, S.ones)):
                    mm = pe.matmul(pa[:, n, 0:128], m, adt.rearrange("p c h -> p (c h)"), start=True, stop=True)
                mm.then_inc(s.sums, 1)
                pe.wait_ge(s.ea, 3)

                def turn(c):
                    pe.wait_ge(s.gated, c + 1)
                    for k in range(8):
                        t = pe.transpose(pd[:, k // 4, (k % 4) * P:(k % 4 + 1) * P], yy[:, k * P:(k + 1) * P],
                                         S.ident)
                    t.then_inc(s.turned, 1)

                for c in range(NC):
                    tok = slice(c * P, (c + 1) * P)
                    if c:
                        pe.wait_ge(s.upd, c)
                    for g in range(SSD_G):
                        mm = pe.matmul(po[:, 0, g * P:(g + 1) * P], xc[:, 8 + g, tok], xc[:, 10 + g, tok],
                                       start=True, stop=True)
                    mm.then_inc(s.G, 1)
                    pe.wait_ge(s.R, c + 1)
                    for q in range(4):
                        pe.matmul(pa[:, q, :], S.t_gt, R[:, 4 * q:4 * q + 4, :].rearrange("p h l -> p (h l)"),
                                  start=True, stop=True).then_inc(s.seg, 1)
                    if c:
                        turn(c - 1)
                    pe.wait_ge(s.gm, c + 1)
                    if c:
                        for g in range(SSD_G):
                            mm = pe.matmul(po[:, g, :], xc[:, 10 + g, tok], st[:, g * HALF:(g + 1) * HALF],
                                           start=True, stop=True)
                        mm.then_inc(s.off, 1)
                    pe.wait_ge(s.M, c + 1)
                    pe.wait_ge(s.xdt, c + 1)
                    if c:
                        pe.wait_ge(s.out, c)
                    for h in range(SSD_H):
                        o = pd[:, h // HG, (h % HG) * SSD_P:(h % HG + 1) * SSD_P]
                        mm = pe.matmul(o, E[:, h, :], xdt[:, h * SSD_P:(h + 1) * SSD_P], start=True, stop=True)
                    mm.then_inc(s.Y, 1)
                    pe.wait_ge(s.xds, c + 1)
                    pe.wait_ge(s.n, c + 1)
                    for g in range(SSD_G):
                        mm = pe.matmul(po[:, g, :], bt[:, c, g * P:(g + 1) * P], xds[:, g * HALF:(g + 1) * HALF],
                                       start=True, stop=True)
                    mm.then_inc(s.st_mm, 1)
                turn(NC - 1)

            @block.vector
            def _(dve):
                step = Chain(dve, s.dve)
                dve.wait_ge(s.in_, 48)
                step(nc.vector.tensor_tensor(dt, f, dtb.unsqueeze(1).broadcast_to([P, NC, SSD_H]), ALU.add))
                step(nc.vector.tensor_scalar(ww, dt, -1.0, None, ALU.mult))
                nc.vector.tensor_tensor(e, ww, dt, ALU.min).then_inc(s.act, 1)
                dve.wait_ge(s.exped, 3)
                log1p_tail(step, nc, e, ln, ww, ww)
                step(nc.vector.tensor_scalar(dt, dt, 0.0, None, ALU.max))
                step(nc.vector.tensor_tensor(dt, dt, ww, ALU.add))
                step(nc.vector.tensor_scalar(alog, alog, -1.0, None, ALU.mult))
                nc.vector.tensor_tensor(adt, dt, alog.unsqueeze(1).broadcast_to([P, NC, SSD_H]), ALU.mult)\
                    .then_inc(s.adt, 1)
                bh = lambda v: v.unsqueeze(2).broadcast_to([P, SSD_H, SSD_P])
                hd = lambda v: v.rearrange("p (h d) -> p h d", d=SSD_P)

                def out(c):
                    dve.wait_ge(s.turned, c + 1)
                    gn, _ = COL["ssd_norm_g_2"]
                    nc.vector.tensor_tensor(mix[:, :, c * P:(c + 1) * P],
                                            pd[:, :, :].rearrange("p a (k t) -> p (a k) t", t=P),
                                            S.cols[:, gn:gn + 8].unsqueeze(2).broadcast_to([P, 8, P]), ALU.mult)\
                        .then_inc(s.out, 1)

                for c in range(NC):
                    dve.wait_ge(s.G, c + 1)
                    nc.vector.tensor_tensor(gm, po[:, 0, 0:2 * P].rearrange("p (g l) -> p g l", l=P),
                                            S.t_le.unsqueeze(1).broadcast_to([P, SSD_G, P]), ALU.mult)\
                        .then_inc(s.gm, 1)
                    dve.wait_ge(s.gm, c + 1)
                    for g in range(SSD_G):
                        dve.wait_ge(s.E, 4 * c + 2 * g + 2)
                        k = nc.vector.tensor_tensor(E[:, g * HG:(g + 1) * HG, :], E[:, g * HG:(g + 1) * HG, :],
                                                    gm[:, g, :].unsqueeze(1).broadcast_to([P, HG, P]), ALU.mult)
                    k.then_inc(s.M, 1)
                    if c:
                        out(c - 1)
                    step(nc.vector.tensor_tensor(hd(yy), hd(xt[:, c, :]), bh(dsk), ALU.mult))
                    if c:
                        dve.wait_ge(s.off, c)
                        dve.wait_ge(s.ms, c)
                        step(nc.vector.tensor_tensor(hd(y2), hd(po[:, :, :].rearrange("p a b -> p (a b)")),
                                                     bh(ea[:, c, :]), ALU.mult))
                        nc.vector.memset(ww[:, 0, 0:1], 0.0).then_inc(s.n, 1)
                        step(nc.vector.tensor_tensor(yy, yy, y2, ALU.add))
                    else:
                        nc.vector.memset(ww[:, 0, 0:1], 0.0).then_inc(s.n, 1)
                    dve.wait_ge(s.Y, c + 1)
                    step(nc.vector.tensor_tensor(yy, yy, pd[:, :, :].rearrange("p a b -> p (a b)"), ALU.add))
                    nc.vector.tensor_tensor(yy, yy, zs[:, c, :], ALU.mult).then_inc(s.y_ok, 1)
                    dve.wait_ge(s.st_mm, c + 1)
                    if c:
                        step(nc.vector.tensor_tensor(hd(st), hd(st), bh(et[:, c, :]), ALU.mult))
                        k = nc.vector.tensor_tensor(st, st, po[:, :, :].rearrange("p a b -> p (a b)"), ALU.add)
                    else:
                        k = nc.vector.tensor_copy(st, po[:, :, :].rearrange("p a b -> p (a b)"))
                    k.then_inc(s.upd, 1)
                    dve.wait_ge(s.sq, 2 * c + 2)
                    nc.vector.tensor_scalar(ms, ms, 1.0 / HALF, EPS, ALU.mult, ALU.add).then_inc(s.ms, 1)
                    dve.wait_ge(s.root, c + 1)
                    step(nc.vector.reciprocal(ms, ms))
                    for g in range(2):
                        k = nc.vector.tensor_scalar(yy[:, g * HALF:(g + 1) * HALF], yy[:, g * HALF:(g + 1) * HALF],
                                                    ms[:, g:g + 1], None, ALU.mult)
                    k.then_inc(s.gated, 1)
                out(NC - 1)


def stage_out(nc, I, S):
    A = S.arena
    w = I["w_out_2"].rearrange("l (k p) n -> p (l k) n", p=P)
    wv = [A.view(Z0 + q * MT * HALF, MT, HALF) for q in range(2)]
    x2 = A.view(Z0 + MT * D, KT, T)
    ot = A.view(C0, 4, HALF)
    att, lru = A.view(MA0, 4, T), A.view(ML0, 4, T)
    def mix(k):
        return att[:, k, :] if k < 4 else S.hT[:, k - 4, :] if k < 12 else lru[:, k - 12, :]
    with memory(S) as ctx:
        s = semaphores(nc, S, ctx, "fo", "x w0 w1 w2 w3 w4 done copied o0 o1 o2 o3")
        parts = [s.w0, s.w1, s.w2, s.w3]
        sent = [s.o0, s.o1, s.o2, s.o3]
        ps = psum(nc, ctx, "fo_ps", 8, PSB)
        jobs = [(q, i) for q in range(2) for i in range(NT)]
        with block_of(nc, S) as block:
            @block.sync
            def _(sp):
                for part in range(4):
                    rows = slice(4 * part, 4 * part + 4)
                    sp.dma_start(wv[0][:, rows, :], w[:, rows, 0:HALF]).then_inc(parts[part], 16)
                sp.dma_start(x2, S.kept[1].rearrange("p (k t) -> p k t", t=T)).then_inc(s.x, 16)
                sp.dma_start(wv[1], w[:, :, HALF:]).then_inc(s.w4, 16)
                for n, (q, i) in enumerate(jobs):
                    sp.wait_ge(s.copied, n + 1)
                    sp.dma_start(S.out[0, i * P:(i + 1) * P, q * HALF:(q + 1) * HALF], ot[:, n % 4, :])\
                        .then_inc(sent[n % 4], 16)
                for n in range(4):
                    sp.wait_ge(sent[n], 16 * len(jobs) // 4)

            @block.tensor
            def _(pe):
                for n, (q, i) in enumerate(jobs):
                    if q:
                        pe.wait_ge(s.w4, 16)
                    if n >= 8:
                        pe.wait_ge(s.copied, n - 7)
                    tok = slice(i * P, (i + 1) * P)
                    for k in range(MT):
                        if n == 0 and k % 4 == 0:
                            pe.wait_ge(parts[k // 4], 16)
                        mm = pe.matmul(ps[:, n % 8, :], mix(k)[:, tok], wv[q][:, k, :], start=(k == 0),
                                       stop=(k == MT - 1))
                        if k == MT - 2:
                            pe.wait_ge(s.x, 16)
                            for f in range(4):
                                pe.matmul(ps[:, n % 8, f * P:(f + 1) * P], x2[:, 4 * q + f, tok], S.ident,
                                          start=False, stop=False, skip_group_check=True)
                    mm.then_inc(s.done, 1)

            @block.scalar
            def _(act):
                for n, (q, i) in enumerate(jobs):
                    act.wait_ge(s.done, n + 1)
                    if n >= 4:
                        act.wait_ge(sent[n % 4], 16 * (n // 4))
                    nc.scalar.activation(ot[:, n % 4, :], ps[:, n % 8, :], ACT.Copy).then_inc(s.copied, 1)


def mixer_views(S):
    A = S.arena
    S.xT = A.view(X0, KT, T)
    S.ctxT = A.view(C0, KT, TC)
    S.z = A.view(Z0, Z_TILES, T)
    S.kc = A.view(KC0, 2, TC)
    S.vt = A.view(VT0, (NT + NTC) * HEADS, HD + 1)
    S.gates = A.view(GT0, NT + NTC, 16)
    S.sv = A.view(SV0, NT, W_MIX)
    S.u5 = A.view(U50, S5G, S5L, S5P)
    S.u5c = A.view(U5C0, S5G, S5L, S5P)
    S.htok = A.view(Z0 + 10 * T, NT * HEADS, HD).rearrange("p (i h) d -> p i h d", h=HEADS)
    S.htmp = A.view(C0, 8, HD).rearrange("p (c j) d -> p c j d", c=2)
    S.crow = A.view(C0, T)[0:ATT_H, :]


def build(nc, I, out, upto=99, dumps=()):
    used_semaphores[0] = 0
    with ExitStack() as ctx:
        S = Views()
        S.group = None
        arena = ctx.enter_context(nc.sbuf_tensor("arena", [P, X0], F32))
        A = S.arena = Arena(arena, SIZE)
        S.ident, S.ones, S.mean, S.t_le, S.t_ge, S.t_lt, S.t_gt, S.blk = (
            A.view(m, P) for m in (M_IDENT, M_ONES, M_MEAN, M_TLE, M_TGE, M_TLT, M_TGT, M_BLK))
        S.cols = A.view(M_COLS, N_COLS)
        S.mod = A.view(M_MOD, 48, 2)
        S.cs = A.view(M_CS, KT, 2)
        S.sc1 = A.view(M_SC1, KT, 2)
        S.sc2 = A.view(M_SC2, KT)
        S.small = A.view(M_SMALL, 300)
        S.x_w, S.x_b, S.h_w, S.h_b = (A.view(M_WX + 8 * i, KT) for i in range(4))
        S.hT = A.view(H0, KT, T)
        S.yT = S.hT
        S.a = A.view(M_SMALL, NT + NTC, 8)
        S.expn = A.view(M_SMALL + 80, NT, 8)
        S.M = [A.view(H0 + d * T, T)[0:8, :] for d in range(2)]
        S.out = out
        S.kept = [nc.dram_tensor(f"kept_{i}", (P, TILE8), F32, kind="Internal").ap() for i in range(2)]
        n = 0
        for number, phase in enumerate(PHASES):
            with ExitStack() as memory_of_phase:
                if number == 1:
                    ffn_memory(nc, memory_of_phase, S)
                else:
                    A.work = memory_of_phase.enter_context(nc.sbuf_tensor(f"work_{number}", [P, SIZE - X0], F32))
                    mixer_views(S)
                for stage in phase:
                    if n < upto:
                        stage(nc, I, S)
                    n += 1
                for i, (d, at, k) in enumerate(dumps):
                    if n >= upto and n - len(phase) < upto:
                        with nc.semaphore(f"dump{i}") as sd, nc.Block() as block:
                            @block.sync
                            def _(sp):
                                sp.dma_start(d, A.view(at, k)).then_inc(sd, 16)
                                sp.wait_ge(sd, 16)


PHASES = [[stage_constants, beside(40, stage_project_1, stage_keep_x, stage_mod_rest),
          beside(40, stage_project_tokens_1, stage_conv), stage_sgu,
          stage_s5_params, stage_s5, stage_s5_glu, stage_mlstm_gates, beside(20, stage_mlstm, stage_back_x),
          stage_mlstm_out, beside(40, stage_w_out_1)], [stage_ffn], [stage_norm_2,
          beside(20, stage_rms), beside(40, stage_project_att, stage_forget, stage_att_values), stage_attention,
          beside(40, stage_lru), beside(40, stage_keep_dt, stage_project_ssd), stage_ssd, stage_out]]


_OUT = (1, T, D)


def kernel(**inputs):
    import numpy as _np
    import concourse.bacc as _bacc
    from concourse.bass_utils import run_bass_kernel_spmd as _run

    nc = _bacc.Bacc("TRN2", target_bir_lowering=False, num_devices=1)
    arrays, args = {}, {}
    for name, a in inputs.items():
        a = _np.ascontiguousarray(a)
        arrays[f"in_{name}"] = a
        args[name] = nc.dram_tensor(f"in_{name}", a.shape, F32, kind="ExternalInput").ap()
    out = nc.dram_tensor("out_0", _OUT, F32, kind="ExternalOutput").ap()
    build(nc, args, out)
    return _run(nc, [arrays], core_ids=[0]).results[0]["out_0"]
```
